# Optimizing a Trainium2 kernel written in Bass

```python
import math
import jax
import jax.numpy as jnp
from jax import lax
import numpy as np

D_MODEL = 1024
BATCH = 1
SEQ = 128
DEPTH = 2
DEC_BATCH = 1
DEC_SEQ = 256
PAST_LEN = 128

GRID_W = 64
EPS = 1e-6
NEG_INF = -1e30

N_HEADS = 8
N_KV_HEADS = 2
GQA_GROUP = N_HEADS // N_KV_HEADS
HEAD_DIM = 64
ATTN_WIDTH = N_HEADS * HEAD_DIM
KV_WIDTH = N_KV_HEADS * HEAD_DIM
WINDOW = 128
BLOCK = 128
ROPE_THETA = 10000.0

SSD_HEADS = 8
SSD_HEADDIM = 64
SSD_WIDTH = SSD_HEADS * SSD_HEADDIM
SSD_GROUPS = 2
D_STATE = 64
BC_WIDTH = SSD_GROUPS * D_STATE
D_CONV = 5
CHUNK = 128
XBC_WIDTH = SSD_WIDTH + 2 * BC_WIDTH

MIX_WIDTH = ATTN_WIDTH + SSD_WIDTH
IN_WIDTH = ATTN_WIDTH + 2 * KV_WIDTH + XBC_WIDTH + SSD_WIDTH + 2 * SSD_HEADS

N_EXPERTS = 16
N_EXPERT_GROUPS = 4
EXPERTS_PER_GROUP = N_EXPERTS // N_EXPERT_GROUPS
TOP_K = 2
D_FF = 256

kernel_name = 'hybrid_diffusion_ssd_swa_moe_step'

def rmsnorm(x, w):
    xf = x.astype(jnp.float32)
    y = xf * lax.rsqrt(jnp.mean(xf * xf, axis=-1, keepdims=True) + EPS)
    return (y * w.astype(jnp.float32)).astype(x.dtype)

def adaln(cvec, w_ada_l, b_ada_l):
    m = jax.nn.silu(cvec) @ w_ada_l + b_ada_l
    return jnp.split(m[:, None, :], 6, axis=-1)

def modulate(h, shift, scale):
    return h * (1 + scale) + shift

def axial_rope_tables(n_tokens, dtype):
    rows = n_tokens // GRID_W
    row = jnp.broadcast_to(jnp.arange(rows, dtype=jnp.float32)[:, None], (rows, GRID_W)).reshape(-1)
    col = jnp.broadcast_to(jnp.arange(GRID_W, dtype=jnp.float32)[None, :], (rows, GRID_W)).reshape(-1)
    n_freq = HEAD_DIM // 4
    inv_freq = jnp.power(ROPE_THETA, -jnp.arange(n_freq, dtype=jnp.float32) / n_freq)
    ang = jnp.concatenate([row[:, None] * inv_freq, col[:, None] * inv_freq], axis=-1)
    return jnp.cos(ang).astype(dtype), jnp.sin(ang).astype(dtype)

def apply_rope(x, cos, sin):
    half = HEAD_DIM // 2
    x1, x2 = x[..., :half], x[..., half:]
    c = cos[None, :, None, :]
    s = sin[None, :, None, :]
    return jnp.concatenate([x1 * c - x2 * s, x1 * s + x2 * c], axis=-1)

def depthwise_conv_centred(u, w, b):
    pad = (D_CONV - 1) // 2
    y = lax.conv_general_dilated(u, w[:, None, :].astype(u.dtype), window_strides=(1,),
                                 padding=[(pad, pad)], dimension_numbers=('NWC', 'WIO', 'NWC'),
                                 feature_group_count=u.shape[-1])
    return y + b.astype(u.dtype)

def project(h, w_in_l, conv_w_l, conv_b_l):
    b, l, _ = h.shape
    p = h @ w_in_l
    o1 = ATTN_WIDTH
    o2 = o1 + KV_WIDTH
    o3 = o2 + KV_WIDTH
    o4 = o3 + XBC_WIDTH
    o5 = o4 + SSD_WIDTH
    q = p[..., :o1].reshape(b, l, N_HEADS, HEAD_DIM)
    k = p[..., o1:o2].reshape(b, l, N_KV_HEADS, HEAD_DIM)
    v = p[..., o2:o3].reshape(b, l, N_KV_HEADS, HEAD_DIM)
    xbc = jax.nn.silu(depthwise_conv_centred(p[..., o3:o4], conv_w_l, conv_b_l))
    z = p[..., o4:o5]
    dt_raw = p[..., o5:].reshape(b, l, 2, SSD_HEADS)
    xs = xbc[..., :SSD_WIDTH].reshape(b, l, SSD_HEADS, SSD_HEADDIM)
    rep = SSD_HEADS // SSD_GROUPS
    bm = jnp.repeat(xbc[..., SSD_WIDTH:SSD_WIDTH + BC_WIDTH].reshape(b, l, SSD_GROUPS, D_STATE), rep, axis=2)
    cm = jnp.repeat(xbc[..., SSD_WIDTH + BC_WIDTH:].reshape(b, l, SSD_GROUPS, D_STATE), rep, axis=2)
    return q, k, v, xs, bm, cm, z, dt_raw

def segsum(a):
    t = a.shape[-1]
    cs = jnp.cumsum(a, axis=-1)
    seg = cs[..., :, None] - cs[..., None, :]
    mask = jnp.tril(jnp.ones((t, t), dtype=bool))
    return jnp.where(mask, seg, -jnp.inf)

def ssd_scan(xs, dt, a, bm, cm, init_state):
    b, l, h, p = xs.shape
    nc = l // CHUNK
    f32 = jnp.float32
    x = (xs.astype(f32) * dt[..., None]).reshape(b, nc, CHUNK, h, p)
    bc = bm.astype(f32).reshape(b, nc, CHUNK, h, D_STATE)
    cc = cm.astype(f32).reshape(b, nc, CHUNK, h, D_STATE)
    da = (dt * a).reshape(b, nc, CHUNK, h).transpose(0, 3, 1, 2)
    da_cs = jnp.cumsum(da, axis=-1)
    decay_in = jnp.exp(segsum(da))
    scores = jnp.einsum('bclhn,bcshn->bhcls', cc, bc) * decay_in
    y_diag = jnp.einsum('bhcls,bcshp->bclhp', scores, x)
    decay_to_end = jnp.exp(da_cs[..., -1:] - da_cs)
    chunk_states = jnp.einsum('bclhn,bhcl,bclhp->bchpn', bc, decay_to_end, x)
    chunk_states = jnp.concatenate([init_state[:, None], chunk_states], axis=1)
    chunk_decay = jnp.exp(segsum(jnp.pad(da_cs[..., -1], ((0, 0), (0, 0), (1, 0)))))
    states = jnp.einsum('bhzc,bchpn->bzhpn', chunk_decay, chunk_states)
    y_off = jnp.einsum('bclhn,bchpn,bhcl->bclhp', cc, states[:, :-1], jnp.exp(da_cs))
    y = (y_diag + y_off).reshape(b, l, h, p)
    return y, states[:, -1]

def gated_rmsnorm(y, z, w):
    shape = y.shape
    g = y.astype(jnp.float32) * jax.nn.silu(z.astype(jnp.float32))
    g = g.reshape(shape[:-1] + (SSD_GROUPS, SSD_WIDTH // SSD_GROUPS))
    g = g * lax.rsqrt(jnp.mean(g * g, axis=-1, keepdims=True) + EPS)
    return g.reshape(shape) * w.astype(jnp.float32)

def ssd_bidirectional(xs, bm, cm, z, dt_raw, dt_bias_l, a_log_l, d_l, norm_w_l, init_f, init_b):
    b, l = xs.shape[:2]
    dt = jax.nn.softplus(dt_raw.astype(jnp.float32) + dt_bias_l.astype(jnp.float32))
    a = -jnp.exp(a_log_l.astype(jnp.float32))
    y_f, s_f = ssd_scan(xs, dt[:, :, 0], a[0], bm, cm, init_f)
    flip = lambda t: jnp.flip(t, axis=1)
    y_b, s_b = ssd_scan(flip(xs), flip(dt[:, :, 1]), a[1], flip(bm), flip(cm), init_b)
    y = y_f + flip(y_b) + d_l.astype(jnp.float32)[:, None] * xs.astype(jnp.float32)
    out = gated_rmsnorm(y.reshape(b, l, SSD_WIDTH), z, norm_w_l).astype(xs.dtype)
    return out, s_f, s_b

def sink_probs(scores, sink):
    s = sink.astype(jnp.float32)[:, :, None]
    m = s
    for sc in scores:
        m = jnp.maximum(m, sc.max(axis=-1))
    probs = [jnp.exp(sc - m[..., None]) for sc in scores]
    denom = jnp.exp(s - m)
    for pr in probs:
        denom = denom + pr.sum(axis=-1)
    inv = 1.0 / denom
    return [pr * inv[..., None] for pr in probs]

def attn_context(q, k, v, sink):
    b, s = q.shape[:2]
    nq = s // BLOCK
    scale = HEAD_DIM ** -0.5
    sink = sink.reshape(N_KV_HEADS, GQA_GROUP)
    qb = q.reshape(b, nq, BLOCK, N_KV_HEADS, GQA_GROUP, HEAD_DIM).transpose(1, 0, 2, 3, 4, 5)

    def one_block(qblk):
        sc = jnp.einsum('bqkgd,bskd->bkgqs', qblk, k).astype(jnp.float32) * scale
        (pr,) = sink_probs([sc], sink)
        return jnp.einsum('bkgqs,bskd->bqkgd', pr, v.astype(jnp.float32))

    out = lax.map(one_block, qb)
    return out.transpose(1, 0, 2, 3, 4, 5).reshape(b, s, ATTN_WIDTH).astype(q.dtype)

def attn_latent(q, k, v, kc, vc, sink):
    b, l = q.shape[:2]
    nb = l // BLOCK
    scale = HEAD_DIM ** -0.5
    sink = sink.reshape(N_KV_HEADS, GQA_GROUP)
    qb = q.reshape(b, nb, BLOCK, N_KV_HEADS, GQA_GROUP, HEAD_DIM)
    pad = ((0, 0), (BLOCK, BLOCK), (0, 0), (0, 0))
    kp = jnp.pad(k, pad).reshape(b, nb + 2, BLOCK, N_KV_HEADS, HEAD_DIM)
    vp = jnp.pad(v, pad).reshape(b, nb + 2, BLOCK, N_KV_HEADS, HEAD_DIM)
    kband = jnp.concatenate([kp[:, :-2], kp[:, 1:-1], kp[:, 2:]], axis=2)
    vband = jnp.concatenate([vp[:, :-2], vp[:, 1:-1], vp[:, 2:]], axis=2)
    s_band = jnp.einsum('bnqkgd,bnskd->bnkgqs', qb, kband).astype(jnp.float32) * scale
    s_ctx = jnp.einsum('bnqkgd,bpkd->bnkgqp', qb, kc.astype(q.dtype)).astype(jnp.float32) * scale
    qpos = jnp.arange(BLOCK)[:, None]
    kpos = jnp.arange(3 * BLOCK)[None, :] - BLOCK
    within = jnp.abs(qpos - kpos) <= WINDOW
    key_abs = jnp.arange(nb)[:, None] * BLOCK + kpos
    valid = (key_abs >= 0) & (key_abs < l)
    mask = within[None, :, :] & valid[:, None, :]
    s_band = jnp.where(mask[None, :, None, None, :, :], s_band, NEG_INF)
    p_ctx, p_band = sink_probs([s_ctx, s_band], sink)
    out = (jnp.einsum('bnkgqp,bpkd->bnqkgd', p_ctx, vc.astype(jnp.float32))
           + jnp.einsum('bnkgqs,bnskd->bnqkgd', p_band, vband.astype(jnp.float32)))
    return out.reshape(b, l, ATTN_WIDTH).astype(q.dtype)

def mixer_context(h, w_in_l, conv_w_l, conv_b_l, sink_l, dt_bias_l, a_log_l, d_l, ssd_norm_l, w_out_l):
    q, k, v, xs, bm, cm, z, dt_raw = project(h, w_in_l, conv_w_l, conv_b_l)
    b = h.shape[0]
    attn = attn_context(q, k, v, sink_l)
    zero = jnp.zeros((b, SSD_HEADS, SSD_HEADDIM, D_STATE), jnp.float32)
    ssd, s_f, s_b = ssd_bidirectional(xs, bm, cm, z, dt_raw, dt_bias_l, a_log_l, d_l, ssd_norm_l, zero, zero)
    out = jnp.concatenate([attn, ssd], axis=-1) @ w_out_l
    state = jnp.stack([s_f, s_b], axis=1).astype(h.dtype)
    return out, k, v, state

def mixer_latent(h, kc, vc, st, rope_cos, rope_sin, w_in_l, conv_w_l, conv_b_l, sink_l,
                 dt_bias_l, a_log_l, d_l, ssd_norm_l, w_out_l):
    q, k, v, xs, bm, cm, z, dt_raw = project(h, w_in_l, conv_w_l, conv_b_l)
    q = apply_rope(q, rope_cos, rope_sin)
    k = apply_rope(k, rope_cos, rope_sin)
    attn = attn_latent(q, k, v, kc, vc, sink_l)
    init_f = st[:, 0].astype(jnp.float32)
    init_b = st[:, 1].astype(jnp.float32)
    ssd, _, _ = ssd_bidirectional(xs, bm, cm, z, dt_raw, dt_bias_l, a_log_l, d_l, ssd_norm_l, init_f, init_b)
    return jnp.concatenate([attn, ssd], axis=-1) @ w_out_l

def moe_ffn(h, w_router, router_bias, w_gate_l, w_up_l, w_down_l):
    b, l, d = h.shape
    t = h.reshape(b * l, d)
    scores = jax.nn.sigmoid((t @ w_router).astype(jnp.float32))
    sel = scores + router_bias.astype(jnp.float32)
    grp = sel.reshape(-1, N_EXPERT_GROUPS, EXPERTS_PER_GROUP)
    grp_score = lax.top_k(grp, TOP_K)[0].sum(axis=-1)
    best = jnp.argmax(grp_score, axis=-1)
    in_group = (jnp.arange(N_EXPERTS) // EXPERTS_PER_GROUP)[None, :] == best[:, None]
    masked = jnp.where(in_group, sel, NEG_INF)
    _, idx = lax.top_k(masked, TOP_K)
    w = jnp.take_along_axis(scores, idx, axis=-1)
    w = w / w.sum(axis=-1, keepdims=True)
    gates = jnp.sum(jax.nn.one_hot(idx, N_EXPERTS, dtype=jnp.float32) * w[..., None], axis=1)
    hid = jax.nn.silu(jnp.einsum('nd,edf->enf', t, w_gate_l)) * jnp.einsum('nd,edf->enf', t, w_up_l)
    hid = hid * gates.T[:, :, None].astype(hid.dtype)
    out = jnp.einsum('enf,efd->nd', hid, w_down_l)
    return out.reshape(b, l, d)

def setup_inputs(seed: int = 0) -> dict:
    key = jax.random.key(seed)
    ks = jax.random.split(key, 26)
    f32 = jnp.float32

    def nrm(k, shape, scale):
        return jax.random.normal(k, shape, f32) * scale

    x_prompt = nrm(ks[0], (BATCH, SEQ, D_MODEL), 1.0)
    x_sample = nrm(ks[1], (DEC_BATCH, DEC_SEQ, D_MODEL), 1.0)
    cache_k = nrm(ks[2], (DEC_BATCH, DEPTH, PAST_LEN, N_KV_HEADS, HEAD_DIM), 1.0)
    cache_v = nrm(ks[3], (DEC_BATCH, DEPTH, PAST_LEN, N_KV_HEADS, HEAD_DIM), 1.0)
    state_ssm = nrm(ks[4], (DEC_BATCH, DEPTH, 2, SSD_HEADS, SSD_HEADDIM, D_STATE), 0.1)
    c = nrm(ks[5], (DEC_BATCH, D_MODEL), 1.0)
    c_ctx = nrm(ks[6], (D_MODEL,), 1.0)
    norm1_w = 1.0 + nrm(ks[7], (DEPTH, D_MODEL), 0.02)
    norm2_w = 1.0 + nrm(ks[8], (DEPTH, D_MODEL), 0.02)
    final_norm_w = 1.0 + nrm(ks[9], (D_MODEL,), 0.02)
    w_ada = nrm(ks[10], (DEPTH, D_MODEL, 6 * D_MODEL), 0.5 * D_MODEL ** -0.5)
    b_ada = nrm(ks[11], (DEPTH, 6 * D_MODEL), 0.02)
    w_in = nrm(ks[12], (DEPTH, D_MODEL, IN_WIDTH), D_MODEL ** -0.5)
    conv_w = nrm(ks[13], (DEPTH, D_CONV, XBC_WIDTH), D_CONV ** -0.5)
    conv_b = nrm(ks[14], (DEPTH, XBC_WIDTH), 0.01)
    attn_sink = nrm(ks[15], (DEPTH, N_HEADS), 0.5)
    dt0 = jnp.exp(jax.random.uniform(ks[16], (DEPTH, 2, SSD_HEADS), f32, math.log(1e-3), math.log(1e-1)))
    dt_bias = dt0 + jnp.log(-jnp.expm1(-dt0))
    a_log = jnp.log(jax.random.uniform(ks[17], (DEPTH, 2, SSD_HEADS), f32, 1.0, 16.0))
    d_skip = 1.0 + nrm(ks[18], (DEPTH, SSD_HEADS), 0.1)
    ssd_norm_w = 1.0 + nrm(ks[19], (DEPTH, SSD_WIDTH), 0.02)
    w_out = nrm(ks[20], (DEPTH, MIX_WIDTH, D_MODEL), MIX_WIDTH ** -0.5)
    w_router = nrm(ks[21], (D_MODEL, N_EXPERTS), D_MODEL ** -0.5)
    router_bias = nrm(ks[22], (N_EXPERTS,), 0.01)
    w_gate = nrm(ks[23], (DEPTH, N_EXPERTS, D_MODEL, D_FF), D_MODEL ** -0.5)
    w_up = nrm(ks[24], (DEPTH, N_EXPERTS, D_MODEL, D_FF), D_MODEL ** -0.5)
    w_down = nrm(ks[25], (DEPTH, N_EXPERTS, D_FF, D_MODEL), D_FF ** -0.5)
    return {'x_prompt': x_prompt, 'x_sample': x_sample, 'cache_k': cache_k, 'cache_v': cache_v,
            'state_ssm': state_ssm, 'c': c, 'c_ctx': c_ctx, 'norm1_w': norm1_w, 'norm2_w': norm2_w,
            'final_norm_w': final_norm_w, 'w_ada': w_ada, 'b_ada': b_ada, 'w_in': w_in,
            'conv_w': conv_w, 'conv_b': conv_b, 'attn_sink': attn_sink, 'dt_bias': dt_bias,
            'a_log': a_log, 'd_skip': d_skip, 'ssd_norm_w': ssd_norm_w, 'w_out': w_out,
            'w_router': w_router, 'router_bias': router_bias, 'w_gate': w_gate, 'w_up': w_up,
            'w_down': w_down}

def reference(x_prompt, x_sample, cache_k, cache_v, state_ssm, c, c_ctx,
              norm1_w, norm2_w, final_norm_w, w_ada, b_ada, w_in, conv_w, conv_b,
              attn_sink, dt_bias, a_log, d_skip, ssd_norm_w, w_out,
              w_router, router_bias, w_gate, w_up, w_down):
    xp = x_prompt
    xs = x_sample
    rope_cos, rope_sin = axial_rope_tables(xs.shape[1], xs.dtype)
    ctx_vec = c_ctx[None, :]
    new_k, new_v, new_s = [], [], []
    for l in range(DEPTH):
        sh1, sc1, g1, sh2, sc2, g2 = adaln(ctx_vec, w_ada[l], b_ada[l])
        h = modulate(rmsnorm(xp, norm1_w[l]), sh1, sc1)
        mix, k_ctx, v_ctx, s_ctx = mixer_context(h, w_in[l], conv_w[l], conv_b[l], attn_sink[l],
                                                 dt_bias[l], a_log[l], d_skip[l], ssd_norm_w[l], w_out[l])
        xp = xp + g1 * mix
        h = modulate(rmsnorm(xp, norm2_w[l]), sh2, sc2)
        xp = xp + g2 * moe_ffn(h, w_router, router_bias, w_gate[l], w_up[l], w_down[l])
        new_k.append(k_ctx)
        new_v.append(v_ctx)
        new_s.append(s_ctx)
        sh1, sc1, g1, sh2, sc2, g2 = adaln(c, w_ada[l], b_ada[l])
        h = modulate(rmsnorm(xs, norm1_w[l]), sh1, sc1)
        mix = mixer_latent(h, cache_k[:, l], cache_v[:, l], state_ssm[:, l], rope_cos, rope_sin,
                           w_in[l], conv_w[l], conv_b[l], attn_sink[l], dt_bias[l], a_log[l],
                           d_skip[l], ssd_norm_w[l], w_out[l])
        xs = xs + g1 * mix
        h = modulate(rmsnorm(xs, norm2_w[l]), sh2, sc2)
        xs = xs + g2 * moe_ffn(h, w_router, router_bias, w_gate[l], w_up[l], w_down[l])
    y_prompt = rmsnorm(xp, final_norm_w)
    y_sample = rmsnorm(xs, final_norm_w)
    new_cache_k = jnp.stack(new_k, axis=1)
    new_cache_v = jnp.stack(new_v, axis=1)
    new_state_ssm = jnp.stack(new_s, axis=1)
    return (y_prompt, y_sample, new_cache_k, new_cache_v, new_state_ssm)


_drawn_inputs = setup_inputs


def setup_inputs(seed=0):
    import zlib

    import numpy as np

    out = dict(_drawn_inputs(seed))
    spreads = {}
    factors = {'final_norm_w': 23.017, 'attn_sink': 18.425, 'conv_b': 3.635, 'ssd_norm_w': 2.916}
    for name, (base, spread) in spreads.items():
        noise = np.random.default_rng([zlib.crc32(name.encode()), seed]).standard_normal(out[name].shape)
        drawn = base * np.exp(spread * noise) if base else spread * noise
        out[name] = jnp.asarray(drawn.astype(out[name].dtype))
    for name, factor in factors.items():
        out[name] = (out[name] * factor).astype(out[name].dtype)
    return out
```

```python
import concourse.bass as bass
from concourse import mybir
from contextlib import ExitStack
import numpy as np

P = 128
DM = 1024
KT = DM // P
DEPTH = 2
NT = 3
H = 8
HD = 64
KVH = 2
FREQ = HD // 2
AW = H * HD
IN_W = 2064
XBC0, Z0, DT0 = 768, 1536, 2048
XM = 6
TAPS = 5
PADW = 392
CONVW = PADW - (TAPS - 1)
SEG = (0, 132)
E = 16
F = 256
SMALL = 18
SLOTS = 6
UNIT = KT * 512
ADA_U, IN_U, OUT_U, MOE_U = 12, 4, 2, 24
LAYER_U = ADA_U + IN_U + OUT_U + MOE_U
EPS = 1e-6
NEG = -1e30
SCALE = HD ** -0.5


def hybrid_step(nc, x_prompt, x_sample, cache_k, cache_v, state_ssm, c, c_ctx, norm1_w, norm2_w,
                final_norm_w, w_ada, b_ada, w_in, conv_w, conv_b, attn_sink, dt_bias, a_log, d_skip,
                ssd_norm_w, w_out, w_router, router_bias, w_gate, w_up, w_down, rope_cos, rope_sin,
                y_prompt, y_sample, new_k, new_v, new_state):
    fp32 = mybir.dt.float32
    ALU = mybir.AluOpType
    ACT = mybir.ActivationFunctionType
    AX = mybir.AxisListType

    ctx = ExitStack()
    with ctx:
        def sb(name, *shape):
            return ctx.enter_context(nc.sbuf_tensor(name, [P, *shape], fp32))

        def sem(name):
            return ctx.enter_context(nc.semaphore(name))

        ring = sb("ring", SLOTS, UNIT)
        x = sb("x", NT, DM)
        xn = sb("xn", NT, DM)
        mixed = xn
        acc = xn
        hT = sb("hT", KT, NT * P)
        probs = hT[:, :, :]
        qkv = sb("qkv", NT, 768)
        rot = sb("rot", 2, 640)
        pT = rot[:, :, 0:NT * P]
        xpad = sb("xpad", XM * 512)
        xpd = xpad[:, 0:XM * PADW].rearrange("p (m w) -> p m w", m=XM)
        xdt = xpad[:, :].rearrange("p (d t c) -> p d t c", d=2, t=NT)
        gateB = xpad[:, 0:2 * DM].rearrange("p (g c) -> p g c", g=2)
        conv = sb("conv", XM, CONVW)
        scT = conv[:, :, :].rearrange("p m w -> p (m w)")[:, 0:3 * 512].rearrange("p (n c) -> p n c", n=3)
        xs_tok = sb("xs_tok", NT, 512)
        b_tok = sb("b_tok", NT, P)
        ssd = hT[:, :, :].rearrange("p k c -> p (k c)")
        gm = ssd[:, 0:12 * P].rearrange("p (d t g c) -> p d t g c", d=2, t=NT, g=2)
        init_st, next_st, final_st = (ssd[:, 12 * P + i * 512:12 * P + (i + 1) * 512].rearrange("p (d c) -> p d c", d=2)
                             for i in range(3))
        qT = sb("qT", NT, 4, P)
        kT = sb("kT", 4, P)
        work = sb("work", 4, 512)
        hid = qkv[:, :, :].rearrange("p t c -> p (t c)")[:, 0:2 * 2 * NT * P].rearrange(
            "p (b f c) -> p b f c", b=2, f=2)
        sil = qkv[:, :, :].rearrange("p t c -> p (t c)")[:, 1536:2304].rearrange("p (f c) -> p f c", f=2)

        ident = sb("ident", P)
        tri = sb("tri", 2, P)
        ones = sb("ones", P)
        amask = sb("amask", 5, P)
        rope = sb("rope", 2, 2, FREQ)
        prm_rows = work[:, 0, 0:P]
        bada_rows = work[:, 0, P:2 * P]
        prm = sb("prm", P)
        bada = sb("bada", 96)
        cT = sb("cT", KT, 2)
        ada_row = work[:, 2:4, :]
        modT = sb("modT", DEPTH, 48, 2)
        amod = sb("amod", 2 * DEPTH, KT, 2)
        wr = sb("wr", KT, E)
        wdt = sb("wdt", DEPTH, KT, 2 * H)
        vec = sb("vec", DEPTH, 16 + 16 + 8 + 8)
        rb = sb("rb", E)
        snw = qT[:, 2, :, :].rearrange("p a c -> p (a c)")
        ckv = sb("ckv", 2, DEPTH, P)
        st_in = sb("st_in", 2, 2, 2, HD)
        diag = qT[:, 0, :, :]
        st_out = diag[:, :, :].rearrange("p a c -> p (a c)")
        epst = sb("epst", 4)
        ss = sb("ss", 5, NT)
        rstd = sb("rstd", 5, NT)
        mx = sb("mx", NT, H)
        nm = sb("nm", NT, H)
        es = sb("es", NT, H)
        rs = sb("rs", NT, H)
        den = sb("den", NT, H)
        dtr = sb("dtr", 2, NT, H)
        dtu = sb("dtu", 2, NT, H)
        dtv = sb("dtv", 2, NT, H)
        dtw = sb("dtw", 2, NT, H)
        dt = sb("dt", 2, NT, H)
        da = sb("da", 2, NT, H)
        cs = sb("cs", 2, NT, H)
        tot = sb("tot", 2, NT, H)
        ecs = sb("ecs", 2, NT, H)
        etot = sb("etot", 2, NT, H)
        wend = sb("wend", 2, NT, H)
        gss = sb("gss", NT, 2)
        grs = sb("grs", NT, 2)
        rt = qT[:, 1, :, :].rearrange("p a c -> p (a c)")[:, 0:8 * NT * E].rearrange(
            "p (n t e) -> p n t e", n=8, t=NT)
        tie = sb("tie", 2, NT, E)
        gates = sb("gates", NT, E)

        bank = [ctx.enter_context(nc.psum_tensor(f"bank{i}", [P, 512], fp32)) for i in range(8)]

        landed = [sem(f"landed{i}") for i in range(SLOTS)]
        freed = [sem(f"freed{i}") for i in range(SLOTS)]
        s_rows, s_x, s_small, s_state = sem("rows_landed"), sem("x_landed"), sem("small_landed"), sem("state_landed")
        s_snw, s_fnw = sem("snw_landed"), sem("fnw_landed")
        s_const = sem("consts_made")
        s_pool, s_dve, s_act = sem("pool_step"), sem("dve_step"), sem("act_step")
        s_zero, s_ctxs, s_bada = sem("borders_zeroed"), sem("ctx_state_copied"), sem("bada_copied")
        s_prmT, s_prm, s_cT, s_a = sem("prm_transposed"), sem("prm_copied"), sem("c_silu"), sem("a_made")
        s_ada, s_row, s_rowT, s_mod = sem("ada_mm"), sem("ada_row_copied"), sem("ada_transposed"), sem("mod_made")
        s_ss, s_rstd, s_xn, s_tr, s_hA, s_hD = (sem(n) for n in (
            "sumsq_made", "rstd_made", "xn_made", "xn_transposed", "hT_by_act", "hT_by_dve"))
        s_amod = sem("amod_made")
        s_q, s_kv, s_xbc, s_z = sem("q_mm"), sem("kv_mm"), sem("xbc_mm"), sem("z_mm")
        s_qc, s_kvc, s_xbcc, s_zc, s_dtr = (sem(n) for n in (
            "q_copied", "kv_copied", "xbc_copied", "z_silu", "dt_raw"))
        s_rope, s_qtr, s_qTc, s_conv, s_silu = (sem(n) for n in (
            "rope_done", "q_transposed", "qT_copied", "conv_done", "xbc_silu"))
        s_sc, s_scc, s_nm, s_exp, s_es, s_ptr, s_pTc, s_pv, s_attn = (sem(n) for n in (
            "scores_mm", "scores_masked", "max_made", "exp_done", "sink_exp", "probs_transposed",
            "pT_copied", "pv_mm", "attn_done"))
        s_dt1, s_dt2, s_da, s_cum, s_cs, s_ecs = (sem(n) for n in (
            "dt_abs", "dt_ln", "da_made", "cumsum_mm", "cs_copied", "decays_made"))
        s_xtr, s_xtc, s_g, s_gm = sem("xs_transposed"), sem("xs_copied"), sem("g_mm"), sem("g_masked")
        s_xdt, s_xw, s_st, s_stc, s_snx = (sem(n) for n in (
            "xdt_made", "xw_made", "state_mm", "state_copied", "state_next"))
        s_sto, s_stoc, s_yoff, s_cdec, s_seg, s_dexp, s_scm, s_y = (sem(n) for n in (
            "state_out_transposed", "state_out_copied", "yoff_mm", "decay_rows", "seg_made", "decay_exp",
            "decay_scores", "y_mm"))
        s_yv, s_yt, s_yp, s_gss, s_grs, s_ssd = (sem(n) for n in (
            "y_skip_made", "yoff_scaled", "y_summed", "gated_sumsq", "gated_rstd", "ssd_done"))
        s_dg, s_gb, s_gbc = sem("diag_made"), sem("gate_mm"), sem("gate_copied")
        s_mt, s_mA, s_mD, s_o, s_oc, s_x1 = (sem(n) for n in (
            "mixed_transposed", "mixT_by_act", "mixT_by_dve", "out_mm", "out_gated", "x_updated"))
        s_r, s_re, s_gate = sem("router_mm"), sem("router_exp"), sem("gates_made")
        s_gate_mm, s_up_mm, s_sil, s_hid, s_dn, s_acc, s_acc0, s_fin, s_x2 = (sem(n) for n in (
            "gate_mm_done", "up_mm_done", "silu_done", "hid_made", "down_mm", "acc_added", "acc_zeroed", "moe_gated", "moe_added"))
        s_y_out, s_yst, s_out = sem("final_made"), sem("y_stored"), sem("stored")

        def slot(u):
            return ring[:, u % SLOTS, :].rearrange("p (k n) -> p k n", k=KT)

        def bc(v, w):
            return v.unsqueeze(2).broadcast_to([v.shape[0], v.shape[1], w])

        def rep(v, n):
            return v.unsqueeze(1).broadcast_to([v.shape[0], n, v.shape[1]])

        def heads(v, n=H):
            return v.rearrange("p (h c) -> p h c", h=n)

        def tile_at(t):
            return (0, 132, 260)[t]

        def grp(t):
            return min(t, 1)

        STATES = ((0, 0), (1, 0), (0, 1), (1, 2))
        YOFF_BANK = {(1, 0): 3, (1, 1): 4, (2, 0): 5, (2, 1): 0}
        STORES = 2 + 4
        ADD = 6 * E

        block = ctx.enter_context(nc.Block())

        @block.sync
        def _(sp):
            def load(u, parts, turn):
                if turn is not None:
                    sp.wait_ge(freed[u % SLOTS], turn)
                for dst, src in parts:
                    sp.dma_start(dst, src).then_inc(landed[u % SLOTS], 16)

            def columns(u, w):
                v = w.rearrange("(k p) n -> p k n", p=P)
                load(u, [(slot(u)[:, 4 * i:4 * i + 4, :], v[:, 4 * i:4 * i + 4, :]) for i in range(2)],
                     u // SLOTS or None)

            def expert_unit(l, e, j, s, turn):
                if j < 2:
                    load(s, [(slot(s)[:, :, i * F:(i + 1) * F],
                              w[l, e + j].rearrange("(k p) f -> p k f", p=P))
                             for i, w in enumerate((w_gate, w_up))], turn)
                else:
                    load(s, [(ring[:, s, i * 2 * DM:(i + 1) * 2 * DM].rearrange("p (f n) -> p f n", f=2),
                              w_down[l, e + i].rearrange("(f p) n -> p f n", p=P)) for i in range(2)], turn)

            u = 0
            for l in range(DEPTH):
                for units, w in ((ADA_U, w_ada), (IN_U, w_in), (OUT_U, w_out)):
                    for j in range(units):
                        columns(u, w[l, :, j * 512:(j + 1) * 512])
                        u += 1
                turn = u // SLOTS
                with sp.Fori(0, E // 4) as i:
                    for s in range(SLOTS):
                        expert_unit(l, 4 * i + 2 * (s // 3), s % 3, s, i + turn)
                u += MOE_U
            for t in range(NT):
                sp.wait_ge(s_y_out, t + 1)
                dst = y_prompt[0] if t == 0 else y_sample[0, (t - 1) * P:t * P, :]
                sp.dma_start(dst, xn[:, t, :]).then_inc(s_yst, 16)
            sp.wait_ge(s_yst, 16 * NT)
            sp.wait_ge(s_out, 16 * STORES * DEPTH)

        @block.gpsimd
        def _(pool):
            n = [0]

            def step(ins):
                n[0] += 1
                ins.then_inc(s_pool, 1)
                pool.wait_ge(s_pool, n[0])

            pool.memset(ident[:, :], 0.0)
            pool.memset(tri[:, :, :], 1.0)
            pool.memset(amask[:, :, :], 0.0)
            pool.memset(epst[:, 0:NT], -0.5)
            step(pool.memset(ones[:, :], 1.0))
            pool.affine_select(out=ident[:, :], in_=ident[:, :], compare_op=ALU.not_equal, fill=1.0, base=0,
                               pattern=[[-1, P]], channel_multiplier=1)
            pool.affine_select(out=tri[:, 0, :], in_=tri[:, 0, :], compare_op=ALU.is_ge, fill=0.0, base=0,
                               pattern=[[1, P]], channel_multiplier=-1)
            pool.affine_select(out=tri[:, 1, :], in_=tri[:, 1, :], compare_op=ALU.is_ge, fill=0.0, base=0,
                               pattern=[[-1, P]], channel_multiplier=1)
            pool.affine_select(out=amask[:, 1, :], in_=amask[:, 1, :], compare_op=ALU.is_ge, fill=NEG, base=0,
                               pattern=[[1, P]], channel_multiplier=-1)
            pool.affine_select(out=amask[:, 4, :], in_=amask[:, 4, :], compare_op=ALU.is_ge, fill=NEG, base=0,
                               pattern=[[-1, P]], channel_multiplier=1).then_inc(s_const, 1)

            def norm_rstd(k):
                pool.wait_ge(s_ss, NT * (k + 1))
                step(pool.tensor_scalar(ss[:, k, :], ss[:, k, :], 1.0 / DM, EPS, ALU.mult, ALU.add))
                pool.tensor_tensor(rstd[:, k, :], ss[:, k, :], epst[:, 0:NT], ALU.pow).then_inc(s_rstd, 1)

            for l in range(DEPTH):
                if l:
                    pool.wait_ge(s_stc, l)
                for d in range(2):
                    for jj in range(2):
                        pool.dma_start(st_in[:, d, jj, :, :],
                                       state_ssm[0, l, d].rearrange("(g j hh) p n -> j (hh p) g n", g=2, j=2)[jj]
                                       ).then_inc(s_state, 16)
                norm_rstd(2 * l)
                if l:
                    pool.wait_ge(s_fin, NT * l)
                for b, w in ((0, 2), (130, 4), (390, 2)):
                    last = pool.memset(xpd[:, :, b:b + w], 0.0)
                last.then_inc(s_zero, 1)
                if l == 0:
                    pool.wait_ge(s_small, 16 * SMALL)
                for t in (1, 2):
                    pool.wait_ge(s_qc, NT * l + t + 1)
                    pool.wait_ge(s_kvc, NT * l + t + 1)
                    v = qkv[:, t, 0:640].rearrange("p (h d) -> p h d", d=HD)
                    o = rot[:, t - 1, :].rearrange("p (h d) -> p h d", d=HD)
                    x1, x2 = v[:, :, 0:FREQ], v[:, :, FREQ:HD]
                    co, si = (rep(rope[:, i, t - 1, :], 10) for i in range(2))
                    x2s, x2c = (work[:, 2 * (t - 1) + i, 0:320].rearrange("p (h d) -> p h d", d=FREQ)
                                for i in range(2))
                    pool.tensor_tensor(o[:, :, 0:FREQ], x1, co, ALU.mult)
                    pool.tensor_tensor(o[:, :, FREQ:HD], x1, si, ALU.mult)
                    pool.tensor_tensor(x2s, x2, si, ALU.mult)
                    step(pool.tensor_tensor(x2c, x2, co, ALU.mult))
                    pool.tensor_tensor(o[:, :, 0:FREQ], o[:, :, 0:FREQ], x2s, ALU.subtract)
                    pool.tensor_tensor(o[:, :, FREQ:HD], o[:, :, FREQ:HD], x2c, ALU.add).then_inc(s_rope, 1)
                pool.wait_ge(s_da, l + 1)
                for t in range(NT):
                    pool.wait_ge(s_xtc, 4 * l + t + 1)
                    for d in range(2):
                        last = pool.tensor_tensor(heads(xdt[:, d, t, :]), heads(xs_tok[:, t, :]),
                                                  bc(dt[:, d, t, :], HD), ALU.mult)
                last.then_inc(s_xdt, 1)
                pool.wait_ge(s_xdt, l + 1)
                pool.wait_ge(s_ecs, l + 1)
                for k, (d, t) in enumerate(STATES):
                    pool.tensor_tensor(heads(work[:, k, :]), heads(xdt[:, d, t, :]),
                                       bc(wend[:, d, t, :], HD), ALU.mult).then_inc(s_xw, 1)
                for t in range(NT):
                    pool.wait_ge(s_gss, NT * l + t + 1)
                    step(pool.tensor_scalar(gss[:, t, :], gss[:, t, :], 1.0 / 256, EPS, ALU.mult, ALU.add))
                    pool.tensor_tensor(grs[:, t, :], gss[:, t, :], epst[:, 0:2], ALU.pow).then_inc(s_grs, 1)
                for k in range(6):
                    pool.wait_ge(s_oc, 6 * l + k + 1)
                    hf, t = k // 3, k % 3
                    xx = x[:, t, hf * 512:(hf + 1) * 512]
                    pool.tensor_tensor(xx, xx, work[:, k % 4, :], ALU.add).then_inc(s_x1, 1)
                norm_rstd(2 * l + 1)
                pool.wait_ge(s_tr, KT * (2 * l + 2))
                pool.memset(acc[:, :, :], 0.0).then_inc(s_acc0, 1)
                for t in range(NT):
                    pool.wait_ge(s_fin, NT * l + t + 1)
                    pool.tensor_tensor(x[:, t, :], x[:, t, :], acc[:, t, :], ALU.add).then_inc(s_x2, 1)
            norm_rstd(2 * DEPTH)

        @block.scalar
        def _(act):
            dma = act.dma_start
            rows = lambda w: w.rearrange("l (k p) -> (l k) p", p=P)
            for dst, src in (
                    (prm_rows[0:16, :], rows(norm1_w)),
                    (prm_rows[16:32, :], rows(norm2_w)),
                    (prm_rows[32:40, :], c_ctx.rearrange("(k p) -> k p", p=P)),
                    (prm_rows[40:48, :], rows(c)),
                    (prm_rows[48:108, :], conv_w.rearrange("l t (m p) -> (l t m) p", p=P)),
                    (prm_rows[108:120, :], rows(conv_b)),
                    (bada_rows[0:96, :], rows(b_ada))):
                dma(dst, src).then_inc(s_rows, 16)
            dma(x[:, 0, :], x_prompt[0]).then_inc(s_x, 16)
            dma(x[:, 1:3, :], x_sample[0].rearrange("(t p) d -> p t d", p=P)).then_inc(s_x, 16)
            small = [(wr[:, :, :], w_router.rearrange("(k p) n -> p k n", p=P)),
                     (rb[:, :], router_bias.partition_broadcast(P)),
                     (rope[:, 0, :, :], rope_cos.rearrange("(t p) f -> p t f", p=P)),
                     (rope[:, 1, :, :], rope_sin.rearrange("(t p) f -> p t f", p=P))]
            for l in range(DEPTH):
                small += [(wdt[:, l, :, :], w_in[l, :, DT0:IN_W].rearrange("(k p) n -> p k n", p=P)),
                          (vec[:, l, 0:16], dt_bias[l].rearrange("d h -> (d h)").partition_broadcast(P)),
                          (vec[:, l, 16:32], a_log[l].rearrange("d h -> (d h)").partition_broadcast(P)),
                          (vec[:, l, 32:40], d_skip[l].partition_broadcast(P)),
                          (vec[:, l, 40:48], attn_sink[l].partition_broadcast(P)),
                          (ckv[:, 0, l, :], cache_k[0, l].rearrange("s k d -> s (k d)")),
                          (ckv[:, 1, l, :], cache_v[0, l].rearrange("s k d -> s (k d)"))]
            assert len(small) == SMALL
            for dst, src in small:
                dma(dst, src).then_inc(s_small, 16)

            act.wait_ge(s_prmT, 1)
            act.activation(prm[:, 0:120], bank[0][:, 0:120], ACT.Copy).then_inc(s_prm, 1)
            act.wait_ge(s_prm, 1)
            act.activation(cT[:, :, :].rearrange("p k g -> p g k"),
                           prm[:, 32:48].rearrange("p (g k) -> p g k", g=2), ACT.Silu).then_inc(s_cT, 1)
            act.wait_ge(s_small, 16 * SMALL)
            act.activation(vec[:, :, 16:32], vec[:, :, 16:32], ACT.Exp).then_inc(s_a, 1)

            def ada(l):
                for k in range(ADA_U * l, ADA_U * (l + 1)):
                    act.wait_ge(s_ada, k + 1)
                    if k >= 2:
                        act.wait_ge(s_rowT, k - 1)
                    act.activation(ada_row[0:2, k % 2, :], bank[6 + k % 2][0:2, :], ACT.Copy).then_inc(s_row, 1)

            def sumsq(k):
                l = (k - 1) // 2
                if k == 0:
                    act.wait_ge(s_x, 32)
                for t in range(NT):
                    if k % 2:
                        act.wait_ge(s_x1, 6 * l + 4 + t)
                        act.wait_ge(s_mt, KT * (l + 1))
                    elif k:
                        act.wait_ge(s_x2, NT * (k // 2 - 1) + t + 1)
                        if t == 0:
                            act.wait_ge(s_x2, NT * (k // 2))
                    act.activation(xn[:, t, :], x[:, t, :], ACT.Square,
                                   accum_out=ss[:, k, t:t + 1]).then_inc(s_ss, 1)

            def modulated(k):
                l, w = k // 2, k % 2
                act.wait_ge(s_amod, k + 1)
                for kt in range(0, KT, 2):
                    act.wait_ge(s_tr, KT * k + kt + 1)
                    for g, (a, b) in enumerate(((0, P), (P, 3 * P))):
                        last = act.activation(hT[:, kt, a:b], bank[kt][:, a:b], ACT.Identity,
                                              bias=modT[:, l, 24 * w + kt, g:g + 1],
                                              scale=amod[:, k, kt, g:g + 1])
                    last.then_inc(s_hA, 1)

            def gate_copies(l, w):
                for k in range(4):
                    act.wait_ge(s_gb, 8 * l + 4 * w + k + 1)
                    if w and k == 0:
                        act.wait_ge(s_oc, 6 * (l + 1))
                    act.activation(gateB[:, k // 2, (k % 2) * 512:(k % 2 + 1) * 512], bank[6 + k % 2][:, :],
                                   ACT.Copy).then_inc(s_gbc, 1)

            for l in range(DEPTH):
                ada(l)
                sumsq(2 * l)
                modulated(2 * l)
                for t in range(NT):
                    act.wait_ge(s_q, NT * l + t + 1)
                    act.activation(qkv[:, t, 0:AW].rearrange("p (j a d) -> p a j d", a=2, d=HD),
                                   bank[t][:, :].rearrange("p (a j d) -> p a j d", a=2, d=HD),
                                   ACT.Copy).then_inc(s_qc, 1)
                act.wait_ge(s_zero, l + 1)
                for m in range(XM):
                    act.wait_ge(s_xbc, XM * l + m + 1)
                    b = bank[(6 + m) % 8]
                    act.activation(xpd[:, m, 2:2 + P], b[:, 0:P], ACT.Copy)
                    act.activation(xpd[:, m, 134:390], b[:, P:3 * P], ACT.Copy).then_inc(s_xbcc, 1)
                for t in range(NT):
                    act.wait_ge(s_z, NT * l + t + 1)
                    act.activation(mixed[:, t, 512:1024], bank[4 + t][:, :], ACT.Silu).then_inc(s_zc, 1)
                act.wait_ge(s_kvc, NT * l + 1)
                dma(new_k[0, l].rearrange("s k d -> s (k d)"), qkv[:, 0, 512:640]).then_inc(s_out, 16)
                dma(new_v[0, l].rearrange("s k d -> s (k d)"), qkv[:, 0, 640:768]).then_inc(s_out, 16)
                for m in range(XM):
                    act.wait_ge(s_conv, XM * l + m + 1)
                    act.activation(conv[:, m, :], conv[:, m, :], ACT.Silu).then_inc(s_silu, 1)
                for i in range(4):
                    act.wait_ge(s_qtr, 4 * l + i + 1)
                    dst = qT[:, i, :, :] if i < 3 else kT[:, :, :]
                    act.activation(dst.rearrange("p a b -> p (a b)"), bank[(7, 0, 1, 2)[i]][:, :],
                                   ACT.Copy).then_inc(s_qTc, 1)
                act.wait_ge(s_dt1, 2 * l + 1)
                act.activation(dtu[:, :, :, :], dtu[:, :, :, :], ACT.Exp, scale=-1.0).then_inc(s_dt2, 1)
                act.wait_ge(s_dt1, 2 * l + 2)
                act.activation(dtw[:, :, :, :], dtv[:, :, :, :], ACT.Ln).then_inc(s_dt2, 1)
                for t in range(NT):
                    nk = P if t == 0 else 3 * P
                    act.wait_ge(s_nm, NT * l + t + 1)
                    for h in range(H):
                        act.activation(probs[:, h, 0:nk], probs[:, h, 0:nk], ACT.Exp, scale=SCALE,
                                       bias=nm[:, t, h:h + 1], accum_out=rs[:, t, h:h + 1]).then_inc(s_exp, 1)
                    act.activation(es[:, t, :], es[:, t, :], ACT.Exp).then_inc(s_es, 1)
                act.wait_ge(s_attn, NT * (l + 1))
                dma(snw, ssd_norm_w[l].partition_broadcast(P)).then_inc(s_snw, 16)
                for i in range(4):
                    act.wait_ge(s_xtr, 5 * l + i + 1)
                    dst = xs_tok[:, i, :] if i < NT else b_tok[:, :, :].rearrange("p t c -> p (t c)")
                    act.activation(dst, bank[i][:, 0:512 if i < NT else NT * P], ACT.Copy).then_inc(s_xtc, 1)
                act.wait_ge(s_xtr, 5 * l + 5)
                act.activation(init_st[:, :, :].rearrange("p d c -> p (d c)"), bank[4][:, :],
                               ACT.Copy).then_inc(s_stc, 1)
                act.wait_ge(s_cs, l + 1)
                act.activation(ecs[:, :, :, :], cs[:, :, :, :], ACT.Exp)
                act.activation(etot[:, :, :, :], tot[:, :, :, :], ACT.Exp)
                act.activation(wend[:, :, :, :], wend[:, :, :, :], ACT.Exp).then_inc(s_ecs, 1)
                act.wait_ge(s_sto, l + 1)
                act.activation(st_out, bank[2][:, :], ACT.Copy).then_inc(s_stoc, 1)
                act.wait_ge(s_stoc, l + 1)
                for d in range(2):
                    for jj in range(2):
                        dma(new_state[0, l, d].rearrange("(g j hh) p n -> j (hh p) g n", g=2, j=2)[jj],
                            st_out.rearrange("p (d j g n) -> p d j g n", d=2, j=2, g=2)[:, d, jj]
                            ).then_inc(s_out, 16)
                for k in range(12):
                    act.wait_ge(s_seg, 12 * l + k + 1)
                    act.activation(work[:, k % 2, :], work[:, k % 2, :], ACT.Exp).then_inc(s_dexp, 1)
                gate_copies(l, 0)
                for kt in range(0, KT, 2):
                    act.wait_ge(s_mt, KT * l + kt + 1)
                    act.activation(hT[:, kt, :], bank[kt][:, 0:3 * P], ACT.Copy).then_inc(s_mA, 1)
                sumsq(2 * l + 1)
                modulated(2 * l + 1)
                act.wait_ge(s_r, l + 1)
                act.activation(rt[:, 0, :, :].rearrange("p t e -> p (t e)"), bank[0][:, 0:NT * E], ACT.Exp,
                               scale=-1.0).then_inc(s_re, 1)
                gate_copies(l, 1)
                with act.Fori(0, E) as e:
                    for f in range(2):
                        act.wait_ge(s_gate_mm, 2 * e + (2 * E * l + f + 1))
                        act.wait_ge(s_hid, 2 * e + (2 * E * l + f + 1))
                        act.activation(sil[:, f, :], bank[2 * f][:, 0:3 * P], ACT.Silu).then_inc(s_sil, 1)
            act.wait_ge(s_fin, NT * DEPTH)
            dma(gateB[:, 0, :], final_norm_w.partition_broadcast(P)).then_inc(s_fnw, 16)
            sumsq(2 * DEPTH)

        @block.vector
        def _(dve):
            n = [0]

            def step(ins):
                n[0] += 1
                ins.then_inc(s_dve, 1)
                dve.wait_ge(s_dve, n[0])

            dve.sem_inc(s_hid, 2)
            dve.sem_inc(s_acc, 4)
            dve.wait_ge(s_prmT, 2)
            dve.tensor_copy(bada[:, :], bank[1][:, 0:96]).then_inc(s_bada, 1)
            dve.wait_ge(s_bada, 1)
            dve.wait_ge(s_a, 1)
            step(dve.tensor_scalar(vec[:, :, 16:32], vec[:, :, 16:32], -1.0, None, ALU.mult))

            def ada(l):
                for j in range(ADA_U):
                    k = ADA_U * l + j
                    dve.wait_ge(s_rowT, k + 1)
                    dve.tensor_tensor(modT[:, l, 4 * j:4 * j + 4, :],
                                      bank[4 + k % 2][:, 0:8].rearrange("p (j g) -> p j g", g=2),
                                      bc(bada[:, 48 * l + 4 * j:48 * l + 4 * j + 4], 2), ALU.add
                                      ).then_inc(s_mod, 1)
                dve.wait_ge(s_mod, ADA_U * (l + 1))
                if l == 0:
                    dve.wait_ge(s_prm, 1)
                for w in range(2):
                    dve.scalar_tensor_tensor(
                        out=amod[:, 2 * l + w, :, :], in0=modT[:, l, 24 * w + 8:24 * w + 16, :], scalar=1.0,
                        in1=bc(prm[:, 16 * w + 8 * l:16 * w + 8 * l + 8], 2), op0=ALU.add, op1=ALU.mult
                    ).then_inc(s_amod, 1)

            def normed(k):
                dve.wait_ge(s_rstd, k + 1)
                for t in range(NT):
                    dve.tensor_scalar(xn[:, t, :], x[:, t, :], rstd[:, k, t:t + 1], None,
                                      ALU.mult).then_inc(s_xn, 1)

            def modulated(k):
                l, w = k // 2, k % 2
                dve.wait_ge(s_amod, k + 1)
                for kt in range(1, KT, 2):
                    dve.wait_ge(s_tr, KT * k + kt + 1)
                    for g, (a, b) in enumerate(((0, P), (P, 3 * P))):
                        last = dve.tensor_scalar(hT[:, kt, a:b], bank[kt][:, a:b], amod[:, k, kt, g:g + 1],
                                                 modT[:, l, 24 * w + kt, g:g + 1], ALU.mult, ALU.add)
                    last.then_inc(s_hD, 1)

            def gate_diags(l, w):
                for k in range(4):
                    i = 8 * l + 4 * w + k
                    if i:
                        dve.wait_ge(s_gb, i)
                    if w == 0 and k == 0:
                        dve.wait_ge(s_out, 16 * STORES * (l + 1))
                    col = 16 + 24 * w + 4 * (k % 2)
                    dve.tensor_tensor(diag[:, :, :], rep(ident[:, :], 4),
                                      bc(modT[:, l, col:col + 4, k // 2], P), ALU.mult).then_inc(s_dg, 1)

            for l in range(DEPTH):
                ada(l)
                normed(2 * l)
                modulated(2 * l)
                for t in range(NT):
                    dve.wait_ge(s_kv, NT * l + t + 1)
                    dve.tensor_copy(qkv[:, t, 512:768], bank[3 + t][:, 0:256])
                    dve.tensor_tensor(dtr[:, :, t, :], bank[3 + t][:, 256:272].rearrange("p (d h) -> p d h", d=2),
                                      vec[:, l, 0:16].rearrange("p (d h) -> p d h", d=2), ALU.add
                                      ).then_inc(s_kvc, 1)
                dve.wait_ge(s_kvc, NT * (l + 1))
                flat = lambda v: v[:, :, :, :].rearrange("p d t h -> p (d t h)")
                dve.scalar_tensor_tensor(out=flat(dtu), in0=flat(dtr), scalar=-1.0, in1=flat(dtr),
                                         op0=ALU.mult, op1=ALU.max).then_inc(s_dt1, 1)
                for m in range(XM):
                    dve.wait_ge(s_xbcc, XM * l + m + 1)
                    tap = lambda k: prm[:, 48 + 30 * l + 6 * k + m:49 + 30 * l + 6 * k + m]
                    bias = prm[:, 108 + 6 * l + m:109 + 6 * l + m]
                    step(dve.tensor_scalar(conv[:, m, :], xpd[:, m, 0:CONVW], tap(0), bias, ALU.mult, ALU.add))
                    for k in range(1, TAPS):
                        ins = dve.scalar_tensor_tensor(out=conv[:, m, :], in0=xpd[:, m, k:k + CONVW], scalar=tap(k),
                                                       in1=conv[:, m, :], op0=ALU.mult, op1=ALU.add)
                        if k < TAPS - 1:
                            step(ins)
                    ins.then_inc(s_conv, 1)
                dve.wait_ge(s_dt2, 2 * l + 1)
                dve.tensor_scalar(dtv[:, :, :, :], dtu[:, :, :, :], 1.0, None, ALU.add).then_inc(s_dt1, 1)
                dve.wait_ge(s_dt1, 2 * l + 2)
                step(dve.tensor_scalar(dt[:, :, :, :], dtv[:, :, :, :], 1.0, None, ALU.subtract))
                step(dve.tensor_tensor(dtu[:, :, :, :], dtu[:, :, :, :], dt[:, :, :, :], ALU.subtract))
                dve.wait_ge(s_dt2, 2 * l + 2)
                step(dve.reciprocal(dtv[:, :, :, :], dtv[:, :, :, :]))
                step(dve.tensor_tensor(dtu[:, :, :, :], dtu[:, :, :, :], dtv[:, :, :, :], ALU.mult))
                step(dve.tensor_tensor(dtu[:, :, :, :], dtu[:, :, :, :], dtw[:, :, :, :], ALU.add))
                step(dve.scalar_tensor_tensor(out=flat(dt), in0=flat(dtr), scalar=0.0, in1=flat(dtu),
                                              op0=ALU.max, op1=ALU.add))
                for d in range(2):
                    ins = dve.tensor_tensor(da[:, d, :, :], dt[:, d, :, :],
                                            rep(vec[:, l, 16 + 8 * d:24 + 8 * d], NT), ALU.mult)
                ins.then_inc(s_da, 1)

                def masked(t, h):
                    k = 24 * l + 8 * t + h
                    nk, m0 = ((P, 2), (3 * P, 2), (3 * P, 0))[t]
                    dve.wait_ge(s_sc, k + 1)
                    dve.tensor_tensor_reduce(out=probs[:, h, 0:nk], in0=bank[(8 * t + h) % 3][:, 0:nk],
                                             in1=amask[:, m0:m0 + nk // P, :].rearrange("p a b -> p (a b)"),
                                             scale=1.0, scalar=2 * NEG, op0=ALU.add, op1=ALU.max,
                                             accum_out=mx[:, t, h:h + 1]).then_inc(s_scc, 1)

                def maxima(t):
                    dve.wait_ge(s_scc, 24 * l + 8 * (t + 1))
                    step(dve.scalar_tensor_tensor(out=mx[:, t, :], in0=mx[:, t, :], scalar=SCALE,
                                                  in1=vec[:, l, 40:48], op0=ALU.mult, op1=ALU.max))
                    dve.tensor_tensor(es[:, t, :], vec[:, l, 40:48], mx[:, t, :], ALU.subtract)
                    dve.tensor_scalar(nm[:, t, :], mx[:, t, :], -1.0, None, ALU.mult).then_inc(s_nm, 1)

                for h in range(H):
                    masked(0, h)
                maxima(0)
                for t in range(NT):
                    nk = P if t == 0 else 3 * P
                    for h in range(H):
                        k = 24 * l + 8 * t + h
                        dve.wait_ge(s_ptr, k + 1)
                        if k >= 2:
                            dve.wait_ge(s_pv, k - 1)
                        dve.tensor_copy(pT[:, h % 2, 0:nk], bank[3 + h % 2][:, 0:nk]).then_inc(s_pTc, 1)
                        if t + 1 < NT:
                            masked(t + 1, h)
                    if t + 1 < NT:
                        maxima(t + 1)
                    dve.wait_ge(s_es, NT * l + t + 1)
                    step(dve.tensor_tensor(den[:, t, :], rs[:, t, :], es[:, t, :], ALU.add))
                    step(dve.reciprocal(den[:, t, :], den[:, t, :]))
                    dve.wait_ge(s_pv, 24 * l + 8 * (t + 1))
                    dve.tensor_tensor(heads(mixed[:, t, 0:512]), heads(bank[5 + t][:, :]),
                                      bc(den[:, t, :], HD), ALU.mult).then_inc(s_attn, 1)

                dve.wait_ge(s_cum, l + 1)
                dve.tensor_copy(flat(cs), bank[5][:, 0:48])
                step(dve.tensor_copy(flat(tot), bank[5][:, 48:96]))
                dve.tensor_tensor(wend[:, :, :, :], tot[:, :, :, :], cs[:, :, :, :], ALU.subtract).then_inc(s_cs, 1)
                dve.wait_ge(s_g, l + 1)
                for d in range(2):
                    for g in range(2):
                        ins = dve.tensor_tensor(gm[:, d, :, g, :], heads(bank[6 + g][:, 0:NT * P], NT),
                                                rep(tri[:, d, :], NT), ALU.mult)
                ins.then_inc(s_gm, 1)
                dve.wait_ge(s_st, 2 * l + 1)
                dve.tensor_copy(final_st[:, :, :].rearrange("p d c -> p (d c)"), bank[0][:, :]).then_inc(s_ctxs, 1)
                dve.wait_ge(s_stc, l + 1)
                dve.wait_ge(s_ecs, l + 1)
                for d, t in STATES[2:]:
                    for g in range(2):
                        r = slice(g * HD, (g + 1) * HD)
                        ins = dve.tensor_tensor(heads(next_st[r, d, :], 4), heads(init_st[r, d, :], 4),
                                                bc(etot[r, d, t, 4 * g:4 * g + 4], HD), ALU.mult)
                step(ins)
                dve.wait_ge(s_st, 2 * l + 2)
                nx = next_st[:, :, :].rearrange("p d c -> p (d c)")
                dve.tensor_tensor(nx, nx, bank[1][:, :], ALU.add).then_inc(s_snx, 1)

                def seg(k):
                    t, g, d = k // 4, k // 2 % 2, k % 2
                    dve.wait_ge(s_cdec, 12 * l + k + 1)
                    if k >= 2:
                        dve.wait_ge(s_scm, 12 * l + k - 1)
                    w = heads(work[:, k % 2, :], 4)
                    step(dve.tensor_tensor(w, heads(bank[1 + k % 2][:, :], 4),
                                           bc(cs[:, d, t, 4 * g:4 * g + 4], P), ALU.subtract))
                    dve.tensor_scalar(work[:, k % 2, :], work[:, k % 2, :], 0.0, None, ALU.min).then_inc(s_seg, 1)

                def decayed(k):
                    t, g, d = k // 4, k // 2 % 2, k % 2
                    dve.wait_ge(s_dexp, 12 * l + k + 1)
                    if k >= 3:
                        dve.wait_ge(s_y, 6 * l + (k - 3) // 2 + 1)
                    dve.tensor_tensor(heads(scT[:, k % 3, :], 4), heads(work[:, k % 2, :], 4),
                                      rep(gm[:, d, t, g, :], 4), ALU.mult).then_inc(s_scm, 1)

                def finish(t):
                    v = xs_tok[:, t, :]
                    dve.wait_ge(s_xdt, l + 1)
                    step(dve.tensor_tensor(heads(v), heads(v), bc(vec[:, l, 32:40], HD), ALU.mult))
                    dve.wait_ge(s_y, 6 * l + 2 * t + 2)
                    step(dve.tensor_tensor(v, v, bank[6 + t % 2][:, :], ALU.add))
                    if t:
                        dve.wait_ge(s_yoff, 4 * (l + 1))
                        for g in range(2):
                            for d in range(2):
                                ins = dve.tensor_tensor(heads(work[:, 2 + g, d * 256:(d + 1) * 256], 4),
                                                        heads(bank[YOFF_BANK[t, g]][:, d * 256:(d + 1) * 256], 4),
                                                        bc(ecs[:, d, t, 4 * g:4 * g + 4], HD), ALU.mult)
                        step(ins)
                        for d in range(2):
                            step(dve.tensor_tensor(heads(v, 2), heads(v, 2), work[:, 2:4, d * 256:(d + 1) * 256],
                                                   ALU.add))
                    z = mixed[:, t, 512:1024]
                    step(dve.tensor_tensor(z, v, z, ALU.mult))
                    for g in range(2):
                        zg = z[:, g * 256:(g + 1) * 256]
                        ins = dve.tensor_tensor_reduce(out=work[:, 2, g * 256:(g + 1) * 256], in0=zg, in1=zg, scale=1.0,
                                                       scalar=0.0, op0=ALU.mult, op1=ALU.add,
                                                       accum_out=gss[:, t, g:g + 1])
                    ins.then_inc(s_gss, 1)
                    dve.wait_ge(s_grs, NT * l + t + 1)
                    for g in range(2):
                        zg = z[:, g * 256:(g + 1) * 256]
                        ins = dve.scalar_tensor_tensor(out=zg, in0=zg, scalar=grs[:, t, g:g + 1],
                                                       in1=snw[:, g * 256:(g + 1) * 256],
                                                       op0=ALU.mult, op1=ALU.mult)
                    ins.then_inc(s_ssd, 1)

                dve.wait_ge(s_snw, 16 * (l + 1))
                seg(0)
                for k in range(12):
                    if k + 1 < 12:
                        seg(k + 1)
                    decayed(k)
                    if k % 4 == 3:
                        finish(k // 4)

                gate_diags(l, 0)
                for kt in range(1, KT, 2):
                    dve.wait_ge(s_mt, KT * l + kt + 1)
                    dve.tensor_copy(hT[:, kt, :], bank[kt][:, 0:3 * P]).then_inc(s_mD, 1)
                dve.wait_ge(s_gbc, 8 * l + 4)
                for k in range(6):
                    hf, t = k // 3, k % 3
                    dve.wait_ge(s_o, 6 * l + k + 1)
                    if k >= 4:
                        dve.wait_ge(s_x1, 6 * l + k - 3)
                    dve.tensor_tensor(work[:, k % 4, :], bank[k][:, :],
                                      gateB[:, grp(t), hf * 512:(hf + 1) * 512], ALU.mult).then_inc(s_oc, 1)
                normed(2 * l + 1)
                modulated(2 * l + 1)

                R = lambda i: rt[:, i, :, :].rearrange("p t e -> p (t e)")
                G4 = lambda v: v.rearrange("p (a j) -> p a j", j=4)
                E3 = lambda v: v.rearrange("p (t e) -> p t e", e=E)
                dve.wait_ge(s_re, l + 1)
                if l == 0:
                    for e in range(E):
                        dve.memset(tie[:, 0, :, e:e + 1], float(E - e))
                    for g in range(4):
                        ins = dve.memset(tie[:, 1, :, g:g + 1], float(4 - g))
                    step(ins)
                step(dve.tensor_scalar(R(0), R(0), 1.0, None, ALU.add))
                step(dve.reciprocal(R(0), R(0)))
                step(dve.tensor_tensor(E3(R(1)), E3(R(0)), rep(rb[:, :], NT), ALU.add))
                s4, p4, q4 = G4(R(1)), G4(R(2)), G4(R(3))
                dve.tensor_tensor(p4[:, :, 0:3], s4[:, :, 0:3], s4[:, :, 1:4], ALU.add)
                dve.tensor_tensor(q4[:, :, 0:2], s4[:, :, 0:2], s4[:, :, 2:4], ALU.add)
                step(dve.tensor_tensor(p4[:, :, 3:4], s4[:, :, 0:1], s4[:, :, 3:4], ALU.add))
                step(dve.tensor_tensor(q4[:, :, 0:2], q4[:, :, 0:2], p4[:, :, 0:2], ALU.max))
                step(dve.tensor_tensor(q4[:, :, 0:2], q4[:, :, 0:2], p4[:, :, 2:4], ALU.max))
                gs = rt[:, 4, :, 0:4]
                step(dve.tensor_tensor(gs, q4[:, :, 0:1].rearrange("p (t a) j -> p t (a j)", t=NT),
                                       q4[:, :, 1:2].rearrange("p (t a) j -> p t (a j)", t=NT), ALU.max))
                gmax = rt[:, 4, :, 4:5]

                def first_of_max(v, m, weight, width):
                    step(dve.tensor_reduce(m, v, AX.X, ALU.max))
                    step(dve.tensor_tensor(v, v, m.broadcast_to([P, NT, width]), ALU.is_equal))
                    step(dve.tensor_tensor(v, v, weight, ALU.mult))
                    step(dve.tensor_reduce(m, v, AX.X, ALU.max))
                    step(dve.tensor_tensor(v, v, m.broadcast_to([P, NT, width]), ALU.is_equal))

                first_of_max(gs, gmax, tie[:, 1, :, 0:4], 4)
                ing = rt[:, 5, :, :]
                step(dve.tensor_copy(ing.rearrange("p t (a j) -> p t a j", j=4),
                                     gs.unsqueeze(3).broadcast_to([P, NT, 4, 4])))
                off = rt[:, 6, :, :]
                step(dve.tensor_scalar(off, ing, -NEG, NEG, ALU.mult, ALU.add))
                step(dve.tensor_tensor(R(2), R(1), R(5), ALU.mult))
                step(dve.tensor_tensor(R(2), R(2), R(6), ALU.add))
                step(dve.tensor_copy(R(3), R(2)))
                first_of_max(rt[:, 3, :, :], rt[:, 4, :, 5:6], tie[:, 0, :, :], E)
                step(dve.tensor_scalar(R(5), R(3), 4 * NEG, None, ALU.mult))
                step(dve.tensor_tensor(R(2), R(2), R(5), ALU.add))
                first_of_max(rt[:, 2, :, :], rt[:, 4, :, 6:7], tie[:, 0, :, :], E)
                step(dve.tensor_tensor(R(3), R(3), R(2), ALU.add))
                step(dve.tensor_tensor(R(3), R(3), R(0), ALU.mult))
                step(dve.tensor_reduce(rt[:, 4, :, 7:8], rt[:, 3, :, :], AX.X, ALU.add))
                step(dve.reciprocal(rt[:, 4, :, 7:8], rt[:, 4, :, 7:8]))
                step(dve.tensor_tensor(gates[:, :, :], rt[:, 3, :, :],
                                       rt[:, 4, :, 7:8].broadcast_to([P, NT, E]), ALU.mult))
                gate_diags(l, 1)

                def hidden(e, b):
                    for f in range(2):
                        dve.wait_ge(s_sil, 2 * e + (2 * E * l + f + 1))
                        dve.wait_ge(s_up_mm, 2 * e + (2 * E * l + f + 1))
                        dve.tensor_tensor(hid[:, b, f, :], sil[:, f, :], bank[2 * f + 1][:, 0:3 * P],
                                          ALU.mult).then_inc(s_hid, 1)

                def added(e, b):
                    for o in range(6):
                        t, hf = o // 2, o % 2
                        dve.wait_ge(s_dn, 6 * e + (ADD * l + o + 1))
                        dve.wait_ge(s_acc, 6 * e + (ADD * l + o + 1))
                        a = acc[:, t, hf * 512:(hf + 1) * 512]
                        dve.scalar_tensor_tensor(out=a, in0=bank[4 + (6 * b + o) % 4][:, :],
                                                 scalar=gates[:, t, bass.ds(e, 1)], in1=a,
                                                 op0=ALU.mult, op1=ALU.add).then_inc(s_acc, 1)

                dve.wait_ge(s_acc0, l + 1)
                hidden(0, 0)
                with dve.Fori(0, E // 2 - 1) as i:
                    hidden(2 * i + 1, 1)
                    added(2 * i, 0)
                    hidden(2 * i + 2, 0)
                    added(2 * i + 1, 1)
                hidden(E - 1, 1)
                added(E - 2, 0)
                added(E - 1, 1)
                dve.wait_ge(s_acc, ADD * (l + 1) + 4)
                dve.wait_ge(s_gbc, 8 * l + 8)
                for t in range(NT):
                    dve.tensor_tensor(acc[:, t, :], acc[:, t, :], gateB[:, grp(t), :], ALU.mult).then_inc(s_fin, 1)
            dve.wait_ge(s_rstd, 2 * DEPTH + 1)
            dve.wait_ge(s_fnw, 16)
            for t in range(NT):
                dve.scalar_tensor_tensor(out=xn[:, t, :], in0=x[:, t, :], scalar=rstd[:, 2 * DEPTH, t:t + 1],
                                         in1=gateB[:, 0, :], op0=ALU.mult, op1=ALU.mult).then_inc(s_y_out, 1)

        @block.tensor
        def _(pe):
            mm, tr = pe.matmul, pe.transpose

            def arrived(u):
                pe.wait_ge(landed[u % SLOTS], 32 * (u // SLOTS + 1))

            pe.wait_ge(s_const, 1)
            pe.wait_ge(s_rows, 16 * 7)
            tr(bank[0][:, 0:120], prm_rows[0:120, :], ident[0:120, 0:120]).then_inc(s_prmT, 1)
            tr(bank[1][:, 0:96], bada_rows[0:96, :], ident[0:96, 0:96]).then_inc(s_prmT, 1)

            def ada(l, u0):
                def columns(k):
                    pe.wait_ge(s_row, k + 1)
                    if k >= 2:
                        pe.wait_ge(s_mod, k - 1)
                    for j in range(4):
                        last = tr(bank[4 + k % 2][:, 2 * j:2 * j + 2], ada_row[0:2, k % 2, j * P:(j + 1) * P],
                                  ident[0:2, 0:2])
                    last.then_inc(s_rowT, 1)

                for j in range(ADA_U):
                    k, u = ADA_U * l + j, u0 + j
                    arrived(u)
                    if k >= 2:
                        pe.wait_ge(s_row, k - 1)
                    for kt in range(KT):
                        last = mm(bank[6 + k % 2][0:2, :], cT[:, kt, :], slot(u)[:, kt, :],
                                  start=kt == 0, stop=kt == KT - 1)
                    last.then_inc(s_ada, 1)
                    if j:
                        columns(k - 1)
                    pe.wait_ge(s_ada, k + 1)
                    pe.sem_inc(freed[u % SLOTS], 1)
                columns(ADA_U * (l + 1) - 1)

            def norm_transposes(k):
                for t in range(NT):
                    pe.wait_ge(s_xn, NT * k + t + 1)
                for kt in range(KT):
                    for t in range(NT):
                        last = tr(bank[kt][:, t * P:(t + 1) * P], xn[:, t, kt * P:(kt + 1) * P], ident[:, :])
                    last.then_inc(s_tr, 1)
                pe.wait_ge(s_hA, 4 * (k + 1))
                pe.wait_ge(s_hD, 4 * (k + 1))

            def gate_rows(l, w):
                for k in range(4):
                    i = 8 * l + 4 * w + k
                    pe.wait_ge(s_dg, i + 1)
                    if k >= 2:
                        pe.wait_ge(s_gbc, i - 1)
                    mm(bank[6 + k % 2][:, :], ones[:, :], diag[:, :, :].rearrange("p a c -> p (a c)"),
                       start=True, stop=True).then_inc(s_gb, 1)

            pe.wait_ge(s_cT, 1)
            pe.wait_ge(s_bada, 1)
            u = 0
            for l in range(DEPTH):
                if l:
                    pe.wait_ge(s_acc, ADD * l + 4)
                ada(l, u)
                u += ADA_U
                pe.wait_ge(s_mod, ADA_U * (l + 1))
                norm_transposes(2 * l)

                tok = lambda kt, t: hT[:, kt, t * P:(t + 1) * P]
                arrived(u)
                for t in range(NT):
                    for kt in range(KT):
                        last = mm(bank[t][:, :], tok(kt, t), slot(u)[:, kt, :], start=kt == 0, stop=kt == KT - 1)
                    last.then_inc(s_q, 1)
                pe.wait_ge(s_q, NT * (l + 1))
                pe.sem_inc(freed[u % SLOTS], 1)
                arrived(u + 1)
                if l == 0:
                    pe.wait_ge(s_small, 16 * SMALL)
                for t in range(NT):
                    for kt in range(KT):
                        mm(bank[3 + t][:, 0:256], tok(kt, t), slot(u + 1)[:, kt, 0:256],
                           start=kt == 0, stop=kt == KT - 1)
                    for kt in range(KT):
                        last = mm(bank[3 + t][:, 256:272], tok(kt, t), wdt[:, l, kt, :],
                                  start=kt == 0, stop=kt == KT - 1)
                    last.then_inc(s_kv, 1)
                for m in range(XM):
                    v, col = (u + 1, 256 + m * P) if m < 2 else (u + 2, (m - 2) * P)
                    if m == 2:
                        pe.sem_inc(freed[(u + 1) % SLOTS], 1)
                        arrived(v)
                    if 2 <= m < 5:
                        pe.wait_ge(s_qc, NT * l + m - 1)
                    if m == 5:
                        pe.wait_ge(s_kvc, NT * l + 1)
                    for kt in range(KT):
                        last = mm(bank[(6 + m) % 8][:, 0:3 * P], slot(v)[:, kt, col:col + P], hT[:, kt, :],
                                  start=kt == 0, stop=kt == KT - 1)
                    last.then_inc(s_xbc, 1)
                    if m in (1, 5):
                        pe.wait_ge(s_xbc, XM * l + m + 1)
                pe.sem_inc(freed[(u + 2) % SLOTS], 1)
                arrived(u + 3)
                for t in range(NT):
                    if t < 2:
                        pe.wait_ge(s_kvc, NT * l + t + 2)
                    else:
                        pe.wait_ge(s_xbcc, XM * l + 1)
                    for kt in range(KT):
                        last = mm(bank[4 + t][:, :], tok(kt, t), slot(u + 3)[:, kt, :],
                                  start=kt == 0, stop=kt == KT - 1)
                    last.then_inc(s_z, 1)
                pe.wait_ge(s_z, NT * (l + 1))
                pe.sem_inc(freed[(u + 3) % SLOTS], 1)
                u += IN_U

                for t in range(NT):
                    pe.wait_ge(s_xbcc, XM * l + t + 2)
                    if t:
                        pe.wait_ge(s_rope, 2 * l + t)
                    else:
                        pe.wait_ge(s_qc, NT * l + 1)
                        pe.wait_ge(s_kvc, NT * l + 1)
                    src = qkv[:, 0, 0:512] if t == 0 else rot[:, t - 1, 0:512]
                    for j in range(4):
                        last = tr(bank[(7, 0, 1)[t]][:, j * P:(j + 1) * P], src[:, j * P:(j + 1) * P], ident[:, :])
                    last.then_inc(s_qtr, 1)
                pe.wait_ge(s_xbcc, XM * l + 5)
                for i, src in enumerate((ckv[:, 0, l, :], rot[:, 0, 512:640], rot[:, 1, 512:640], qkv[:, 0, 512:640])):
                    last = tr(bank[2][:, i * P:(i + 1) * P], src, ident[:, :])
                last.then_inc(s_qtr, 1)

                def scores(t, h):
                    k = 24 * l + 8 * t + h
                    if 8 * t + h >= 3:
                        pe.wait_ge(s_scc, k - 2)
                    r = slice(HD * (h // 4), HD * (h // 4 + 1))
                    keys = kT[r, 3:4, :] if t == 0 else kT[r, 0:3, :]
                    nk = P if t == 0 else 3 * P
                    mm(bank[(8 * t + h) % 3][:, 0:nk], qT[r, t, h % 4, :], keys.rearrange("p a c -> p (a c)"),
                       start=True, stop=True).then_inc(s_sc, 1)

                pe.wait_ge(s_qTc, 4 * (l + 1))
                pe.wait_ge(s_zc, NT * (l + 1))
                pe.wait_ge(s_xbcc, XM * (l + 1))
                for h in range(H):
                    scores(0, h)
                for t in range(NT):
                    parts = 1 if t == 0 else 3
                    for h in range(H):
                        k = 24 * l + 8 * t + h
                        pe.wait_ge(s_exp, k + 1)
                        if 8 * t + h >= 2:
                            pe.wait_ge(s_pTc, k - 1)
                        for a in range(parts):
                            last = tr(bank[3 + h % 2][:, a * P:(a + 1) * P], probs[:, h, a * P:(a + 1) * P],
                                      ident[:, :])
                        last.then_inc(s_ptr, 1)
                        if t + 1 < NT:
                            scores(t + 1, h)
                        pe.wait_ge(s_pTc, k + 1)
                        kv = HD * (h // 4)
                        vals = (qkv[:, 0, 640:768],) if t == 0 else (ckv[:, 1, l, :], qkv[:, 1, 640:768],
                                                                     qkv[:, 2, 640:768])
                        for a in range(parts):
                            last = mm(bank[5 + t][:, h * HD:(h + 1) * HD], pT[:, h % 2, a * P:(a + 1) * P],
                                      vals[a][:, kv:kv + HD], start=a == 0, stop=a == parts - 1)
                        last.then_inc(s_pv, 1)

                pe.wait_ge(s_silu, XM * (l + 1))
                for t in range(NT):
                    o = tile_at(t)
                    for m in range(4):
                        last = tr(bank[t][:, m * P:(m + 1) * P], conv[:, m, o:o + P], ident[:, :])
                    last.then_inc(s_xtr, 1)
                for t in range(NT):
                    o = tile_at(t)
                    last = tr(bank[3][:, t * P:(t + 1) * P], conv[:, 4, o:o + P], ident[:, :])
                last.then_inc(s_xtr, 1)
                pe.wait_ge(s_state, 64 * (l + 1))
                for d in range(2):
                    for jj in range(2):
                        i = 2 * d + jj
                        last = tr(bank[4][:, i * P:(i + 1) * P],
                                  st_in[:, d, jj, :, :].rearrange("p g n -> p (g n)"), ident[:, :])
                last.then_inc(s_xtr, 1)
                pe.wait_ge(s_da, l + 1)
                pe.wait_ge(s_attn, NT * (l + 1))
                for d in range(2):
                    mm(bank[5][:, 24 * d:24 * d + 24], tri[:, d, :], da[:, d, :, :].rearrange("p t h -> p (t h)"),
                       start=True, stop=True)
                mm(bank[5][:, 48:96], ones[:, :], da[:, :, :, :].rearrange("p d t h -> p (d t h)"),
                   start=True, stop=True).then_inc(s_cum, 1)
                for i in range(6):
                    t, g = i // 2, i % 2
                    o, r = tile_at(t), slice(g * HD, (g + 1) * HD)
                    last = mm(bank[6 + g][:, t * P:(t + 1) * P], conv[r, 4, o:o + P],
                              conv[r, 5, o:o + P], start=True, stop=True)
                last.then_inc(s_g, 1)
                pe.wait_ge(s_xtc, 4 * (l + 1))
                for k, (d, t) in enumerate(STATES):
                    pe.wait_ge(s_xw, 4 * l + k + 1)
                    for g in range(2):
                        r = slice(g * HD, (g + 1) * HD)
                        last = mm(bank[k // 2][r, d * 256:(d + 1) * 256], b_tok[:, t, g * HD:(g + 1) * HD],
                                  work[:, k, g * 256:(g + 1) * 256], start=True, stop=True)
                    if k % 2:
                        last.then_inc(s_st, 1)
                pe.wait_ge(s_ctxs, l + 1)
                for i in range(4):
                    last = tr(bank[2][:, i * P:(i + 1) * P], final_st[:, i // 2, (i % 2) * P:(i % 2 + 1) * P],
                              ident[:, :])
                last.then_inc(s_sto, 1)
                pe.wait_ge(s_stc, l + 1)
                pe.wait_ge(s_cs, l + 1)
                for t, d, s in ((1, 0, init_st), (2, 1, init_st), (1, 1, next_st), (2, 0, next_st)):
                    if s is next_st:
                        pe.wait_ge(s_snx, l + 1)
                    o = tile_at(t)
                    for g in range(2):
                        r = slice(g * HD, (g + 1) * HD)
                        last = mm(bank[YOFF_BANK[t, g]][:, d * 256:(d + 1) * 256], conv[r, 5, o:o + P],
                                  s[r, d, :], start=True, stop=True)
                    last.then_inc(s_yoff, 1)

                def decay_rows(k):
                    t, g, d = k // 4, k // 2 % 2, k % 2
                    if k >= 2:
                        pe.wait_ge(s_seg, 12 * l + k - 1)
                    for h in range(4):
                        last = mm(bank[1 + k % 2][:, h * P:(h + 1) * P],
                                  da[:, d, t, 4 * g + h:4 * g + h + 1].broadcast_to([P, P]), tri[:, d, :],
                                  start=True, stop=True)
                    last.then_inc(s_cdec, 1)

                pe.wait_ge(s_stoc, l + 1)
                pe.wait_ge(s_snx, l + 1)
                pe.wait_ge(s_gm, l + 1)
                pe.wait_ge(s_xdt, l + 1)
                decay_rows(0)
                decay_rows(1)
                for p in range(6):
                    if p < 5:
                        decay_rows(2 * p + 2)
                        decay_rows(2 * p + 3)
                    t, g = p // 2, p % 2
                    if p == 4:
                        pe.wait_ge(s_gss, NT * l + 1)
                    pe.wait_ge(s_scm, 12 * l + 2 * p + 2)
                    for h in range(4):
                        hh = 4 * g + h
                        for d in range(2):
                            last = mm(bank[6 + t % 2][:, hh * HD:(hh + 1) * HD],
                                      scT[:, (2 * p + d) % 3, h * P:(h + 1) * P],
                                      xdt[:, d, t, hh * HD:(hh + 1) * HD], start=d == 0, stop=d == 1)
                    last.then_inc(s_y, 1)

                pe.wait_ge(s_ssd, NT * (l + 1))
                gate_rows(l, 0)
                pe.wait_ge(s_gbc, 8 * l + 4)
                for kt in range(KT):
                    for t in range(NT):
                        last = tr(bank[kt][:, t * P:(t + 1) * P], mixed[:, t, kt * P:(kt + 1) * P], ident[:, :])
                    last.then_inc(s_mt, 1)
                pe.wait_ge(s_mA, 4 * (l + 1))
                pe.wait_ge(s_mD, 4 * (l + 1))
                for hf in range(2):
                    arrived(u + hf)
                    for t in range(NT):
                        for kt in range(KT):
                            last = mm(bank[3 * hf + t][:, :], tok(kt, t), slot(u + hf)[:, kt, :],
                                      start=kt == 0, stop=kt == KT - 1)
                        last.then_inc(s_o, 1)
                    pe.wait_ge(s_o, 6 * l + 3 * hf + 3)
                    pe.sem_inc(freed[(u + hf) % SLOTS], 1)
                u += OUT_U
                norm_transposes(2 * l + 1)

                for t in range(NT):
                    for kt in range(KT):
                        last = mm(bank[0][:, t * E:(t + 1) * E], tok(kt, t), wr[:, kt, :],
                                  start=kt == 0, stop=kt == KT - 1)
                last.then_inc(s_r, 1)
                gate_rows(l, 1)

                turn = u // SLOTS

                def gate_up(e, s, round):
                    pe.wait_ge(landed[s], 32 * round)
                    for f in range(2):
                        pe.wait_ge(s_hid, 2 * e + (2 * E * l + f + 1))
                        for i, done in enumerate((s_gate_mm, s_up_mm)):
                            for kt in range(KT):
                                c0 = i * F + f * P
                                last = mm(bank[2 * f + i][:, 0:3 * P], slot(s)[:, kt, c0:c0 + P], hT[:, kt, :],
                                          start=kt == 0, stop=kt == KT - 1)
                            last.then_inc(done, 1)
                    pe.wait_ge(s_up_mm, 2 * e + (2 * E * l + 2))
                    pe.sem_inc(freed[s], 1)

                def down(e, b, s, round):
                    if b == 0:
                        pe.wait_ge(landed[s], 32 * round)
                    pe.wait_ge(s_hid, 2 * e + (2 * E * l + 4))
                    w = ring[:, s, b * 2 * DM:(b + 1) * 2 * DM].rearrange("p (f n) -> p f n", f=2)
                    for o in range(6):
                        t, hf = o // 2, o % 2
                        pe.wait_ge(s_acc, 6 * e + (ADD * l + o + 1))
                        for f in range(2):
                            last = mm(bank[4 + (6 * b + o) % 4][:, :], hid[:, b, f, t * P:(t + 1) * P],
                                      w[:, f, hf * 512:(hf + 1) * 512], start=f == 0, stop=f == 1)
                        last.then_inc(s_dn, 1)
                    if b:
                        pe.wait_ge(s_dn, 6 * e + (ADD * l + 6))
                        pe.sem_inc(freed[s], 1)

                pe.wait_ge(s_re, l + 1)
                pe.wait_ge(s_gbc, 8 * l + 8)
                GU, DN = (0, 1, 3, 4), (2, 2, 5, 5)
                gate_up(0, GU[0], turn + 1)
                with pe.Fori(0, E // 4 - 1) as i:
                    for j in range(4):
                        nxt = (j + 1) % 4
                        gate_up(4 * i + j + 1, GU[nxt], i + (turn + 1 + (j == 3)))
                        down(4 * i + j, j % 2, DN[j], i + (turn + 1))
                for j in range(4):
                    i = E // 4 - 1
                    if j < 3:
                        gate_up(4 * i + j + 1, GU[j + 1], i + turn + 1)
                    down(4 * i + j, j % 2, DN[j], i + turn + 1)
                u += MOE_U


def rope_tables():
    tokens, grid_w = 256, 64
    row = (np.arange(tokens) // grid_w).astype(np.float32)
    col = (np.arange(tokens) % grid_w).astype(np.float32)
    n = HD // 4
    inv = np.power(np.float32(10000.0), -np.arange(n, dtype=np.float32) / np.float32(n)).astype(np.float32)
    ang = np.concatenate([row[:, None] * inv, col[:, None] * inv], axis=-1).astype(np.float32)
    return np.cos(ang).astype(np.float32), np.sin(ang).astype(np.float32)


_INS = ['x_prompt', 'x_sample', 'cache_k', 'cache_v', 'state_ssm', 'c', 'c_ctx', 'norm1_w', 'norm2_w',
        'final_norm_w', 'w_ada', 'b_ada', 'w_in', 'conv_w', 'conv_b', 'attn_sink', 'dt_bias', 'a_log',
        'd_skip', 'ssd_norm_w', 'w_out', 'w_router', 'router_bias', 'w_gate', 'w_up', 'w_down']
_OUTS = [(1, 128, 1024), (1, 256, 1024), (1, 2, 128, 2, 64), (1, 2, 128, 2, 64), (1, 2, 2, 8, 64, 64)]


def kernel(**inputs):
    import numpy as _np
    import concourse.bacc as _bacc
    from concourse import mybir as _mybir
    from concourse.bass_utils import run_bass_kernel_spmd as _run

    nc = _bacc.Bacc("TRN2", target_bir_lowering=False, num_devices=1)
    arrays, args = {}, []
    cos, sin = rope_tables()
    for name, a in [(n, inputs[n]) for n in _INS] + [("rope_cos", cos), ("rope_sin", sin)]:
        a = _np.ascontiguousarray(a)
        arrays[f"in_{name}_dram"] = a
        args.append(nc.dram_tensor(f"in_{name}_dram", a.shape, _mybir.dt.from_np(a.dtype), kind="ExternalInput").ap())
    for i, shape in enumerate(_OUTS):
        args.append(nc.dram_tensor(f"out_{i}_dram", shape, _mybir.dt.float32, kind="ExternalOutput").ap())
    hybrid_step(nc, *args)
    r = _run(nc, [arrays], core_ids=[0])
    return tuple(r.results[0][f"out_{i}_dram"] for i in range(len(_OUTS)))
```

```python
import concourse.bass as bass
from concourse import mybir
from contextlib import ExitStack
import numpy as np

P = 128
DM = 1024
KT = DM // P
DEPTH = 2
NT = 3
H = 8
HD = 64
KVH = 2
FREQ = HD // 2
AW = H * HD
IN_W = 2064
XBC0, Z0, DT0 = 768, 1536, 2048
XM = 6
TAPS = 5
PADW = 392
CONVW = PADW - (TAPS - 1)
SEG = (0, 132)
E = 16
F = 256
CAP = 128
MORE = -(-NT * P // CAP) - 1
SMALL = 18
SLOTS = 6
UNIT = KT * 512
ADA_U, IN_U, OUT_U, MOE_U = 12, 4, 2, 24
LAYER_U = ADA_U + IN_U + OUT_U + MOE_U
EPS = 1e-6
NEG = -1e30
SCALE = HD ** -0.5


def hybrid_step(nc, x_prompt, x_sample, cache_k, cache_v, state_ssm, c, c_ctx, norm1_w, norm2_w,
                final_norm_w, w_ada, b_ada, w_in, conv_w, conv_b, attn_sink, dt_bias, a_log, d_skip,
                ssd_norm_w, w_out, w_router, router_bias, w_gate, w_up, w_down, rope_cos, rope_sin,
                y_prompt, y_sample, new_k, new_v, new_state):
    fp32, bf16, i32, u32 = mybir.dt.float32, mybir.dt.bfloat16, mybir.dt.int32, mybir.dt.uint32
    ALU = mybir.AluOpType
    ACT = mybir.ActivationFunctionType
    AX = mybir.AxisListType

    ctx = ExitStack()
    with ctx:
        def sb(name, *shape):
            return ctx.enter_context(nc.sbuf_tensor(name, [P, *shape], fp32))

        def sem(name):
            return ctx.enter_context(nc.semaphore(name))

        ring = sb("ring", SLOTS, UNIT)
        x = sb("x", NT, DM)
        xn = sb("xn", NT, DM)
        mixed = xn
        acc = xn
        hT = sb("hT", KT, NT * P)
        probs = hT[:, :, :]
        qkv = sb("qkv", NT, 768)
        rot = sb("rot", 2, 640)
        pT = rot[:, :, 0:NT * P]
        xpad = sb("xpad", XM * 512)
        xpd = xpad[:, 0:XM * PADW].rearrange("p (m w) -> p m w", m=XM)
        xdt = xpad[:, :].rearrange("p (d t c) -> p d t c", d=2, t=NT)
        gateB = xpad[:, 0:2 * DM].rearrange("p (g c) -> p g c", g=2)
        conv = sb("conv", XM, CONVW)
        scT = conv[:, :, :].rearrange("p m w -> p (m w)")[:, 0:3 * 512].rearrange("p (n c) -> p n c", n=3)
        xs_tok = sb("xs_tok", NT, 512)
        b_tok = sb("b_tok", NT, P)
        ssd = hT[:, :, :].rearrange("p k c -> p (k c)")
        gm = ssd[:, 0:12 * P].rearrange("p (d t g c) -> p d t g c", d=2, t=NT, g=2)
        init_st, next_st, final_st = (ssd[:, 12 * P + i * 512:12 * P + (i + 1) * 512].rearrange("p (d c) -> p d c", d=2)
                             for i in range(3))
        qT = sb("qT", NT, 4, P)
        kT = sb("kT", 4, P)
        work = sb("work", 4, 512)
        xg = [ssd[:, i * DM:(i + 1) * DM] for i in range(3)] + [
            rot[:, :, :].rearrange("p a c -> p (a c)")[:, 0:DM]]
        xgT = work[:, :, :].rearrange("p (b a) c -> p b (a c)", b=2)
        sil, hid, hidT = (xs_tok[:, i, :].rearrange("p (b c) -> p b c", b=2) for i in range(3))
        y_rows = qkv[:, :, :].rearrange("p t c -> p (t c)")[:, 0:2 * DM].rearrange("p (b c) -> p b c", b=2)
        onehot = conv[:, :, :].rearrange("p m w -> p (m w)")[:, 0:4 * NT * P // 2].bitcast(bf16).rearrange(
            "p (b t c) -> p b t c", b=4, t=NT)

        ident = sb("ident", P)
        tri = sb("tri", 2, P)
        one = sb("one", 1)
        slots_f = sb("slots_f", CAP)
        tok_id = ctx.enter_context(nc.sbuf_tensor("tok_id", [P, NT, 2], bf16))
        e_row = sb("e_row", E)
        idx = ctx.enter_context(nc.sbuf_tensor("idx", [P, E], u32))
        y_idx = ctx.enter_context(nc.sbuf_tensor("y_idx", [P, 2, NT], u32))
        rounds = ctx.enter_context(nc.sbuf_tensor("rounds", [P, DEPTH], i32))
        gw = sb("gw", 2, NT)
        wt = sb("wt", 2, NT)
        amask = sb("amask", 5, P)
        rope = sb("rope", 2, 2, FREQ)
        prm_rows = work[:, 0, 0:P]
        bada_rows = work[:, 0, P:2 * P]
        prm = sb("prm", P)
        bada = sb("bada", 96)
        cT = sb("cT", KT, 2)
        ada_row = work[:, 2:4, :]
        modT = sb("modT", DEPTH, 48, 2)
        amod = sb("amod", 2 * DEPTH, KT, 2)
        wr = sb("wr", KT, E)
        wdt = sb("wdt", DEPTH, KT, 2 * H)
        vec = sb("vec", DEPTH, 16 + 16 + 8 + 8)
        rb = sb("rb", E)
        snw = qT[:, 2, :, :].rearrange("p a c -> p (a c)")
        ckv = sb("ckv", 2, DEPTH, P)
        st_in = sb("st_in", 2, 2, 2, HD)
        diag = qT[:, 0, :, :]
        st_out = diag[:, :, :].rearrange("p a c -> p (a c)")
        epst = sb("epst", 4)
        ss = sb("ss", 5, NT)
        rstd = sb("rstd", 5, NT)
        mx = sb("mx", NT, H)
        nm = sb("nm", NT, H)
        es = sb("es", NT, H)
        rs = sb("rs", NT, H)
        den = sb("den", NT, H)
        dtr = sb("dtr", 2, NT, H)
        dtu = sb("dtu", 2, NT, H)
        dtv = sb("dtv", 2, NT, H)
        dtw = sb("dtw", 2, NT, H)
        dt = sb("dt", 2, NT, H)
        da = sb("da", 2, NT, H)
        cs = sb("cs", 2, NT, H)
        tot = sb("tot", 2, NT, H)
        ecs = sb("ecs", 2, NT, H)
        etot = sb("etot", 2, NT, H)
        wend = sb("wend", 2, NT, H)
        gss = sb("gss", NT, 2)
        grs = sb("grs", NT, 2)
        rt = qT[:, 1, :, :].rearrange("p a c -> p (a c)")[:, 0:8 * NT * E].rearrange(
            "p (n t e) -> p n t e", n=8, t=NT)
        tie = sb("tie", E)
        h_rows = nc.dram_tensor("h_rows", [NT * P, DM], fp32)
        y_exp = nc.dram_tensor("y_exp", [E * CAP, DM], fp32)

        bank = [ctx.enter_context(nc.psum_tensor(f"bank{i}", [P, 512], fp32)) for i in range(8)]

        landed = [sem(f"landed{i}") for i in range(SLOTS)]
        s_rows, s_x, s_small, s_state = sem("rows_landed"), sem("x_landed"), sem("small_landed"), sem("state_landed")
        s_snw, s_fnw = sem("snw_landed"), sem("fnw_landed")
        s_const = sem("consts_made")
        s_pool, s_dve, s_act = sem("pool_step"), sem("dve_step"), sem("act_step")
        s_zero, s_ctxs, s_bada = sem("borders_zeroed"), sem("ctx_state_copied"), sem("bada_copied")
        s_prmT, s_prm, s_cT, s_a = sem("prm_transposed"), sem("prm_copied"), sem("c_silu"), sem("a_made")
        s_ada, s_row, s_rowT, s_mod = sem("ada_mm"), sem("ada_row_copied"), sem("ada_transposed"), sem("mod_made")
        s_ss, s_rstd, s_xn, s_tr, s_hA, s_hD = (sem(n) for n in (
            "sumsq_made", "rstd_made", "xn_made", "xn_transposed", "hT_by_act", "hT_by_dve"))
        s_amod = sem("amod_made")
        s_q, s_kv, s_xbc, s_z = sem("q_mm"), sem("kv_mm"), sem("xbc_mm"), sem("z_mm")
        s_qc, s_kvc, s_xbcc, s_zc, s_dtr = (sem(n) for n in (
            "q_copied", "kv_copied", "xbc_copied", "z_silu", "dt_raw"))
        s_rope, s_qtr, s_qTc, s_conv, s_silu = (sem(n) for n in (
            "rope_done", "q_transposed", "qT_copied", "conv_done", "xbc_silu"))
        s_sc, s_scc, s_nm, s_exp, s_es, s_ptr, s_pTc, s_pv, s_attn = (sem(n) for n in (
            "scores_mm", "scores_masked", "max_made", "exp_done", "sink_exp", "probs_transposed",
            "pT_copied", "pv_mm", "attn_done"))
        s_dt1, s_dt2, s_da, s_cum, s_cs, s_ecs = (sem(n) for n in (
            "dt_abs", "dt_ln", "da_made", "cumsum_mm", "cs_copied", "decays_made"))
        s_xtr, s_xtc, s_g, s_gm = sem("xs_transposed"), sem("xs_copied"), sem("g_mm"), sem("g_masked")
        s_xdt, s_xw, s_st, s_stc, s_snx = (sem(n) for n in (
            "xdt_made", "xw_made", "state_mm", "state_copied", "state_next"))
        s_sto, s_stoc, s_yoff, s_cdec, s_seg, s_dexp, s_scm, s_y = (sem(n) for n in (
            "state_out_transposed", "state_out_copied", "yoff_mm", "decay_rows", "seg_made", "decay_exp",
            "decay_scores", "y_mm"))
        s_yv, s_yt, s_yp, s_gss, s_grs, s_ssd = (sem(n) for n in (
            "y_skip_made", "yoff_scaled", "y_summed", "gated_sumsq", "gated_rstd", "ssd_done"))
        s_dg, s_gb, s_gbc = sem("diag_made"), sem("gate_mm"), sem("gate_copied")
        s_mt, s_mA, s_mD, s_o, s_oc, s_x1 = (sem(n) for n in (
            "mixed_transposed", "mixT_by_act", "mixT_by_dve", "out_mm", "out_gated", "x_updated"))
        s_r, s_re, s_gate = sem("router_mm"), sem("router_exp"), sem("gates_made")
        s_fin, s_x2 = sem("moe_gated"), sem("moe_added")
        s_iota, s_sel, s_pos, s_posm, s_oh, s_idm, s_idx, s_yidx = (sem(n) for n in (
            "iotas_made", "experts_chosen", "positions_mm", "positions_made", "onehot_made", "ids_mm",
            "slot_tokens_made", "result_rows_made"))
        s_bt, s_btc, s_h = sem("h_transposed_back"), sem("h_rows_copied"), sem("h_rows_stored")
        gathered = [sem(f"gathered{i}") for i in range(4)]
        s_tx, s_xgc, s_gu, s_sil, s_hid, s_th, s_htc, s_dn, s_yc = (sem(n) for n in (
            "xg_transposed", "xgT_copied", "gate_up_mm", "silu_done", "hid_made", "hid_transposed",
            "hidT_copied", "down_mm", "y_copied"))
        y_stored = [sem(f"y_stored{i}") for i in range(2)]
        combined = [sem(f"results_gathered{i}") for i in range(NT)]
        RESULT_STEPS = 11
        s_rounds, o_pass, o_step, o_rows, o_add, o_c, o_pos, o_sel, o_c0 = (sem(n) for n in (
            "rounds_counted", "over_passed", "over_step", "over_rows", "over_added", "over_results", "over_positions", "over_column", "over_ids_copied"))
        o_oh, o_idm, o_idx, o_w, o_g, o_tx, o_xgc, o_gu, o_sil, o_hid, o_th, o_htc, o_dn, o_yc, o_yst = (
            sem("over_" + n) for n in ("onehot", "ids_mm", "idx", "weights", "gathered", "xg_transposed",
                                       "xgT_copied", "gate_up_mm", "silu", "hid", "hid_transposed",
                                       "hidT_copied", "down_mm", "y_copied", "y_stored"))
        s_y_out, s_yst, s_out = sem("final_made"), sem("y_stored"), sem("stored")

        def slot(u):
            return ring[:, u % SLOTS, :].rearrange("p (k n) -> p k n", k=KT)

        def bc(v, w):
            return v.unsqueeze(2).broadcast_to([v.shape[0], v.shape[1], w])

        def rep(v, n):
            return v.unsqueeze(1).broadcast_to([v.shape[0], n, v.shape[1]])

        def heads(v, n=H):
            return v.rearrange("p (h c) -> p h c", h=n)

        def tile_at(t):
            return (0, 132, 260)[t]

        def grp(t):
            return min(t, 1)

        STATES = ((0, 0), (1, 0), (0, 1), (1, 2))
        YOFF_BANK = {(1, 0): 3, (1, 1): 4, (2, 0): 5, (2, 1): 0}
        STORES = 2 + 4
        onesP = one[:, 0:1].broadcast_to([P, P])
        done_rounds = {}

        def overflow(eng, l, step, start=None, stop=None, end=None):
            eng.wait_ge(s_rounds, l + 1)
            more = eng.value_load(rounds[0:1, l:l + 1], min_val=0, max_val=MORE)
            before = done_rounds.get((id(eng), l - 1), 0)
            with eng.If(more > 0):
                with eng.Fori(0, more) as r:
                    if start:
                        start(before + r)
                    with eng.Fori(0, E) as e:
                        step(e, before * E + r * E + e)
                    if stop:
                        stop(before + r)
                if end:
                    end(before * E + more * E)
            done_rounds[id(eng), l] = before + more

        block = ctx.enter_context(nc.Block())

        @block.sync
        def _(sp):
            def used(u):
                l, j = divmod(u, LAYER_U)
                if j < ADA_U:
                    return s_ada, ADA_U * l + j + 1
                j -= ADA_U
                if j < IN_U:
                    return ((s_q, NT * (l + 1)), (s_xbc, XM * l + 2), (s_xbc, XM * (l + 1)), (s_z, NT * (l + 1)))[j]
                j -= IN_U
                if j < OUT_U:
                    return s_o, 6 * l + 3 * j + 3
                j -= OUT_U
                pair, k = divmod(j, 3)
                return (s_gu, E * l + 2 * pair + k + 1) if k < 2 else (s_dn, E * l + 2 * pair + 2)

            def load(s, parts):
                for dst, src in parts:
                    sp.dma_start(dst, src).then_inc(landed[s], 16)

            def columns(u, w):
                v = w.rearrange("(k p) n -> p k n", p=P)
                if u >= SLOTS:
                    sp.wait_ge(*used(u - SLOTS))
                load(u % SLOTS, [(slot(u)[:, 4 * i:4 * i + 4, :], v[:, 4 * i:4 * i + 4, :]) for i in range(2)])

            def expert_unit(l, e, j, s):
                if j < 2:
                    load(s, [(slot(s)[:, :, i * F:(i + 1) * F],
                              w[l, e + j].rearrange("(k p) f -> p k f", p=P))
                             for i, w in enumerate((w_gate, w_up))])
                else:
                    load(s, [(ring[:, s, i * 2 * DM:(i + 1) * 2 * DM].rearrange("p (f n) -> p f n", f=2),
                              w_down[l, e + i].rearrange("(f p) n -> p f n", p=P)) for i in range(2)])

            u = 0
            for l in range(DEPTH):
                for units, w in ((ADA_U, w_ada), (IN_U, w_in), (OUT_U, w_out)):
                    for j in range(units):
                        columns(u, w[l, :, j * 512:(j + 1) * 512])
                        u += 1
                for s in range(SLOTS):
                    sp.wait_ge(*used(u + s - SLOTS))
                    expert_unit(l, 2 * (s // 3), s % 3, s)
                with sp.Fori(1, E // 4) as i:
                    for s in range(SLOTS):
                        pair, k = divmod(s, 3)
                        if k < 2:
                            sp.wait_ge(s_gu, 4 * i + (E * l + 2 * pair + k + 1 - 4))
                        else:
                            sp.wait_ge(s_dn, 4 * i + (E * l + 2 * pair + 2 - 4))
                        expert_unit(l, 4 * i + 2 * pair, k, s)
                u += MOE_U
                sp.wait_ge(s_dn, E * (l + 1))

                def again(e, q):
                    sp.wait_ge(o_dn, q + 1)
                    for i, w in enumerate((w_gate, w_up)):
                        sp.dma_start(slot(0)[:, :, i * F:(i + 1) * F],
                                     w[l, e].rearrange("(k p) f -> p k f", p=P)).then_inc(o_w, 16)
                    sp.dma_start(ring[:, 2, 0:2 * DM].rearrange("p (f n) -> p f n", f=2),
                                 w_down[l, e].rearrange("(f p) n -> p f n", p=P)).then_inc(o_w, 16)

                def all_used(steps):
                    sp.wait_ge(o_dn, steps + 1)
                    sp.sem_inc(o_pass, 1)

                overflow(sp, l, again, end=all_used)
            for t in range(NT):
                sp.wait_ge(s_y_out, t + 1)
                dst = y_prompt[0] if t == 0 else y_sample[0, (t - 1) * P:t * P, :]
                sp.dma_start(dst, xn[:, t, :]).then_inc(s_yst, 16)
            sp.wait_ge(s_yst, 16 * NT)
            sp.wait_ge(s_out, 16 * STORES * DEPTH)

        @block.gpsimd
        def _(pool):
            n = [0]

            def step(ins):
                n[0] += 1
                ins.then_inc(s_pool, 1)
                pool.wait_ge(s_pool, n[0])

            pool.sem_inc(o_c, 16)
            pool.memset(ident[:, :], 0.0)
            pool.memset(tri[:, :, :], 1.0)
            pool.memset(amask[:, :, :], 0.0)
            pool.memset(epst[:, 0:NT], -0.5)
            step(pool.memset(one[:, :], 1.0))
            iota = work[:, 3, :].bitcast(i32)
            pool.iota(iota[:, 0:CAP], pattern=[[1, CAP]], base=0, channel_multiplier=0)
            pool.iota(iota[:, CAP:CAP + 3], pattern=[[0, 3]], base=0, channel_multiplier=1)
            pool.iota(iota[:, CAP + 3:CAP + 6], pattern=[[P, 3]], base=0, channel_multiplier=0)
            pool.iota(iota[:, CAP + 6:CAP + 6 + E], pattern=[[CAP, E]], base=0, channel_multiplier=0)
            pool.iota(iota[:, 160:160 + E], pattern=[[-1, E]], base=E, channel_multiplier=0).then_inc(s_iota, 1)
            pool.affine_select(out=ident[:, :], in_=ident[:, :], compare_op=ALU.not_equal, fill=1.0, base=0,
                               pattern=[[-1, P]], channel_multiplier=1)
            pool.affine_select(out=tri[:, 0, :], in_=tri[:, 0, :], compare_op=ALU.is_ge, fill=0.0, base=0,
                               pattern=[[1, P]], channel_multiplier=-1)
            pool.affine_select(out=tri[:, 1, :], in_=tri[:, 1, :], compare_op=ALU.is_ge, fill=0.0, base=0,
                               pattern=[[-1, P]], channel_multiplier=1)
            pool.affine_select(out=amask[:, 1, :], in_=amask[:, 1, :], compare_op=ALU.is_ge, fill=NEG, base=0,
                               pattern=[[1, P]], channel_multiplier=-1)
            pool.affine_select(out=amask[:, 4, :], in_=amask[:, 4, :], compare_op=ALU.is_ge, fill=NEG, base=0,
                               pattern=[[-1, P]], channel_multiplier=1).then_inc(s_const, 1)

            def norm_rstd(k):
                pool.wait_ge(s_ss, NT * (k + 1))
                step(pool.tensor_scalar(ss[:, k, :], ss[:, k, :], 1.0 / DM, EPS, ALU.mult, ALU.add))
                pool.tensor_tensor(rstd[:, k, :], ss[:, k, :], epst[:, 0:NT], ALU.pow).then_inc(s_rstd, 1)

            for l in range(DEPTH):
                if l:
                    pool.wait_ge(s_stc, l)
                for d in range(2):
                    for jj in range(2):
                        pool.dma_start(st_in[:, d, jj, :, :],
                                       state_ssm[0, l, d].rearrange("(g j hh) p n -> j (hh p) g n", g=2, j=2)[jj]
                                       ).then_inc(s_state, 16)
                norm_rstd(2 * l)
                if l:
                    pool.wait_ge(s_fin, NT * l)
                for b, w in ((0, 2), (130, 4), (390, 2)):
                    last = pool.memset(xpd[:, :, b:b + w], 0.0)
                last.then_inc(s_zero, 1)
                if l == 0:
                    pool.wait_ge(s_small, 16 * SMALL)
                for t in (1, 2):
                    pool.wait_ge(s_qc, NT * l + t + 1)
                    pool.wait_ge(s_kvc, NT * l + t + 1)
                    v = qkv[:, t, 0:640].rearrange("p (h d) -> p h d", d=HD)
                    o = rot[:, t - 1, :].rearrange("p (h d) -> p h d", d=HD)
                    x1, x2 = v[:, :, 0:FREQ], v[:, :, FREQ:HD]
                    co, si = (rep(rope[:, i, t - 1, :], 10) for i in range(2))
                    x2s, x2c = (work[:, 2 * (t - 1) + i, 0:320].rearrange("p (h d) -> p h d", d=FREQ)
                                for i in range(2))
                    pool.tensor_tensor(o[:, :, 0:FREQ], x1, co, ALU.mult)
                    pool.tensor_tensor(o[:, :, FREQ:HD], x1, si, ALU.mult)
                    pool.tensor_tensor(x2s, x2, si, ALU.mult)
                    step(pool.tensor_tensor(x2c, x2, co, ALU.mult))
                    pool.tensor_tensor(o[:, :, 0:FREQ], o[:, :, 0:FREQ], x2s, ALU.subtract)
                    pool.tensor_tensor(o[:, :, FREQ:HD], o[:, :, FREQ:HD], x2c, ALU.add).then_inc(s_rope, 1)
                pool.wait_ge(s_da, l + 1)
                for t in range(NT):
                    pool.wait_ge(s_xtc, 4 * l + t + 1)
                    for d in range(2):
                        last = pool.tensor_tensor(heads(xdt[:, d, t, :]), heads(xs_tok[:, t, :]),
                                                  bc(dt[:, d, t, :], HD), ALU.mult)
                last.then_inc(s_xdt, 1)
                pool.wait_ge(s_xdt, l + 1)
                pool.wait_ge(s_ecs, l + 1)
                for k, (d, t) in enumerate(STATES):
                    pool.tensor_tensor(heads(work[:, k, :]), heads(xdt[:, d, t, :]),
                                       bc(wend[:, d, t, :], HD), ALU.mult).then_inc(s_xw, 1)
                for t in range(NT):
                    pool.wait_ge(s_gss, NT * l + t + 1)
                    step(pool.tensor_scalar(gss[:, t, :], gss[:, t, :], 1.0 / 256, EPS, ALU.mult, ALU.add))
                    pool.tensor_tensor(grs[:, t, :], gss[:, t, :], epst[:, 0:2], ALU.pow).then_inc(s_grs, 1)
                for k in range(6):
                    pool.wait_ge(s_oc, 6 * l + k + 1)
                    hf, t = k // 3, k % 3
                    xx = x[:, t, hf * 512:(hf + 1) * 512]
                    pool.tensor_tensor(xx, xx, work[:, k % 4, :], ALU.add).then_inc(s_x1, 1)
                norm_rstd(2 * l + 1)
                pool.wait_ge(s_h, 16 * NT * (l + 1))
                for e in range(E):
                    pool.wait_ge(s_idx, 2 * l + (1 if e < 4 else 2))
                    if E * l + e >= 4:
                        pool.wait_ge(s_tx, E * l + e - 3)
                    pool.indirect_dma_start(
                        out=xg[e % 4], out_offset=None, in_=h_rows[:, :],
                        in_offset=bass.IndirectOffsetOnAxis(ap=idx[:, e:e + 1], axis=0)
                    ).then_inc(gathered[e % 4], 16)
                pool.wait_ge(s_tx, E * (l + 1))

                def gather_again(e, q):
                    pool.wait_ge(o_idx, q + 1)
                    pool.sem_inc(o_pass, 1)
                    pool.indirect_dma_start(
                        out=xg[0], out_offset=None, in_=h_rows[:, :],
                        in_offset=bass.IndirectOffsetOnAxis(ap=idx[:, 0:1], axis=0)).then_inc(o_g, 16)

                for b in range(2):
                    pool.wait_ge(y_stored[b], 16 * (E // 2) * (l + 1) + 16)
                pool.wait_ge(s_yidx, l + 1)

                def result(dst, i, t):
                    return pool.indirect_dma_start(
                        out=dst, out_offset=None, in_=y_exp[:, :],
                        in_offset=bass.IndirectOffsetOnAxis(ap=y_idx[:, i, t:t + 1], axis=0))

                for t in range(NT):
                    result(xg[t], 0, t).then_inc(combined[t], 16)
                    result(acc[:, t, :], 1, t).then_inc(combined[t], 16)

                def gather_results(k):
                    pool.wait_ge(o_yst, 16 * E * k + 16 * E)
                    pool.wait_ge(o_rows, k + 1)
                    for j in range(2 * NT):
                        if j:
                            pool.wait_ge(o_add, 2 * NT * k + j)
                        pool.sem_inc(o_pass, 1)
                        result(xg[0], j % 2, j // 2).then_inc(o_c, 16)

                overflow(pool, l, gather_again, stop=gather_results)
                for t in range(NT):
                    pool.wait_ge(s_fin, NT * l + t + 1)
                    pool.tensor_tensor(x[:, t, :], x[:, t, :], acc[:, t, :], ALU.add).then_inc(s_x2, 1)
            norm_rstd(2 * DEPTH)

        @block.scalar
        def _(act):
            dma = act.dma_start
            act.sem_inc(s_yc, 2)
            for b in range(2):
                act.sem_inc(y_stored[b], 16)
            rows = lambda w: w.rearrange("l (k p) -> (l k) p", p=P)
            for dst, src in (
                    (prm_rows[0:16, :], rows(norm1_w)),
                    (prm_rows[16:32, :], rows(norm2_w)),
                    (prm_rows[32:40, :], c_ctx.rearrange("(k p) -> k p", p=P)),
                    (prm_rows[40:48, :], rows(c)),
                    (prm_rows[48:108, :], conv_w.rearrange("l t (m p) -> (l t m) p", p=P)),
                    (prm_rows[108:120, :], rows(conv_b)),
                    (bada_rows[0:96, :], rows(b_ada))):
                dma(dst, src).then_inc(s_rows, 16)
            dma(x[:, 0, :], x_prompt[0]).then_inc(s_x, 16)
            dma(x[:, 1:3, :], x_sample[0].rearrange("(t p) d -> p t d", p=P)).then_inc(s_x, 16)
            small = [(wr[:, :, :], w_router.rearrange("(k p) n -> p k n", p=P)),
                     (rb[:, :], router_bias.partition_broadcast(P)),
                     (rope[:, 0, :, :], rope_cos.rearrange("(t p) f -> p t f", p=P)),
                     (rope[:, 1, :, :], rope_sin.rearrange("(t p) f -> p t f", p=P))]
            for l in range(DEPTH):
                small += [(wdt[:, l, :, :], w_in[l, :, DT0:IN_W].rearrange("(k p) n -> p k n", p=P)),
                          (vec[:, l, 0:16], dt_bias[l].rearrange("d h -> (d h)").partition_broadcast(P)),
                          (vec[:, l, 16:32], a_log[l].rearrange("d h -> (d h)").partition_broadcast(P)),
                          (vec[:, l, 32:40], d_skip[l].partition_broadcast(P)),
                          (vec[:, l, 40:48], attn_sink[l].partition_broadcast(P)),
                          (ckv[:, 0, l, :], cache_k[0, l].rearrange("s k d -> s (k d)")),
                          (ckv[:, 1, l, :], cache_v[0, l].rearrange("s k d -> s (k d)"))]
            assert len(small) == SMALL
            for dst, src in small:
                dma(dst, src).then_inc(s_small, 16)

            act.wait_ge(s_prmT, 1)
            act.activation(prm[:, 0:120], bank[0][:, 0:120], ACT.Copy).then_inc(s_prm, 1)
            act.wait_ge(s_prm, 1)
            act.activation(cT[:, :, :].rearrange("p k g -> p g k"),
                           prm[:, 32:48].rearrange("p (g k) -> p g k", g=2), ACT.Silu).then_inc(s_cT, 1)
            act.wait_ge(s_small, 16 * SMALL)
            act.activation(vec[:, :, 16:32], vec[:, :, 16:32], ACT.Exp).then_inc(s_a, 1)

            def ada(l):
                for k in range(ADA_U * l, ADA_U * (l + 1)):
                    act.wait_ge(s_ada, k + 1)
                    if k >= 2:
                        act.wait_ge(s_rowT, k - 1)
                    act.activation(ada_row[0:2, k % 2, :], bank[6 + k % 2][0:2, :], ACT.Copy).then_inc(s_row, 1)

            def sumsq(k):
                l = (k - 1) // 2
                if k == 0:
                    act.wait_ge(s_x, 32)
                for t in range(NT):
                    if k % 2:
                        act.wait_ge(s_x1, 6 * l + 4 + t)
                        act.wait_ge(s_mt, KT * (l + 1))
                    elif k:
                        act.wait_ge(s_x2, NT * (k // 2 - 1) + t + 1)
                        if t == 0:
                            act.wait_ge(s_x2, NT * (k // 2))
                    act.activation(xn[:, t, :], x[:, t, :], ACT.Square,
                                   accum_out=ss[:, k, t:t + 1]).then_inc(s_ss, 1)

            def modulated(k):
                l, w = k // 2, k % 2
                act.wait_ge(s_amod, k + 1)
                for kt in range(0, KT, 2):
                    act.wait_ge(s_tr, KT * k + kt + 1)
                    for g, (a, b) in enumerate(((0, P), (P, 3 * P))):
                        last = act.activation(hT[:, kt, a:b], bank[kt][:, a:b], ACT.Identity,
                                              bias=modT[:, l, 24 * w + kt, g:g + 1],
                                              scale=amod[:, k, kt, g:g + 1])
                    last.then_inc(s_hA, 1)

            def gate_copies(l, w):
                for k in range(4):
                    act.wait_ge(s_gb, 8 * l + 4 * w + k + 1)
                    if w and k == 0:
                        act.wait_ge(s_oc, 6 * (l + 1))
                    act.activation(gateB[:, k // 2, (k % 2) * 512:(k % 2 + 1) * 512], bank[6 + k % 2][:, :],
                                   ACT.Copy).then_inc(s_gbc, 1)

            for l in range(DEPTH):
                ada(l)
                sumsq(2 * l)
                modulated(2 * l)
                for t in range(NT):
                    act.wait_ge(s_q, NT * l + t + 1)
                    act.activation(qkv[:, t, 0:AW].rearrange("p (j a d) -> p a j d", a=2, d=HD),
                                   bank[t][:, :].rearrange("p (a j d) -> p a j d", a=2, d=HD),
                                   ACT.Copy).then_inc(s_qc, 1)
                act.wait_ge(s_zero, l + 1)
                for m in range(XM):
                    act.wait_ge(s_xbc, XM * l + m + 1)
                    b = bank[(6 + m) % 8]
                    act.activation(xpd[:, m, 2:2 + P], b[:, 0:P], ACT.Copy)
                    act.activation(xpd[:, m, 134:390], b[:, P:3 * P], ACT.Copy).then_inc(s_xbcc, 1)
                for t in range(NT):
                    act.wait_ge(s_z, NT * l + t + 1)
                    act.activation(mixed[:, t, 512:1024], bank[4 + t][:, :], ACT.Silu).then_inc(s_zc, 1)
                act.wait_ge(s_kvc, NT * l + 1)
                dma(new_k[0, l].rearrange("s k d -> s (k d)"), qkv[:, 0, 512:640]).then_inc(s_out, 16)
                dma(new_v[0, l].rearrange("s k d -> s (k d)"), qkv[:, 0, 640:768]).then_inc(s_out, 16)
                for m in range(XM):
                    act.wait_ge(s_conv, XM * l + m + 1)
                    act.activation(conv[:, m, :], conv[:, m, :], ACT.Silu).then_inc(s_silu, 1)
                for i in range(4):
                    act.wait_ge(s_qtr, 4 * l + i + 1)
                    dst = qT[:, i, :, :] if i < 3 else kT[:, :, :]
                    act.activation(dst.rearrange("p a b -> p (a b)"), bank[(7, 0, 1, 2)[i]][:, :],
                                   ACT.Copy).then_inc(s_qTc, 1)
                act.wait_ge(s_dt1, 2 * l + 1)
                act.activation(dtu[:, :, :, :], dtu[:, :, :, :], ACT.Exp, scale=-1.0).then_inc(s_dt2, 1)
                act.wait_ge(s_dt1, 2 * l + 2)
                act.activation(dtw[:, :, :, :], dtv[:, :, :, :], ACT.Ln).then_inc(s_dt2, 1)
                for t in range(NT):
                    nk = P if t == 0 else 3 * P
                    act.wait_ge(s_nm, NT * l + t + 1)
                    for h in range(H):
                        act.activation(probs[:, h, 0:nk], probs[:, h, 0:nk], ACT.Exp, scale=SCALE,
                                       bias=nm[:, t, h:h + 1], accum_out=rs[:, t, h:h + 1]).then_inc(s_exp, 1)
                    act.activation(es[:, t, :], es[:, t, :], ACT.Exp).then_inc(s_es, 1)
                act.wait_ge(s_attn, NT * (l + 1))
                dma(snw, ssd_norm_w[l].partition_broadcast(P)).then_inc(s_snw, 16)
                for i in range(4):
                    act.wait_ge(s_xtr, 5 * l + i + 1)
                    dst = xs_tok[:, i, :] if i < NT else b_tok[:, :, :].rearrange("p t c -> p (t c)")
                    act.activation(dst, bank[i][:, 0:512 if i < NT else NT * P], ACT.Copy).then_inc(s_xtc, 1)
                act.wait_ge(s_xtr, 5 * l + 5)
                act.activation(init_st[:, :, :].rearrange("p d c -> p (d c)"), bank[4][:, :],
                               ACT.Copy).then_inc(s_stc, 1)
                act.wait_ge(s_cs, l + 1)
                act.activation(ecs[:, :, :, :], cs[:, :, :, :], ACT.Exp)
                act.activation(etot[:, :, :, :], tot[:, :, :, :], ACT.Exp)
                act.activation(wend[:, :, :, :], wend[:, :, :, :], ACT.Exp).then_inc(s_ecs, 1)
                act.wait_ge(s_sto, l + 1)
                act.activation(st_out, bank[2][:, :], ACT.Copy).then_inc(s_stoc, 1)
                act.wait_ge(s_stoc, l + 1)
                for d in range(2):
                    for jj in range(2):
                        dma(new_state[0, l, d].rearrange("(g j hh) p n -> j (hh p) g n", g=2, j=2)[jj],
                            st_out.rearrange("p (d j g n) -> p d j g n", d=2, j=2, g=2)[:, d, jj]
                            ).then_inc(s_out, 16)
                for k in range(12):
                    act.wait_ge(s_seg, 12 * l + k + 1)
                    act.activation(work[:, k % 2, :], work[:, k % 2, :], ACT.Exp).then_inc(s_dexp, 1)
                gate_copies(l, 0)
                for kt in range(0, KT, 2):
                    act.wait_ge(s_mt, KT * l + kt + 1)
                    act.activation(hT[:, kt, :], bank[kt][:, 0:3 * P], ACT.Copy).then_inc(s_mA, 1)
                sumsq(2 * l + 1)
                modulated(2 * l + 1)
                act.wait_ge(s_r, l + 1)
                act.activation(rt[:, 0, :, :].rearrange("p t e -> p (t e)"), bank[0][:, 0:NT * E], ACT.Exp,
                               scale=-1.0).then_inc(s_re, 1)
                for t in range(NT):
                    for hf in range(2):
                        act.wait_ge(s_bt, 6 * l + 2 * t + hf + 1)
                        act.activation(xn[:, t, hf * 512:(hf + 1) * 512], bank[1 + 2 * t + hf][:, :],
                                       ACT.Copy).then_inc(s_btc, 1)
                    act.wait_ge(s_btc, 6 * l + 2 * t + 2)
                    dma(h_rows[t * P:(t + 1) * P, :], xn[:, t, :]).then_inc(s_h, 16)
                gate_copies(l, 1)
                def silu(e, b):
                    act.wait_ge(s_gu, e + (E * l + 1))
                    act.activation(sil[:, b, :], bank[b][:, 0:F], ACT.Silu).then_inc(s_sil, 1)

                def store(e, b, turn):
                    act.wait_ge(s_dn, e + (E * l + 1))
                    act.wait_ge(y_stored[b], 16 * turn + (16 * (E // 2) * l + 16))
                    for hf in range(2):
                        act.activation(y_rows[:, b, hf * 512:(hf + 1) * 512], bank[5 + hf][:, :],
                                       ACT.Copy).then_inc(s_yc, 1)
                    act.wait_ge(s_yc, 2 * e + (2 * E * l + 4))
                    dma(y_exp[bass.ds(e * CAP, CAP), :], y_rows[:, b, :]).then_inc(y_stored[b], 16)

                silu(0, 0)
                with act.Fori(0, E // 2 - 1) as i:
                    silu(2 * i + 1, 1)
                    store(2 * i, 0, i)
                    silu(2 * i + 2, 0)
                    store(2 * i + 1, 1, i)
                silu(E - 1, 1)
                store(E - 2, 0, E // 2 - 1)
                store(E - 1, 1, E // 2 - 1)

                def results_read(k):
                    for t in range(NT):
                        act.wait_ge(combined[t], 32 * (l + 1))
                    act.wait_ge(o_c, 16 * 2 * NT * k + 16)
                    act.sem_inc(o_pass, 1)

                def again(e, q):
                    act.wait_ge(o_gu, q + 1)
                    act.activation(sil[:, 0, :], bank[0][:, 0:F], ACT.Silu).then_inc(o_sil, 1)
                    act.wait_ge(o_dn, q + 2)
                    for hf in range(2):
                        act.activation(y_rows[:, 0, hf * 512:(hf + 1) * 512], bank[5 + hf][:, :],
                                       ACT.Copy).then_inc(o_yc, 1)
                    act.wait_ge(o_yc, 2 * q + 2)
                    dma(y_exp[bass.ds(e * CAP, CAP), :], y_rows[:, 0, :]).then_inc(o_yst, 16)
                    act.wait_ge(o_yst, 16 * q + 16)

                overflow(act, l, again, start=results_read)
            act.wait_ge(s_fin, NT * DEPTH)
            dma(gateB[:, 0, :], final_norm_w.partition_broadcast(P)).then_inc(s_fnw, 16)
            sumsq(2 * DEPTH)

        @block.vector
        def _(dve):
            n = [0]

            def step(ins):
                n[0] += 1
                ins.then_inc(s_dve, 1)
                dve.wait_ge(s_dve, n[0])

            dve.wait_ge(s_iota, 1)
            iota = work[:, 3, :].bitcast(i32)
            dve.tensor_copy(slots_f[:, :], iota[:, 0:CAP])
            dve.tensor_copy(tok_id[:, :, 0], iota[:, CAP:CAP + 3])
            dve.tensor_copy(tok_id[:, :, 1], iota[:, CAP + 3:CAP + 6])
            dve.tensor_copy(e_row[:, :], iota[:, CAP + 6:CAP + 6 + E])
            dve.tensor_copy(tie[:, :], iota[:, 160:160 + E]).then_inc(s_iota, 1)
            dve.wait_ge(s_prmT, 2)
            dve.tensor_copy(bada[:, :], bank[1][:, 0:96]).then_inc(s_bada, 1)
            dve.wait_ge(s_bada, 1)
            dve.wait_ge(s_a, 1)
            step(dve.tensor_scalar(vec[:, :, 16:32], vec[:, :, 16:32], -1.0, None, ALU.mult))

            def ada(l):
                for j in range(ADA_U):
                    k = ADA_U * l + j
                    dve.wait_ge(s_rowT, k + 1)
                    dve.tensor_tensor(modT[:, l, 4 * j:4 * j + 4, :],
                                      bank[4 + k % 2][:, 0:8].rearrange("p (j g) -> p j g", g=2),
                                      bc(bada[:, 48 * l + 4 * j:48 * l + 4 * j + 4], 2), ALU.add
                                      ).then_inc(s_mod, 1)
                dve.wait_ge(s_mod, ADA_U * (l + 1))
                if l == 0:
                    dve.wait_ge(s_prm, 1)
                for w in range(2):
                    dve.scalar_tensor_tensor(
                        out=amod[:, 2 * l + w, :, :], in0=modT[:, l, 24 * w + 8:24 * w + 16, :], scalar=1.0,
                        in1=bc(prm[:, 16 * w + 8 * l:16 * w + 8 * l + 8], 2), op0=ALU.add, op1=ALU.mult
                    ).then_inc(s_amod, 1)

            def normed(k):
                dve.wait_ge(s_rstd, k + 1)
                for t in range(NT):
                    dve.tensor_scalar(xn[:, t, :], x[:, t, :], rstd[:, k, t:t + 1], None,
                                      ALU.mult).then_inc(s_xn, 1)

            def modulated(k):
                l, w = k // 2, k % 2
                dve.wait_ge(s_amod, k + 1)
                for kt in range(1, KT, 2):
                    dve.wait_ge(s_tr, KT * k + kt + 1)
                    for g, (a, b) in enumerate(((0, P), (P, 3 * P))):
                        last = dve.tensor_scalar(hT[:, kt, a:b], bank[kt][:, a:b], amod[:, k, kt, g:g + 1],
                                                 modT[:, l, 24 * w + kt, g:g + 1], ALU.mult, ALU.add)
                    last.then_inc(s_hD, 1)

            def gate_diags(l, w):
                for k in range(4):
                    i = 8 * l + 4 * w + k
                    if i:
                        dve.wait_ge(s_gb, i)
                    if w == 0 and k == 0:
                        dve.wait_ge(s_out, 16 * STORES * (l + 1))
                    col = 16 + 24 * w + 4 * (k % 2)
                    dve.tensor_tensor(diag[:, :, :], rep(ident[:, :], 4),
                                      bc(modT[:, l, col:col + 4, k // 2], P), ALU.mult).then_inc(s_dg, 1)

            for l in range(DEPTH):
                ada(l)
                normed(2 * l)
                modulated(2 * l)
                for t in range(NT):
                    dve.wait_ge(s_kv, NT * l + t + 1)
                    dve.tensor_copy(qkv[:, t, 512:768], bank[3 + t][:, 0:256])
                    dve.tensor_tensor(dtr[:, :, t, :], bank[3 + t][:, 256:272].rearrange("p (d h) -> p d h", d=2),
                                      vec[:, l, 0:16].rearrange("p (d h) -> p d h", d=2), ALU.add
                                      ).then_inc(s_kvc, 1)
                dve.wait_ge(s_kvc, NT * (l + 1))
                flat = lambda v: v[:, :, :, :].rearrange("p d t h -> p (d t h)")
                dve.scalar_tensor_tensor(out=flat(dtu), in0=flat(dtr), scalar=-1.0, in1=flat(dtr),
                                         op0=ALU.mult, op1=ALU.max).then_inc(s_dt1, 1)
                for m in range(XM):
                    dve.wait_ge(s_xbcc, XM * l + m + 1)
                    tap = lambda k: prm[:, 48 + 30 * l + 6 * k + m:49 + 30 * l + 6 * k + m]
                    bias = prm[:, 108 + 6 * l + m:109 + 6 * l + m]
                    step(dve.tensor_scalar(conv[:, m, :], xpd[:, m, 0:CONVW], tap(0), bias, ALU.mult, ALU.add))
                    for k in range(1, TAPS):
                        ins = dve.scalar_tensor_tensor(out=conv[:, m, :], in0=xpd[:, m, k:k + CONVW], scalar=tap(k),
                                                       in1=conv[:, m, :], op0=ALU.mult, op1=ALU.add)
                        if k < TAPS - 1:
                            step(ins)
                    ins.then_inc(s_conv, 1)
                dve.wait_ge(s_dt2, 2 * l + 1)
                dve.tensor_scalar(dtv[:, :, :, :], dtu[:, :, :, :], 1.0, None, ALU.add).then_inc(s_dt1, 1)
                dve.wait_ge(s_dt1, 2 * l + 2)
                step(dve.tensor_scalar(dt[:, :, :, :], dtv[:, :, :, :], 1.0, None, ALU.subtract))
                step(dve.tensor_tensor(dtu[:, :, :, :], dtu[:, :, :, :], dt[:, :, :, :], ALU.subtract))
                dve.wait_ge(s_dt2, 2 * l + 2)
                step(dve.reciprocal(dtv[:, :, :, :], dtv[:, :, :, :]))
                step(dve.tensor_tensor(dtu[:, :, :, :], dtu[:, :, :, :], dtv[:, :, :, :], ALU.mult))
                step(dve.tensor_tensor(dtu[:, :, :, :], dtu[:, :, :, :], dtw[:, :, :, :], ALU.add))
                step(dve.scalar_tensor_tensor(out=flat(dt), in0=flat(dtr), scalar=0.0, in1=flat(dtu),
                                              op0=ALU.max, op1=ALU.add))
                for d in range(2):
                    ins = dve.tensor_tensor(da[:, d, :, :], dt[:, d, :, :],
                                            rep(vec[:, l, 16 + 8 * d:24 + 8 * d], NT), ALU.mult)
                ins.then_inc(s_da, 1)

                def masked(t, h):
                    k = 24 * l + 8 * t + h
                    nk, m0 = ((P, 2), (3 * P, 2), (3 * P, 0))[t]
                    dve.wait_ge(s_sc, k + 1)
                    dve.tensor_tensor_reduce(out=probs[:, h, 0:nk], in0=bank[(8 * t + h) % 3][:, 0:nk],
                                             in1=amask[:, m0:m0 + nk // P, :].rearrange("p a b -> p (a b)"),
                                             scale=1.0, scalar=2 * NEG, op0=ALU.add, op1=ALU.max,
                                             accum_out=mx[:, t, h:h + 1]).then_inc(s_scc, 1)

                def maxima(t):
                    dve.wait_ge(s_scc, 24 * l + 8 * (t + 1))
                    step(dve.scalar_tensor_tensor(out=mx[:, t, :], in0=mx[:, t, :], scalar=SCALE,
                                                  in1=vec[:, l, 40:48], op0=ALU.mult, op1=ALU.max))
                    dve.tensor_tensor(es[:, t, :], vec[:, l, 40:48], mx[:, t, :], ALU.subtract)
                    dve.tensor_scalar(nm[:, t, :], mx[:, t, :], -1.0, None, ALU.mult).then_inc(s_nm, 1)

                for h in range(H):
                    masked(0, h)
                maxima(0)
                for t in range(NT):
                    nk = P if t == 0 else 3 * P
                    for h in range(H):
                        k = 24 * l + 8 * t + h
                        dve.wait_ge(s_ptr, k + 1)
                        if k >= 2:
                            dve.wait_ge(s_pv, k - 1)
                        dve.tensor_copy(pT[:, h % 2, 0:nk], bank[3 + h % 2][:, 0:nk]).then_inc(s_pTc, 1)
                        if t + 1 < NT:
                            masked(t + 1, h)
                    if t + 1 < NT:
                        maxima(t + 1)
                    dve.wait_ge(s_es, NT * l + t + 1)
                    step(dve.tensor_tensor(den[:, t, :], rs[:, t, :], es[:, t, :], ALU.add))
                    step(dve.reciprocal(den[:, t, :], den[:, t, :]))
                    dve.wait_ge(s_pv, 24 * l + 8 * (t + 1))
                    dve.tensor_tensor(heads(mixed[:, t, 0:512]), heads(bank[5 + t][:, :]),
                                      bc(den[:, t, :], HD), ALU.mult).then_inc(s_attn, 1)

                dve.wait_ge(s_cum, l + 1)
                dve.tensor_copy(flat(cs), bank[5][:, 0:48])
                step(dve.tensor_copy(flat(tot), bank[5][:, 48:96]))
                dve.tensor_tensor(wend[:, :, :, :], tot[:, :, :, :], cs[:, :, :, :], ALU.subtract).then_inc(s_cs, 1)
                dve.wait_ge(s_g, l + 1)
                for d in range(2):
                    for g in range(2):
                        ins = dve.tensor_tensor(gm[:, d, :, g, :], heads(bank[6 + g][:, 0:NT * P], NT),
                                                rep(tri[:, d, :], NT), ALU.mult)
                ins.then_inc(s_gm, 1)
                dve.wait_ge(s_st, 2 * l + 1)
                dve.tensor_copy(final_st[:, :, :].rearrange("p d c -> p (d c)"), bank[0][:, :]).then_inc(s_ctxs, 1)
                dve.wait_ge(s_stc, l + 1)
                dve.wait_ge(s_ecs, l + 1)
                for d, t in STATES[2:]:
                    for g in range(2):
                        r = slice(g * HD, (g + 1) * HD)
                        ins = dve.tensor_tensor(heads(next_st[r, d, :], 4), heads(init_st[r, d, :], 4),
                                                bc(etot[r, d, t, 4 * g:4 * g + 4], HD), ALU.mult)
                step(ins)
                dve.wait_ge(s_st, 2 * l + 2)
                nx = next_st[:, :, :].rearrange("p d c -> p (d c)")
                dve.tensor_tensor(nx, nx, bank[1][:, :], ALU.add).then_inc(s_snx, 1)

                def seg(k):
                    t, g, d = k // 4, k // 2 % 2, k % 2
                    dve.wait_ge(s_cdec, 12 * l + k + 1)
                    if k >= 2:
                        dve.wait_ge(s_scm, 12 * l + k - 1)
                    w = heads(work[:, k % 2, :], 4)
                    step(dve.tensor_tensor(w, heads(bank[1 + k % 2][:, :], 4),
                                           bc(cs[:, d, t, 4 * g:4 * g + 4], P), ALU.subtract))
                    dve.tensor_scalar(work[:, k % 2, :], work[:, k % 2, :], 0.0, None, ALU.min).then_inc(s_seg, 1)

                def decayed(k):
                    t, g, d = k // 4, k // 2 % 2, k % 2
                    dve.wait_ge(s_dexp, 12 * l + k + 1)
                    if k >= 3:
                        dve.wait_ge(s_y, 6 * l + (k - 3) // 2 + 1)
                    dve.tensor_tensor(heads(scT[:, k % 3, :], 4), heads(work[:, k % 2, :], 4),
                                      rep(gm[:, d, t, g, :], 4), ALU.mult).then_inc(s_scm, 1)

                def finish(t):
                    v = xs_tok[:, t, :]
                    dve.wait_ge(s_xdt, l + 1)
                    step(dve.tensor_tensor(heads(v), heads(v), bc(vec[:, l, 32:40], HD), ALU.mult))
                    dve.wait_ge(s_y, 6 * l + 2 * t + 2)
                    step(dve.tensor_tensor(v, v, bank[6 + t % 2][:, :], ALU.add))
                    if t:
                        dve.wait_ge(s_yoff, 4 * (l + 1))
                        for g in range(2):
                            for d in range(2):
                                ins = dve.tensor_tensor(heads(work[:, 2 + g, d * 256:(d + 1) * 256], 4),
                                                        heads(bank[YOFF_BANK[t, g]][:, d * 256:(d + 1) * 256], 4),
                                                        bc(ecs[:, d, t, 4 * g:4 * g + 4], HD), ALU.mult)
                        step(ins)
                        for d in range(2):
                            step(dve.tensor_tensor(heads(v, 2), heads(v, 2), work[:, 2:4, d * 256:(d + 1) * 256],
                                                   ALU.add))
                    z = mixed[:, t, 512:1024]
                    step(dve.tensor_tensor(z, v, z, ALU.mult))
                    for g in range(2):
                        zg = z[:, g * 256:(g + 1) * 256]
                        ins = dve.tensor_tensor_reduce(out=work[:, 2, g * 256:(g + 1) * 256], in0=zg, in1=zg, scale=1.0,
                                                       scalar=0.0, op0=ALU.mult, op1=ALU.add,
                                                       accum_out=gss[:, t, g:g + 1])
                    ins.then_inc(s_gss, 1)
                    dve.wait_ge(s_grs, NT * l + t + 1)
                    for g in range(2):
                        zg = z[:, g * 256:(g + 1) * 256]
                        ins = dve.scalar_tensor_tensor(out=zg, in0=zg, scalar=grs[:, t, g:g + 1],
                                                       in1=snw[:, g * 256:(g + 1) * 256],
                                                       op0=ALU.mult, op1=ALU.mult)
                    ins.then_inc(s_ssd, 1)

                dve.wait_ge(s_snw, 16 * (l + 1))
                seg(0)
                for k in range(12):
                    if k + 1 < 12:
                        seg(k + 1)
                    decayed(k)
                    if k % 4 == 3:
                        finish(k // 4)

                gate_diags(l, 0)
                for kt in range(1, KT, 2):
                    dve.wait_ge(s_mt, KT * l + kt + 1)
                    dve.tensor_copy(hT[:, kt, :], bank[kt][:, 0:3 * P]).then_inc(s_mD, 1)
                dve.wait_ge(s_gbc, 8 * l + 4)
                for k in range(6):
                    hf, t = k // 3, k % 3
                    dve.wait_ge(s_o, 6 * l + k + 1)
                    if k >= 4:
                        dve.wait_ge(s_x1, 6 * l + k - 3)
                    dve.tensor_tensor(work[:, k % 4, :], bank[k][:, :],
                                      gateB[:, grp(t), hf * 512:(hf + 1) * 512], ALU.mult).then_inc(s_oc, 1)
                normed(2 * l + 1)
                modulated(2 * l + 1)

                R = lambda i: rt[:, i, :, :].rearrange("p t e -> p (t e)")
                G4 = lambda v: v.rearrange("p (a j) -> p a j", j=4)
                E3 = lambda v: v.rearrange("p (t e) -> p t e", e=E)
                dve.wait_ge(s_re, l + 1)
                step(dve.tensor_scalar(R(0), R(0), 1.0, None, ALU.add))
                step(dve.reciprocal(R(0), R(0)))
                step(dve.tensor_tensor(E3(R(1)), E3(R(0)), rep(rb[:, :], NT), ALU.add))
                s4, p4, q4 = G4(R(1)), G4(R(2)), G4(R(3))
                dve.tensor_tensor(p4[:, :, 0:3], s4[:, :, 0:3], s4[:, :, 1:4], ALU.add)
                dve.tensor_tensor(q4[:, :, 0:2], s4[:, :, 0:2], s4[:, :, 2:4], ALU.add)
                step(dve.tensor_tensor(p4[:, :, 3:4], s4[:, :, 0:1], s4[:, :, 3:4], ALU.add))
                step(dve.tensor_tensor(q4[:, :, 0:2], q4[:, :, 0:2], p4[:, :, 0:2], ALU.max))
                step(dve.tensor_tensor(q4[:, :, 0:2], q4[:, :, 0:2], p4[:, :, 2:4], ALU.max))
                gs = rt[:, 4, :, 0:4]
                step(dve.tensor_tensor(gs, q4[:, :, 0:1].rearrange("p (t a) j -> p t (a j)", t=NT),
                                       q4[:, :, 1:2].rearrange("p (t a) j -> p t (a j)", t=NT), ALU.max))
                gmax = rt[:, 4, :, 4:5]

                def first_of_max(v, m, weight, width):
                    step(dve.tensor_reduce(m, v, AX.X, ALU.max))
                    step(dve.tensor_tensor(v, v, m.broadcast_to([P, NT, width]), ALU.is_equal))
                    step(dve.tensor_tensor(v, v, weight, ALU.mult))
                    step(dve.tensor_reduce(m, v, AX.X, ALU.max))
                    step(dve.tensor_tensor(v, v, m.broadcast_to([P, NT, width]), ALU.is_equal))

                first_of_max(gs, gmax, rep(tie[:, 0:4], NT), 4)
                ing = rt[:, 5, :, :]
                step(dve.tensor_copy(ing.rearrange("p t (a j) -> p t a j", j=4),
                                     gs.unsqueeze(3).broadcast_to([P, NT, 4, 4])))
                off = rt[:, 6, :, :]
                step(dve.tensor_scalar(off, ing, -NEG, NEG, ALU.mult, ALU.add))
                step(dve.tensor_tensor(R(2), R(1), R(5), ALU.mult))
                step(dve.tensor_tensor(R(2), R(2), R(6), ALU.add))
                step(dve.tensor_copy(R(3), R(2)))
                first_of_max(rt[:, 3, :, :], rt[:, 4, :, 5:6], rep(tie[:, :], NT), E)
                step(dve.tensor_scalar(R(5), R(3), 4 * NEG, None, ALU.mult))
                step(dve.tensor_tensor(R(2), R(2), R(5), ALU.add))
                first_of_max(rt[:, 2, :, :], rt[:, 4, :, 6:7], rep(tie[:, :], NT), E)
                dve.tensor_tensor(R(5), R(3), R(2), ALU.add).then_inc(s_sel, 1)
                step(dve.tensor_tensor(R(6), R(3), R(0), ALU.mult))
                dve.wait_ge(s_sel, l + 1)
                dve.tensor_reduce(gw[:, 0, :].unsqueeze(2), rt[:, 6, :, :], AX.X, ALU.add)
                step(dve.tensor_tensor(R(7), R(2), R(0), ALU.mult))
                step(dve.tensor_reduce(gw[:, 1, :].unsqueeze(2), rt[:, 7, :, :], AX.X, ALU.add))
                step(dve.tensor_tensor(R(6)[:, 0:NT], gw[:, 0, :], gw[:, 1, :], ALU.add))
                step(dve.reciprocal(R(6)[:, 0:NT], R(6)[:, 0:NT]))
                step(dve.tensor_tensor(gw[:, :, :], gw[:, :, :], rep(R(6)[:, 0:NT], 2), ALU.mult))
                dve.wait_ge(s_pos, l + 1)
                step(dve.tensor_tensor(R(1), bank[7][:, 0:NT * E], R(5), ALU.mult))
                step(dve.tensor_scalar(R(1), R(1), 1.0, None, ALU.subtract))

                for e in range(E):
                    if e >= 4:
                        dve.wait_ge(s_idm, E * l + e - 3)
                    dve.tensor_tensor(onehot[:, e % 4, :, :], rep(slots_f[:, :], NT), bc(rt[:, 1, :, e], CAP),
                                      ALU.is_equal).then_inc(s_oh, 1)
                    if e in (5, E - 1):
                        a, b = (0, 4) if e == 5 else (4, E)
                        dve.wait_ge(s_idm, E * l + b)
                        v = bank[7 if a == 0 else 0][:, 64:64 + 2 * E].rearrange("p (e i) -> p e i", i=2)
                        step(dve.tensor_copy(R(4)[:, 16 + a:16 + b], v[:, a:b, 0]))
                        dve.tensor_tensor(idx[:, a:b], R(4)[:, 16 + a:16 + b], v[:, a:b, 1],
                                          ALU.add).then_inc(s_idx, 1)
                def result_rows(step):
                    dve.tensor_scalar(R(0), R(1), float(CAP), None, ALU.is_lt)
                    step(dve.tensor_scalar(R(6), R(1), 0.0, None, ALU.is_ge))
                    step(dve.tensor_tensor(R(0), R(0), R(6), ALU.mult))
                    step(dve.tensor_tensor(E3(R(6)), E3(R(1)), rep(e_row[:, :], NT), ALU.add))
                    for i, chosen in enumerate((3, 2)):
                        step(dve.tensor_tensor(R(5), R(chosen), R(0), ALU.mult))
                        dve.tensor_reduce(R(4)[:, 12 + 4 * i:12 + 4 * i + NT].unsqueeze(2), rt[:, 5, :, :],
                                          AX.X, ALU.add)
                        step(dve.tensor_tensor(R(7), R(5), R(6), ALU.mult))
                        step(dve.tensor_reduce(R(4)[:, 4 * i:4 * i + NT].unsqueeze(2), rt[:, 7, :, :],
                                               AX.X, ALU.add))
                        dve.tensor_tensor(wt[:, i, :], gw[:, i, :], R(4)[:, 12 + 4 * i:12 + 4 * i + NT], ALU.mult)
                        step(dve.tensor_copy(y_idx[:, i, :], R(4)[:, 4 * i:4 * i + NT]))

                result_rows(step)
                dve.sem_inc(s_yidx, 1)
                top = R(4)[:, 8:9]
                step(dve.tensor_reduce(top, bank[7][:, 48:64], AX.X, ALU.max))
                step(dve.tensor_scalar(R(4)[:, 9:10], top, float(CAP), None, ALU.is_gt))
                for k in range(2, MORE + 1):
                    step(dve.tensor_scalar(R(4)[:, 10:11], top, float(k * CAP), None, ALU.is_gt))
                    step(dve.tensor_tensor(R(4)[:, 9:10], R(4)[:, 9:10], R(4)[:, 10:11], ALU.add))
                dve.tensor_copy(rounds[:, l:l + 1], R(4)[:, 9:10]).then_inc(s_rounds, 1)
                gate_diags(l, 1)

                def copy_rows(e, b):
                    dve.wait_ge(s_tx, e + (E * l + 1))
                    for hf in range(2):
                        dve.tensor_copy(xgT[:, b, hf * 512:(hf + 1) * 512], bank[3 + hf][:, :]).then_inc(s_xgc, 1)

                def hidden(e, b):
                    dve.wait_ge(s_sil, e + (E * l + 1))
                    dve.tensor_tensor(hid[:, b, :], sil[:, b, :], bank[b][:, F:2 * F], ALU.mult).then_inc(s_hid, 1)

                def copy_hidden(e, b):
                    dve.wait_ge(s_th, e + (E * l + 1))
                    dve.tensor_copy(hidT[:, b, :], bank[2][:, 0:F]).then_inc(s_htc, 1)

                copy_rows(0, 0)
                copy_rows(1, 1)
                hidden(0, 0)
                with dve.Fori(0, E // 2 - 1) as i:
                    copy_hidden(2 * i, 0)
                    copy_rows(2 * i + 2, 0)
                    hidden(2 * i + 1, 1)
                    copy_hidden(2 * i + 1, 1)
                    copy_rows(2 * i + 3, 1)
                    hidden(2 * i + 2, 0)
                copy_hidden(E - 2, 0)
                hidden(E - 1, 1)
                copy_hidden(E - 1, 1)

                def next_round(k):
                    dve.tensor_scalar(R(1), R(1), float(CAP), None, ALU.subtract).then_inc(o_pos, 1)
                    dve.wait_ge(o_pos, k + 1)
                    dve.sem_inc(o_pass, 1)

                def again(e, q):
                    dve.tensor_copy(R(7)[:, 0:NT].unsqueeze(2), rt[:, 1, :, bass.ds(e, 1)]).then_inc(o_sel, 1)
                    dve.wait_ge(o_sel, q + 1)
                    dve.tensor_tensor(onehot[:, 0, :, :], rep(slots_f[:, :], NT), bc(R(7)[:, 0:NT], CAP),
                                      ALU.is_equal).then_inc(o_oh, 1)
                    dve.wait_ge(o_idm, q + 1)
                    dve.tensor_copy(R(4)[:, 16:17], bank[7][:, 64:65]).then_inc(o_c0, 1)
                    dve.wait_ge(o_c0, q + 1)
                    dve.tensor_tensor(idx[:, 0:1], R(4)[:, 16:17], bank[7][:, 65:66], ALU.add).then_inc(o_idx, 1)
                    dve.wait_ge(o_tx, q + 1)
                    dve.tensor_copy(xgT[:, 0, 0:512], bank[3][:, :])
                    dve.tensor_copy(xgT[:, 0, 512:1024], bank[4][:, :]).then_inc(o_xgc, 1)
                    dve.wait_ge(o_sil, q + 1)
                    dve.tensor_tensor(hid[:, 0, :], sil[:, 0, :], bank[0][:, F:2 * F], ALU.mult).then_inc(o_hid, 1)
                    dve.wait_ge(o_th, q + 1)
                    dve.tensor_copy(hidT[:, 0, :], bank[2][:, 0:F]).then_inc(o_htc, 1)

                for t in range(NT):
                    a = acc[:, t, :]
                    dve.wait_ge(combined[t], 32 * (l + 1))
                    step(dve.tensor_scalar(a, a, wt[:, 1, t:t + 1], None, ALU.mult))
                    step(dve.scalar_tensor_tensor(out=a, in0=xg[t], scalar=wt[:, 0, t:t + 1], in1=a,
                                                  op0=ALU.mult, op1=ALU.add))

                def add_results(k):
                    n = [0]

                    def round_step(ins):
                        n[0] += 1
                        ins.then_inc(o_step, 1)
                        dve.wait_ge(o_step, k * RESULT_STEPS + n[0])

                    result_rows(round_step)
                    assert n[0] == RESULT_STEPS
                    dve.sem_inc(o_rows, 1)
                    for j in range(2 * NT):
                        t, i = j // 2, j % 2
                        dve.wait_ge(o_c, 16 * 2 * NT * k + 16 * (j + 2))
                        dve.scalar_tensor_tensor(out=acc[:, t, :], in0=xg[0], scalar=wt[:, i, t:t + 1],
                                                 in1=acc[:, t, :], op0=ALU.mult, op1=ALU.add).then_inc(o_add, 1)
                        dve.wait_ge(o_add, 2 * NT * k + j + 1)
                    dve.sem_inc(o_pass, 1)

                overflow(dve, l, again, start=next_round, stop=add_results)

                dve.wait_ge(s_gbc, 8 * l + 8)
                for t in range(NT):
                    a = acc[:, t, :]
                    dve.tensor_tensor(a, a, gateB[:, grp(t), :], ALU.mult).then_inc(s_fin, 1)
            dve.wait_ge(s_rstd, 2 * DEPTH + 1)
            dve.wait_ge(s_fnw, 16)
            for t in range(NT):
                dve.scalar_tensor_tensor(out=xn[:, t, :], in0=x[:, t, :], scalar=rstd[:, 2 * DEPTH, t:t + 1],
                                         in1=gateB[:, 0, :], op0=ALU.mult, op1=ALU.mult).then_inc(s_y_out, 1)

        @block.tensor
        def _(pe):
            mm, tr = pe.matmul, pe.transpose
            pe.sem_inc(o_dn, 1)

            def arrived(u):
                pe.wait_ge(landed[u % SLOTS], 32 * (u // SLOTS + 1))

            pe.wait_ge(s_const, 1)
            pe.wait_ge(s_rows, 16 * 7)
            tr(bank[0][:, 0:120], prm_rows[0:120, :], ident[0:120, 0:120]).then_inc(s_prmT, 1)
            tr(bank[1][:, 0:96], bada_rows[0:96, :], ident[0:96, 0:96]).then_inc(s_prmT, 1)

            def ada(l, u0):
                def columns(k):
                    pe.wait_ge(s_row, k + 1)
                    if k >= 2:
                        pe.wait_ge(s_mod, k - 1)
                    for j in range(4):
                        last = tr(bank[4 + k % 2][:, 2 * j:2 * j + 2], ada_row[0:2, k % 2, j * P:(j + 1) * P],
                                  ident[0:2, 0:2])
                    last.then_inc(s_rowT, 1)

                for j in range(ADA_U):
                    k, u = ADA_U * l + j, u0 + j
                    arrived(u)
                    if k >= 2:
                        pe.wait_ge(s_row, k - 1)
                    for kt in range(KT):
                        last = mm(bank[6 + k % 2][0:2, :], cT[:, kt, :], slot(u)[:, kt, :],
                                  start=kt == 0, stop=kt == KT - 1)
                    last.then_inc(s_ada, 1)
                    if j:
                        columns(k - 1)
                columns(ADA_U * (l + 1) - 1)

            def norm_transposes(k):
                for t in range(NT):
                    pe.wait_ge(s_xn, NT * k + t + 1)
                for kt in range(KT):
                    for t in range(NT):
                        last = tr(bank[kt][:, t * P:(t + 1) * P], xn[:, t, kt * P:(kt + 1) * P], ident[:, :])
                    last.then_inc(s_tr, 1)
                pe.wait_ge(s_hA, 4 * (k + 1))
                pe.wait_ge(s_hD, 4 * (k + 1))

            def gate_rows(l, w):
                for k in range(4):
                    i = 8 * l + 4 * w + k
                    pe.wait_ge(s_dg, i + 1)
                    if k >= 2:
                        pe.wait_ge(s_gbc, i - 1)
                    mm(bank[6 + k % 2][:, :], onesP, diag[:, :, :].rearrange("p a c -> p (a c)"),
                       start=True, stop=True).then_inc(s_gb, 1)

            pe.wait_ge(s_cT, 1)
            pe.wait_ge(s_bada, 1)
            u = 0
            for l in range(DEPTH):
                ada(l, u)
                u += ADA_U
                pe.wait_ge(s_mod, ADA_U * (l + 1))
                norm_transposes(2 * l)

                tok = lambda kt, t: hT[:, kt, t * P:(t + 1) * P]
                arrived(u)
                for t in range(NT):
                    for kt in range(KT):
                        last = mm(bank[t][:, :], tok(kt, t), slot(u)[:, kt, :], start=kt == 0, stop=kt == KT - 1)
                    last.then_inc(s_q, 1)
                arrived(u + 1)
                if l == 0:
                    pe.wait_ge(s_small, 16 * SMALL)
                for t in range(NT):
                    for kt in range(KT):
                        mm(bank[3 + t][:, 0:256], tok(kt, t), slot(u + 1)[:, kt, 0:256],
                           start=kt == 0, stop=kt == KT - 1)
                    for kt in range(KT):
                        last = mm(bank[3 + t][:, 256:272], tok(kt, t), wdt[:, l, kt, :],
                                  start=kt == 0, stop=kt == KT - 1)
                    last.then_inc(s_kv, 1)
                for m in range(XM):
                    v, col = (u + 1, 256 + m * P) if m < 2 else (u + 2, (m - 2) * P)
                    if m == 2:
                        arrived(v)
                    if 2 <= m < 5:
                        pe.wait_ge(s_qc, NT * l + m - 1)
                    if m == 5:
                        pe.wait_ge(s_kvc, NT * l + 1)
                    for kt in range(KT):
                        last = mm(bank[(6 + m) % 8][:, 0:3 * P], slot(v)[:, kt, col:col + P], hT[:, kt, :],
                                  start=kt == 0, stop=kt == KT - 1)
                    last.then_inc(s_xbc, 1)
                arrived(u + 3)
                for t in range(NT):
                    if t < 2:
                        pe.wait_ge(s_kvc, NT * l + t + 2)
                    else:
                        pe.wait_ge(s_xbcc, XM * l + 1)
                    for kt in range(KT):
                        last = mm(bank[4 + t][:, :], tok(kt, t), slot(u + 3)[:, kt, :],
                                  start=kt == 0, stop=kt == KT - 1)
                    last.then_inc(s_z, 1)
                u += IN_U

                for t in range(NT):
                    pe.wait_ge(s_xbcc, XM * l + t + 2)
                    if t:
                        pe.wait_ge(s_rope, 2 * l + t)
                    else:
                        pe.wait_ge(s_qc, NT * l + 1)
                        pe.wait_ge(s_kvc, NT * l + 1)
                    src = qkv[:, 0, 0:512] if t == 0 else rot[:, t - 1, 0:512]
                    for j in range(4):
                        last = tr(bank[(7, 0, 1)[t]][:, j * P:(j + 1) * P], src[:, j * P:(j + 1) * P], ident[:, :])
                    last.then_inc(s_qtr, 1)
                pe.wait_ge(s_xbcc, XM * l + 5)
                for i, src in enumerate((ckv[:, 0, l, :], rot[:, 0, 512:640], rot[:, 1, 512:640], qkv[:, 0, 512:640])):
                    last = tr(bank[2][:, i * P:(i + 1) * P], src, ident[:, :])
                last.then_inc(s_qtr, 1)

                def scores(t, h):
                    k = 24 * l + 8 * t + h
                    if 8 * t + h >= 3:
                        pe.wait_ge(s_scc, k - 2)
                    r = slice(HD * (h // 4), HD * (h // 4 + 1))
                    keys = kT[r, 3:4, :] if t == 0 else kT[r, 0:3, :]
                    nk = P if t == 0 else 3 * P
                    mm(bank[(8 * t + h) % 3][:, 0:nk], qT[r, t, h % 4, :], keys.rearrange("p a c -> p (a c)"),
                       start=True, stop=True).then_inc(s_sc, 1)

                pe.wait_ge(s_qTc, 4 * (l + 1))
                pe.wait_ge(s_zc, NT * (l + 1))
                pe.wait_ge(s_xbcc, XM * (l + 1))
                for h in range(H):
                    scores(0, h)
                for t in range(NT):
                    parts = 1 if t == 0 else 3
                    for h in range(H):
                        k = 24 * l + 8 * t + h
                        pe.wait_ge(s_exp, k + 1)
                        if 8 * t + h >= 2:
                            pe.wait_ge(s_pTc, k - 1)
                        for a in range(parts):
                            last = tr(bank[3 + h % 2][:, a * P:(a + 1) * P], probs[:, h, a * P:(a + 1) * P],
                                      ident[:, :])
                        last.then_inc(s_ptr, 1)
                        if t + 1 < NT:
                            scores(t + 1, h)
                        pe.wait_ge(s_pTc, k + 1)
                        kv = HD * (h // 4)
                        vals = (qkv[:, 0, 640:768],) if t == 0 else (ckv[:, 1, l, :], qkv[:, 1, 640:768],
                                                                     qkv[:, 2, 640:768])
                        for a in range(parts):
                            last = mm(bank[5 + t][:, h * HD:(h + 1) * HD], pT[:, h % 2, a * P:(a + 1) * P],
                                      vals[a][:, kv:kv + HD], start=a == 0, stop=a == parts - 1)
                        last.then_inc(s_pv, 1)

                pe.wait_ge(s_silu, XM * (l + 1))
                for t in range(NT):
                    o = tile_at(t)
                    for m in range(4):
                        last = tr(bank[t][:, m * P:(m + 1) * P], conv[:, m, o:o + P], ident[:, :])
                    last.then_inc(s_xtr, 1)
                for t in range(NT):
                    o = tile_at(t)
                    last = tr(bank[3][:, t * P:(t + 1) * P], conv[:, 4, o:o + P], ident[:, :])
                last.then_inc(s_xtr, 1)
                pe.wait_ge(s_state, 64 * (l + 1))
                for d in range(2):
                    for jj in range(2):
                        i = 2 * d + jj
                        last = tr(bank[4][:, i * P:(i + 1) * P],
                                  st_in[:, d, jj, :, :].rearrange("p g n -> p (g n)"), ident[:, :])
                last.then_inc(s_xtr, 1)
                pe.wait_ge(s_da, l + 1)
                pe.wait_ge(s_attn, NT * (l + 1))
                for d in range(2):
                    mm(bank[5][:, 24 * d:24 * d + 24], tri[:, d, :], da[:, d, :, :].rearrange("p t h -> p (t h)"),
                       start=True, stop=True)
                mm(bank[5][:, 48:96], onesP, da[:, :, :, :].rearrange("p d t h -> p (d t h)"),
                   start=True, stop=True).then_inc(s_cum, 1)
                for i in range(6):
                    t, g = i // 2, i % 2
                    o, r = tile_at(t), slice(g * HD, (g + 1) * HD)
                    last = mm(bank[6 + g][:, t * P:(t + 1) * P], conv[r, 4, o:o + P],
                              conv[r, 5, o:o + P], start=True, stop=True)
                last.then_inc(s_g, 1)
                pe.wait_ge(s_xtc, 4 * (l + 1))
                for k, (d, t) in enumerate(STATES):
                    pe.wait_ge(s_xw, 4 * l + k + 1)
                    for g in range(2):
                        r = slice(g * HD, (g + 1) * HD)
                        last = mm(bank[k // 2][r, d * 256:(d + 1) * 256], b_tok[:, t, g * HD:(g + 1) * HD],
                                  work[:, k, g * 256:(g + 1) * 256], start=True, stop=True)
                    if k % 2:
                        last.then_inc(s_st, 1)
                pe.wait_ge(s_ctxs, l + 1)
                for i in range(4):
                    last = tr(bank[2][:, i * P:(i + 1) * P], final_st[:, i // 2, (i % 2) * P:(i % 2 + 1) * P],
                              ident[:, :])
                last.then_inc(s_sto, 1)
                pe.wait_ge(s_stc, l + 1)
                pe.wait_ge(s_cs, l + 1)
                for t, d, s in ((1, 0, init_st), (2, 1, init_st), (1, 1, next_st), (2, 0, next_st)):
                    if s is next_st:
                        pe.wait_ge(s_snx, l + 1)
                    o = tile_at(t)
                    for g in range(2):
                        r = slice(g * HD, (g + 1) * HD)
                        last = mm(bank[YOFF_BANK[t, g]][:, d * 256:(d + 1) * 256], conv[r, 5, o:o + P],
                                  s[r, d, :], start=True, stop=True)
                    last.then_inc(s_yoff, 1)

                def decay_rows(k):
                    t, g, d = k // 4, k // 2 % 2, k % 2
                    if k >= 2:
                        pe.wait_ge(s_seg, 12 * l + k - 1)
                    for h in range(4):
                        last = mm(bank[1 + k % 2][:, h * P:(h + 1) * P],
                                  da[:, d, t, 4 * g + h:4 * g + h + 1].broadcast_to([P, P]), tri[:, d, :],
                                  start=True, stop=True)
                    last.then_inc(s_cdec, 1)

                pe.wait_ge(s_stoc, l + 1)
                pe.wait_ge(s_snx, l + 1)
                pe.wait_ge(s_gm, l + 1)
                pe.wait_ge(s_xdt, l + 1)
                decay_rows(0)
                decay_rows(1)
                for p in range(6):
                    if p < 5:
                        decay_rows(2 * p + 2)
                        decay_rows(2 * p + 3)
                    t, g = p // 2, p % 2
                    if p == 4:
                        pe.wait_ge(s_gss, NT * l + 1)
                    pe.wait_ge(s_scm, 12 * l + 2 * p + 2)
                    for h in range(4):
                        hh = 4 * g + h
                        for d in range(2):
                            last = mm(bank[6 + t % 2][:, hh * HD:(hh + 1) * HD],
                                      scT[:, (2 * p + d) % 3, h * P:(h + 1) * P],
                                      xdt[:, d, t, hh * HD:(hh + 1) * HD], start=d == 0, stop=d == 1)
                    last.then_inc(s_y, 1)

                pe.wait_ge(s_ssd, NT * (l + 1))
                gate_rows(l, 0)
                pe.wait_ge(s_gbc, 8 * l + 4)
                for kt in range(KT):
                    for t in range(NT):
                        last = tr(bank[kt][:, t * P:(t + 1) * P], mixed[:, t, kt * P:(kt + 1) * P], ident[:, :])
                    last.then_inc(s_mt, 1)
                pe.wait_ge(s_mA, 4 * (l + 1))
                pe.wait_ge(s_mD, 4 * (l + 1))
                for hf in range(2):
                    arrived(u + hf)
                    for t in range(NT):
                        for kt in range(KT):
                            last = mm(bank[3 * hf + t][:, :], tok(kt, t), slot(u + hf)[:, kt, :],
                                      start=kt == 0, stop=kt == KT - 1)
                        last.then_inc(s_o, 1)
                u += OUT_U
                norm_transposes(2 * l + 1)

                for t in range(NT):
                    for kt in range(KT):
                        last = mm(bank[0][:, t * E:(t + 1) * E], tok(kt, t), wr[:, kt, :],
                                  start=kt == 0, stop=kt == KT - 1)
                last.then_inc(s_r, 1)
                pe.wait_ge(s_re, l + 1)
                for t in range(NT):
                    for hf in range(2):
                        for j in range(4):
                            last = tr(bank[1 + 2 * t + hf][:, j * P:(j + 1) * P], tok(4 * hf + j, t), ident[:, :])
                        last.then_inc(s_bt, 1)
                pe.wait_ge(s_sel, l + 1)
                for t in range(NT):
                    for a in range(t + 1):
                        mm(bank[7][:, t * E:(t + 1) * E], tri[:, 0, :] if a == t else onesP, rt[:, 5, a, :],
                           start=a == 0, stop=a == t)
                for a in range(NT):
                    last = mm(bank[7][:, 48:64], onesP, rt[:, 5, a, :], start=a == 0, stop=a == NT - 1)
                last.then_inc(s_pos, 1)

                def slot_tokens(b, e, done):
                    for t in range(NT):
                        last = mm(bank[7 if e < 4 else 0][:, 64 + 2 * e:66 + 2 * e], onehot[:, b, t, :], tok_id[:, t, :],
                                  start=t == 0, stop=t == NT - 1)
                    last.then_inc(done, 1)

                for e in range(E):
                    pe.wait_ge(s_oh, E * l + e + 1)
                    slot_tokens(e % 4, e, s_idm)

                turn = u // SLOTS

                def rows_transposed(buf, done):
                    for kt in range(KT):
                        last = tr(bank[3 + kt // 4][:, kt % 4 * P:(kt % 4 + 1) * P], buf[:, kt * P:(kt + 1) * P],
                                  ident[:, :])
                    last.then_inc(done, 1)

                def gate_up(b, w, done):
                    for kt in range(KT):
                        last = mm(bank[b][:, :], xgT[:, b, kt * P:(kt + 1) * P], w[:, kt, :],
                                  start=kt == 0, stop=kt == KT - 1)
                    last.then_inc(done, 1)

                def hidden_transposed(b, done):
                    for f in range(2):
                        last = tr(bank[2][:, f * P:(f + 1) * P], hid[:, b, f * P:(f + 1) * P], ident[:, :])
                    last.then_inc(done, 1)

                def down(b, w, done):
                    w = w.rearrange("p (f n) -> p f n", f=2)
                    for hf in range(2):
                        for f in range(2):
                            last = mm(bank[5 + hf][:, :], hidT[:, b, f * P:(f + 1) * P],
                                      w[:, f, hf * 512:(hf + 1) * 512], start=f == 0, stop=f == 1)
                    last.then_inc(done, 1)

                GU, DN = (0, 1, 3, 4), (2, 2, 5, 5)

                def rows(e, j, i):
                    pe.wait_ge(gathered[j], 16 * i + (4 * 16 * l + 16))
                    rows_transposed(xg[j], s_tx)

                def first_half(e, j, i):
                    pe.wait_ge(s_xgc, 2 * e + (2 * E * l + 2))
                    pe.wait_ge(landed[GU[j]], 32 * i + 32 * (turn + 1))
                    gate_up(j % 2, slot(GU[j]), s_gu)

                def hid_of(e, j):
                    pe.wait_ge(s_hid, e + (E * l + 1))
                    hidden_transposed(j % 2, s_th)

                def second_half(e, j, i):
                    pe.wait_ge(s_htc, e + (E * l + 1))
                    pe.wait_ge(s_yc, 2 * e + (2 * E * l + 2))
                    if j % 2 == 0:
                        pe.wait_ge(landed[DN[j]], 32 * i + 32 * (turn + 1))
                    down(j % 2, ring[:, DN[j], j % 2 * 2 * DM:(j % 2 + 1) * 2 * DM], s_dn)

                pe.wait_ge(s_btc, 6 * (l + 1))
                gate_rows(l, 1)
                rows(0, 0, 0)
                pe.wait_ge(s_xgc, 2 * E * l + 2)
                rows(1, 1, 0)
                pe.wait_ge(s_gbc, 8 * l + 8)
                first_half(0, 0, 0)

                def body(i, last=False):
                    for j in range(4):
                        e, n1, n2 = 4 * i + j, (j + 1) % 4, (j + 2) % 4
                        if not (last and j == 3):
                            first_half(e + 1, n1, i + (j == 3))
                        hid_of(e, j)
                        if not (last and j >= 2):
                            rows(e + 2, n2, i + (j >= 2))
                        second_half(e, j, i)

                with pe.Fori(0, E // 4 - 1) as i:
                    body(i)
                body(E // 4 - 1, True)
                u += MOE_U

                def again(e, q):
                    pe.wait_ge(o_oh, q + 1)
                    slot_tokens(0, 0, o_idm)
                    pe.wait_ge(o_g, 16 * q + 16)
                    rows_transposed(xg[0], o_tx)
                    pe.wait_ge(o_xgc, q + 1)
                    pe.wait_ge(o_w, 48 * q + 48)
                    gate_up(0, slot(0), o_gu)
                    pe.wait_ge(o_hid, q + 1)
                    hidden_transposed(0, o_th)
                    pe.wait_ge(o_htc, q + 1)
                    down(0, ring[:, 2, 0:2 * DM], o_dn)

                def banks_read(steps):
                    pe.wait_ge(o_yc, 2 * steps)
                    pe.sem_inc(o_pass, 1)

                overflow(pe, l, again, end=banks_read)
                pe.wait_ge(s_yc, 2 * E * (l + 1) + 2)


def rope_tables():
    tokens, grid_w = 256, 64
    row = (np.arange(tokens) // grid_w).astype(np.float32)
    col = (np.arange(tokens) % grid_w).astype(np.float32)
    n = HD // 4
    inv = np.power(np.float32(10000.0), -np.arange(n, dtype=np.float32) / np.float32(n)).astype(np.float32)
    ang = np.concatenate([row[:, None] * inv, col[:, None] * inv], axis=-1).astype(np.float32)
    return np.cos(ang).astype(np.float32), np.sin(ang).astype(np.float32)


_INS = ['x_prompt', 'x_sample', 'cache_k', 'cache_v', 'state_ssm', 'c', 'c_ctx', 'norm1_w', 'norm2_w',
        'final_norm_w', 'w_ada', 'b_ada', 'w_in', 'conv_w', 'conv_b', 'attn_sink', 'dt_bias', 'a_log',
        'd_skip', 'ssd_norm_w', 'w_out', 'w_router', 'router_bias', 'w_gate', 'w_up', 'w_down']
_OUTS = [(1, 128, 1024), (1, 256, 1024), (1, 2, 128, 2, 64), (1, 2, 128, 2, 64), (1, 2, 2, 8, 64, 64)]


def kernel(**inputs):
    import numpy as _np
    import concourse.bacc as _bacc
    from concourse import mybir as _mybir
    from concourse.bass_utils import run_bass_kernel_spmd as _run

    nc = _bacc.Bacc("TRN2", target_bir_lowering=False, num_devices=1)
    arrays, args = {}, []
    cos, sin = rope_tables()
    for name, a in [(n, inputs[n]) for n in _INS] + [("rope_cos", cos), ("rope_sin", sin)]:
        a = _np.ascontiguousarray(a)
        arrays[f"in_{name}_dram"] = a
        args.append(nc.dram_tensor(f"in_{name}_dram", a.shape, _mybir.dt.from_np(a.dtype), kind="ExternalInput").ap())
    for i, shape in enumerate(_OUTS):
        args.append(nc.dram_tensor(f"out_{i}_dram", shape, _mybir.dt.float32, kind="ExternalOutput").ap())
    hybrid_step(nc, *args)
    r = _run(nc, [arrays], core_ids=[0])
    return tuple(r.results[0][f"out_{i}_dram"] for i in range(len(_OUTS)))
```

```python
import concourse.bass as bass
from concourse import mybir
from contextlib import ExitStack
import numpy as np

P = 128
DM = 1024
KT = DM // P
DEPTH = 2
NT = 3
H = 8
HD = 64
FREQ = HD // 2
AW = H * HD
IN_W = 2064
DT0 = 2048
XM = 6
TAPS = 5
PADW = 392
CONVW = PADW - (TAPS - 1)
E = 16
F = 256
CAP = 128
MORE = -(-NT * P // CAP) - 1
SMALL = 18
SLOTS = 6
UNIT = KT * 512
ADA_U, IN_U, OUT_U, MOE_U = 12, 4, 2, 24
ADA_CUT = (4, 12, 18, 24)
ADA_BLK = 4
ADA_PART = 8
C0 = 2 * (ADA_PART - 1)
ORDER = [("ada", j) for j in range(ADA_CUT[0])]
IN_AT, OUT_AT, MOE_AT = [], [], []
for _l in range(DEPTH):
    IN_AT.append(len(ORDER))
    ORDER += [("in", IN_U * _l + j) for j in range(IN_U)]
    ORDER += [("ada", j) for j in range(ADA_CUT[2 * _l], ADA_CUT[2 * _l + 1])]
    OUT_AT.append(len(ORDER))
    ORDER += [("out", OUT_U * _l + j) for j in range(OUT_U)]
    MOE_AT.append(len(ORDER))
    assert len(ORDER) % SLOTS == 0
    ORDER += [("moe", MOE_U * _l + j) for j in range(MOE_U)]
    if _l + 1 < DEPTH:
        ORDER += [("ada", j) for j in range(ADA_CUT[2 * _l + 1], ADA_CUT[2 * _l + 2])]
        assert len(ORDER) % SLOTS == 0
OVER_GU, OVER_DN = 4, 5
ADA_AT = [ORDER.index(("ada", j)) for j in range(DEPTH * ADA_U)]
EPS = 1e-6
NEG = -1e30
SCALE = HD ** -0.5


def hybrid_step(nc, x_prompt, x_sample, cache_k, cache_v, state_ssm, c, c_ctx, norm1_w, norm2_w,
                final_norm_w, w_ada, b_ada, w_in, conv_w, conv_b, attn_sink, dt_bias, a_log, d_skip,
                ssd_norm_w, w_out, w_router, router_bias, w_gate, w_up, w_down, rope_cos, rope_sin,
                y_prompt, y_sample, new_k, new_v, new_state):
    fp32, bf16, i32, u32 = mybir.dt.float32, mybir.dt.bfloat16, mybir.dt.int32, mybir.dt.uint32
    ALU = mybir.AluOpType
    ACT = mybir.ActivationFunctionType
    AX = mybir.AxisListType

    ctx = ExitStack()
    with ctx:
        def sb(name, *shape):
            return ctx.enter_context(nc.sbuf_tensor(name, [P, *shape], fp32))

        def sem(name):
            return ctx.enter_context(nc.semaphore(name))

        ring = sb("ring", SLOTS, UNIT)
        x = sb("x", NT, DM)
        xn = sb("xn", NT, DM)
        mixed = xn
        acc = xn
        hT = sb("hT", KT, NT * P)
        probs = hT[:, :, :]
        qkv = sb("qkv", NT, 768)
        rot = sb("rot", 2, 640)
        pT = rot[:, :, 0:NT * P]
        xpad = sb("xpad", XM * 512)
        xpd = xpad[:, 0:XM * PADW].rearrange("p (m w) -> p m w", m=XM)
        xdt = xpad[:, :].rearrange("p (d t c) -> p d t c", d=2, t=NT)
        conv = sb("conv", XM, CONVW)
        gate_at = ((xpad[:, 0:DM], xpad[:, DM:2 * DM]),
                   (xpad[:, 2 * DM:3 * DM], conv[:, :, :].rearrange("p m w -> p (m w)")[:, DM:2 * DM]))
        scT = conv[:, :, :].rearrange("p m w -> p (m w)")[:, 0:3 * 512].rearrange("p (n c) -> p n c", n=3)
        xs_tok = sb("xs_tok", NT, 512)
        b_tok = sb("b_tok", NT, P)
        ssd = hT[:, :, :].rearrange("p k c -> p (k c)")
        gm = ssd[:, 0:12 * P].rearrange("p (d t g c) -> p d t g c", d=2, t=NT, g=2)
        init_st, next_st, final_st = (ssd[:, 12 * P + i * 512:12 * P + (i + 1) * 512].rearrange("p (d c) -> p d c", d=2)
                             for i in range(3))
        qT = sb("qT", NT, 4, P)
        kT = sb("kT", 4, P)
        work = sb("work", 4, 512)
        xg = [ssd[:, i * DM:(i + 1) * DM] for i in range(3)] + [
            rot[:, :, :].rearrange("p a c -> p (a c)")[:, 0:DM]]
        xgT = work[:, :, :].rearrange("p (b a) c -> p b (a c)", b=2)
        fnw = xgT[:, 1, :]
        sil, hid, hidT = (xs_tok[:, i, :].rearrange("p (b c) -> p b c", b=2) for i in range(3))
        y_rows = qkv[:, :, :].rearrange("p t c -> p (t c)")[:, 0:2 * DM].rearrange("p (b c) -> p b c", b=2)
        onehot = conv[:, :, :].rearrange("p m w -> p (m w)")[:, 0:4 * NT * P // 2].bitcast(bf16).rearrange(
            "p (b t c) -> p b t c", b=4, t=NT)

        ident = sb("ident", P)
        tri = sb("tri", 2, P)
        one = sb("one", 1)
        tri_b = ctx.enter_context(nc.sbuf_tensor("tri_b", [P, P], bf16))
        one_b = ctx.enter_context(nc.sbuf_tensor("one_b", [P, 2], bf16))
        chosen_b = ctx.enter_context(nc.sbuf_tensor("chosen_b", [P, NT, E], bf16))
        slots_f = sb("slots_f", CAP)
        tok_id = ctx.enter_context(nc.sbuf_tensor("tok_id", [P, NT, 2], bf16))
        e_row = sb("e_row", E)
        idx = ctx.enter_context(nc.sbuf_tensor("idx", [P, E], u32))
        y_idx = ctx.enter_context(nc.sbuf_tensor("y_idx", [P, 2, NT], u32))
        rounds = ctx.enter_context(nc.sbuf_tensor("rounds", [P, DEPTH], i32))
        gw = sb("gw", 2, NT)
        wt = sb("wt", 2, NT)
        amask = sb("amask", 5, P)
        rope = sb("rope", 2, 2, FREQ)
        prm_rows = work[:, 0, 0:P]
        bada_rows = work[:, 0, P:2 * P]
        prm = sb("prm", P)
        bada = sb("bada", 96)
        cpad = sb("cpad", C0 + KT * 2 * ADA_PART)
        cT = cpad[:, C0:C0 + KT * 2 * ADA_PART].rearrange("p (k w) -> p k w", k=KT)[:, :, 0:2]
        ada_row = lambda i: qT[:, 1, :, :].rearrange("p a c -> p (a c)") if i % 2 or i == 0 else work[:, 2, :]
        modT = sb("modT", DEPTH, 48, 2)
        amod = sb("amod", 2 * DEPTH, KT, 2)
        wr = sb("wr", KT, E)
        wdt = sb("wdt", DEPTH, KT, 2 * H)
        vec = sb("vec", DEPTH, 16 + 16 + 8 + 8)
        rb = sb("rb", E)
        snw = qT[:, 2, :, :].rearrange("p a c -> p (a c)")
        ckv = sb("ckv", 2, DEPTH, P)
        st_in = sb("st_in", 2, 2, 2, HD)
        diags = lambda w, k: qT[:, (0, 2 if w else 1)[k % 2], :, :]
        diag = qT[:, 0, :, :]
        st_out = diag[:, :, :].rearrange("p a c -> p (a c)")
        epst = sb("epst", 4)
        ss = sb("ss", 5, NT)
        rstd = sb("rstd", 5, NT)
        mx = sb("mx", NT, H)
        nm = sb("nm", NT, H)
        es = sb("es", NT, H)
        rs = sb("rs", NT, H)
        den = sb("den", NT, H)
        dtr = sb("dtr", 2, NT, H)
        dtu = sb("dtu", 2, NT, H)
        dtv = sb("dtv", 2, NT, H)
        dtw = sb("dtw", 2, NT, H)
        dt = sb("dt", 2, NT, H)
        da = sb("da", 2, NT, H)
        cs = sb("cs", 2, NT, H)
        tot = sb("tot", 2, NT, H)
        ecs = sb("ecs", 2, NT, H)
        etot = sb("etot", 2, NT, H)
        wend = sb("wend", 2, NT, H)
        gss = sb("gss", NT, 2)
        grs = sb("grs", NT, 2)
        rt = qT[:, 1, :, :].rearrange("p a c -> p (a c)")[:, 0:8 * NT * E].rearrange(
            "p (n t e) -> p n t e", n=8, t=NT)
        tie = sb("tie", E)
        h_rows = nc.dram_tensor("h_rows", [NT * P, DM], fp32)
        y_exp = nc.dram_tensor("y_exp", [E * CAP, DM], fp32)

        bank = [ctx.enter_context(nc.psum_tensor(f"bank{i}", [P, 512], fp32)) for i in range(8)]

        landed = [sem(f"landed{i}") for i in range(SLOTS)]
        s_rows, s_x, s_small, s_state = sem("rows_landed"), sem("x_landed"), sem("small_landed"), sem("state_landed")
        s_snw, s_fnw = sem("snw_landed"), sem("fnw_landed")
        s_const = sem("consts_made")
        s_pool, s_dve = sem("pool_step"), sem("dve_step")
        s_zero, s_ctxs, s_bada = sem("borders_zeroed"), sem("ctx_state_copied"), sem("bada_copied")
        s_prmT, s_prm, s_cT, s_a = sem("prm_transposed"), sem("prm_copied"), sem("c_silu"), sem("a_made")
        s_ada, s_row, s_rowT, s_mod = (sem(n) for n in (
            "ada_mm", "ada_rows_copied", "ada_transposed", "mod_made"))
        s_ss, s_rstd, s_xn, s_tr, s_hA, s_hD = (sem(n) for n in (
            "sumsq_made", "rstd_made", "xn_made", "xn_transposed", "hT_by_act", "hT_by_dve"))
        s_amod = sem("amod_made")
        s_q, s_kv, s_xbc, s_z = sem("q_mm"), sem("kv_mm"), sem("xbc_mm"), sem("z_mm")
        s_qc, s_kvc, s_xbcc, s_zc = (sem(n) for n in (
            "q_copied", "kv_copied", "xbc_copied", "z_silu"))
        s_rope, s_qtr, s_qTc, s_conv, s_silu = (sem(n) for n in (
            "rope_done", "q_transposed", "qT_copied", "conv_done", "xbc_silu"))
        s_sc, s_scc, s_nm, s_exp, s_es, s_ptr, s_pTc, s_pv, s_attn = (sem(n) for n in (
            "scores_mm", "scores_masked", "max_made", "exp_done", "sink_exp", "probs_transposed",
            "pT_copied", "pv_mm", "attn_done"))
        s_dt1, s_dt2, s_da, s_cs, s_ecs = (sem(n) for n in (
            "dt_abs", "dt_ln", "da_made", "cs_copied", "decays_made"))
        s_xtr, s_xtc, s_g, s_gm = sem("xs_transposed"), sem("xs_copied"), sem("g_mm"), sem("g_masked")
        s_xdt, s_xw, s_st, s_stc, s_snx = (sem(n) for n in (
            "xdt_made", "xw_made", "state_mm", "state_copied", "state_next"))
        s_sto, s_stoc, s_yoff, s_cdec, s_seg, s_dexp, s_scm, s_y = (sem(n) for n in (
            "state_out_transposed", "state_out_copied", "yoff_mm", "decay_rows", "seg_made", "decay_exp",
            "decay_scores", "y_mm"))
        s_brows = sem("bada_rows_landed")
        s_yv, s_gss, s_grs, s_ssd = (sem(n) for n in (
            "y_skip_made", "gated_sumsq", "gated_rstd", "ssd_done"))
        s_dg, s_gb, s_gbc = sem("diag_made"), sem("gate_mm"), sem("gate_copied")
        s_mt, s_mA, s_mD, s_o, s_oc, s_x1 = (sem(n) for n in (
            "mixed_transposed", "mixT_by_act", "mixT_by_dve", "out_mm", "out_gated", "x_updated"))
        s_r, s_re, s_ret = sem("router_mm"), sem("router_exp"), sem("router_exp_transposed")
        s_w1, s_fin, s_xa, s_x2 = (sem(n) for n in ("second_weighted", "moe_gated", "moe_added", "x_complete"))
        o_gated = sem("over_gated")
        s_iota, s_sel, s_pos, s_oh, s_idm, s_idx, s_yidx = (sem(n) for n in (
            "iotas_made", "experts_chosen", "positions_mm", "onehot_made", "ids_mm",
            "slot_tokens_made", "result_rows_made"))
        s_bt, s_btc, s_h = sem("h_transposed_back"), sem("h_rows_copied"), sem("h_rows_stored")
        gathered = [sem(f"gathered{i}") for i in range(4)]
        s_tx, s_xgc, s_gu, s_sil, s_hid, s_th, s_htc, s_dn, s_yc = (sem(n) for n in (
            "xg_transposed", "xgT_copied", "gate_up_mm", "silu_done", "hid_made", "hid_transposed",
            "hidT_copied", "down_mm", "y_copied"))
        y_stored = [sem(f"y_stored{i}") for i in range(2)]
        combined = [sem(f"results_gathered{i}") for i in range(NT)]
        RESULT_STEPS = 11
        s_rounds, o_pass, o_step, o_rows, o_add, o_c, o_pos, o_sel, o_c0 = (sem(n) for n in (
            "rounds_counted", "over_passed", "over_step", "over_rows", "over_added", "over_results", "over_positions", "over_column", "over_ids_copied"))
        o_oh, o_idm, o_idx, o_w, o_g, o_tx, o_xgc, o_gu, o_sil, o_hid, o_th, o_htc, o_dn, o_yc, o_yst = (
            sem("over_" + n) for n in ("onehot", "ids_mm", "idx", "weights", "gathered", "xg_transposed",
                                       "xgT_copied", "gate_up_mm", "silu", "hid", "hid_transposed",
                                       "hidT_copied", "down_mm", "y_copied", "y_stored"))
        s_y_out, s_yst, s_out = sem("final_made"), sem("y_stored"), sem("stored")

        def slot(u):
            return ring[:, u % SLOTS, :].rearrange("p (k n) -> p k n", k=KT)

        def bc(v, w):
            return v.unsqueeze(2).broadcast_to([v.shape[0], v.shape[1], w])

        def rep(v, n):
            return v.unsqueeze(1).broadcast_to([v.shape[0], n, v.shape[1]])

        def heads(v, n=H):
            return v.rearrange("p (h c) -> p h c", h=n)

        def tile_at(t):
            return (0, 132, 260)[t]

        def grp(t):
            return min(t, 1)

        STATES = ((0, 0), (1, 0), (0, 1), (1, 2))
        YOFF_BANK = (3, 4)
        Y_BANK = (6, 5, 0)
        router_psum = bank[7][:, 128:128 + NT * E]
        exp_rows = work[0:E, 0, 0:NT * P]
        PV_BANK = (5, 6, 5)
        ADA_BANK = 7
        MIX_BANK = (5, 6, 7, 1, 2, 0, 3, 4)
        MIX_ACT = (0, 1, 2, 3, 5)
        GATE_BANK = ((6, 7, 1, 2), (6, 7, 0, 1))
        g_psum = lambda g: bank[5][:, 96:96 + NT * P] if g else bank[6][:, 0:NT * P]
        STORES = 2 + 4
        onesP = one[:, 0:1].broadcast_to([P, P])
        ones_b = one_b[:, 0:1].broadcast_to([P, P])
        F0, F1, F2, F3, F4 = 100, 450, 550, 650, 1000
        rows = lambda w: w.rearrange("l (k p) -> (l k) p", p=P)
        done_rounds = {}

        def overflow(eng, l, step, start=None, stop=None, end=None):
            eng.wait_ge(s_rounds, l + 1)
            more = eng.value_load(rounds[0:1, l:l + 1], min_val=0, max_val=MORE)
            before = done_rounds.get((id(eng), l - 1), 0)
            with eng.If(more > 0):
                with eng.Fori(0, more) as r:
                    if start:
                        start(before + r)
                    with eng.Fori(0, E) as e:
                        step(e, before * E + r * E + e)
                    if stop:
                        stop(before + r)
                if end:
                    end(before * E + more * E)
            done_rounds[id(eng), l] = before + more

        block = ctx.enter_context(nc.Block())

        @block.sync
        def _(sp):
            def used(u):
                kind, n = ORDER[u]
                if kind == "ada":
                    return s_ada, n + 1
                if kind == "in":
                    l, j = divmod(n, IN_U)
                    return ((s_q, NT * (l + 1)), (s_xbc, XM * l + 2), (s_xbc, XM * (l + 1)), (s_z, NT * (l + 1)))[j]
                if kind == "out":
                    return s_o, 3 * n + 3
                l, j = divmod(n, MOE_U)
                pair, k = divmod(j, 3)
                return (s_gu, E * l + 2 * pair + k + 1) if k < 2 else (s_dn, E * l + 2 * pair + 2)

            def load(s, parts):
                for dst, src in parts:
                    sp.dma_start(dst, src).then_inc(landed[s], 16)

            def columns(u, w):
                v = w.rearrange("(k p) n -> p k n", p=P)
                if u >= SLOTS:
                    sp.wait_ge(*used(u - SLOTS))
                load(u % SLOTS, [(slot(u)[:, 4 * i:4 * i + 4, :], v[:, 4 * i:4 * i + 4, :]) for i in range(2)])

            def following(u):
                kind, n = ORDER[u]
                w, units = {"ada": (w_ada, ADA_U), "in": (w_in, IN_U), "out": (w_out, OUT_U)}[kind]
                columns(u, w[n // units, :, n % units * 512:(n % units + 1) * 512])

            def expert_unit(l, e, j, s):
                if j < 2:
                    load(s, [(slot(s)[:, :, i * F:(i + 1) * F],
                              w[l, e + j].rearrange("(k p) f -> p k f", p=P))
                             for i, w in enumerate((w_gate, w_up))])
                else:
                    load(s, [(ring[:, s, i * 2 * DM:(i + 1) * 2 * DM].rearrange("p (f n) -> p f n", f=2),
                              w_down[l, e + i].rearrange("(f p) n -> p f n", p=P)) for i in range(2)])

            for dst, src in ((prm_rows[32:40, :], c_ctx.rearrange("(k p) -> k p", p=P)),
                             (prm_rows[40:48, :], rows(c)),
                             (prm_rows[108:120, :], rows(conv_b))):
                sp.dma_start(dst, src).then_inc(s_rows, 16)
            u = 0
            for l in range(DEPTH):
                while u < MOE_AT[l]:
                    if u == ADA_CUT[0]:
                        sp.dma_start(x[:, 0, :], x_prompt[0]).then_inc(s_x, 16)
                        sp.dma_start(x[:, 1:3, :], x_sample[0].rearrange("(t p) d -> p t d", p=P)).then_inc(s_x, 16)
                    following(u)
                    u += 1
                for s in range(SLOTS):
                    sp.wait_ge(*used(u + s - SLOTS))
                    expert_unit(l, 2 * (s // 3), s % 3, s)
                with sp.Fori(1, E // 4) as i:
                    for s in range(SLOTS):
                        pair, k = divmod(s, 3)
                        if k < 2:
                            sp.wait_ge(s_gu, 4 * i + (E * l + 2 * pair + k + 1 - 4))
                        else:
                            sp.wait_ge(s_dn, 4 * i + (E * l + 2 * pair + 2 - 4))
                        expert_unit(l, 4 * i + 2 * pair, k, s)
                u += MOE_U
                if l + 1 < DEPTH:
                    while u < IN_AT[l + 1] + IN_U:
                        following(u)
                        u += 1
                    sp.wait_ge(s_ada, ADA_CUT[2 * l + 2])
                sp.wait_ge(s_dn, E * (l + 1))

                def again(e, q):
                    sp.wait_ge(o_dn, q + 1)
                    for i, w in enumerate((w_gate, w_up)):
                        sp.dma_start(slot(OVER_GU)[:, :, i * F:(i + 1) * F],
                                     w[l, e].rearrange("(k p) f -> p k f", p=P)).then_inc(o_w, 16)
                    sp.dma_start(ring[:, OVER_DN, 0:2 * DM].rearrange("p (f n) -> p f n", f=2),
                                 w_down[l, e].rearrange("(f p) n -> p f n", p=P)).then_inc(o_w, 16)

                def all_used(steps):
                    sp.wait_ge(o_dn, steps + 1)
                    sp.sem_inc(o_pass, 1)

                overflow(sp, l, again, end=all_used)
            for t in range(NT):
                sp.wait_ge(s_y_out, t + 1)
                dst = y_prompt[0] if t == 0 else y_sample[0, (t - 1) * P:t * P, :]
                sp.dma_start(dst, xn[:, t, :]).then_inc(s_yst, 16)
            sp.wait_ge(s_yst, 16 * NT)
            sp.wait_ge(s_out, 16 * STORES * DEPTH)

        @block.gpsimd
        def _(pool):
            n = [0]

            def step(ins):
                n[0] += 1
                ins.then_inc(s_pool, 1)
                pool.wait_ge(s_pool, n[0])

            pool.memset(ident[:, :], 0.0)
            pool.memset(tri[:, :, :], 1.0)
            pool.memset(amask[:, :, :], 0.0)
            pool.memset(cpad[:, :], 0.0)
            pool.memset(epst[:, 0:NT], -0.5)
            step(pool.memset(one[:, :], 1.0))
            iota = work[:, 3, :].bitcast(i32)
            pool.iota(iota[:, 0:CAP], pattern=[[1, CAP]], base=1, channel_multiplier=0)
            pool.iota(iota[:, CAP:CAP + 3], pattern=[[0, 3]], base=0, channel_multiplier=1)
            pool.iota(iota[:, CAP + 3:CAP + 6], pattern=[[P, 3]], base=0, channel_multiplier=0)
            pool.iota(iota[:, CAP + 6:CAP + 6 + E], pattern=[[CAP, E]], base=-1, channel_multiplier=0)
            pool.iota(iota[:, 160:160 + E], pattern=[[-1, E]], base=E, channel_multiplier=0).then_inc(s_iota, 1)
            pool.affine_select(out=ident[:, :], in_=ident[:, :], compare_op=ALU.not_equal, fill=1.0, base=0,
                               pattern=[[-1, P]], channel_multiplier=1)
            pool.affine_select(out=tri[:, 0, :], in_=tri[:, 0, :], compare_op=ALU.is_ge, fill=0.0, base=0,
                               pattern=[[1, P]], channel_multiplier=-1)
            pool.affine_select(out=tri[:, 1, :], in_=tri[:, 1, :], compare_op=ALU.is_ge, fill=0.0, base=0,
                               pattern=[[-1, P]], channel_multiplier=1)
            pool.affine_select(out=amask[:, 1, :], in_=amask[:, 1, :], compare_op=ALU.is_ge, fill=NEG, base=0,
                               pattern=[[1, P]], channel_multiplier=-1)
            pool.affine_select(out=amask[:, 4, :], in_=amask[:, 4, :], compare_op=ALU.is_ge, fill=NEG, base=0,
                               pattern=[[-1, P]], channel_multiplier=1).then_inc(s_const, 1)

            def norm_rstd(k):
                for t in range(NT):
                    pool.wait_ge(s_ss, NT * k + t + 1)
                    v = ss[:, k, t:t + 1]
                    step(pool.tensor_scalar(v, v, 1.0 / DM, EPS, ALU.mult, ALU.add))
                    pool.tensor_tensor(rstd[:, k, t:t + 1], v, epst[:, 0:1], ALU.pow).then_inc(s_rstd, 1)

            for l in range(DEPTH):
                norm_rstd(2 * l)
                if l:
                    pool.wait_ge(s_stc, l)
                for d in range(2):
                    for jj in range(2):
                        pool.dma_start(st_in[:, d, jj, :, :],
                                       state_ssm[0, l, d].rearrange("(g j hh) p n -> j (hh p) g n", g=2, j=2)[jj]
                                       ).then_inc(s_state, 16)
                if l:
                    pool.wait_ge(s_fin, NT * l)
                for b, w in ((0, 2), (130, 4), (390, 2)):
                    last = pool.memset(xpd[:, :, b:b + w], 0.0)
                last.then_inc(s_zero, 1)
                if l == 0:
                    pool.wait_ge(s_small, 16 * SMALL)
                for t in (1, 2):
                    pool.wait_ge(s_qc, NT * l + t + 1)
                    pool.wait_ge(s_kvc, NT * l + t + 1)
                    v = qkv[:, t, 0:640].rearrange("p (h d) -> p h d", d=HD)
                    o = rot[:, t - 1, :].rearrange("p (h d) -> p h d", d=HD)
                    x1, x2 = v[:, :, 0:FREQ], v[:, :, FREQ:HD]
                    co, si = (rep(rope[:, i, t - 1, :], 10) for i in range(2))
                    x2s, x2c = (work[:, 2 * (t - 1) + i, 0:320].rearrange("p (h d) -> p h d", d=FREQ)
                                for i in range(2))
                    pool.tensor_tensor(o[:, :, 0:FREQ], x1, co, ALU.mult)
                    pool.tensor_tensor(o[:, :, FREQ:HD], x1, si, ALU.mult)
                    pool.tensor_tensor(x2s, x2, si, ALU.mult)
                    step(pool.tensor_tensor(x2c, x2, co, ALU.mult))
                    pool.tensor_tensor(o[:, :, 0:FREQ], o[:, :, 0:FREQ], x2s, ALU.subtract)
                    pool.tensor_tensor(o[:, :, FREQ:HD], o[:, :, FREQ:HD], x2c, ALU.add).then_inc(s_rope, 1)
                pool.wait_ge(s_da, l + 1)
                for t in range(NT):
                    pool.wait_ge(s_xtc, 4 * l + t + 1)
                    for d in range(2):
                        last = pool.tensor_tensor(heads(xdt[:, d, t, :]), heads(xs_tok[:, t, :]),
                                                  bc(dt[:, d, t, :], HD), ALU.mult)
                last.then_inc(s_xdt, 1)
                pool.wait_ge(s_xdt, l + 1)
                pool.wait_ge(s_ecs, l + 1)
                for k, (d, t) in enumerate(STATES):
                    pool.tensor_tensor(heads(work[:, k, :]), heads(xdt[:, d, t, :]),
                                       bc(wend[:, d, t, :], HD), ALU.mult).then_inc(s_xw, 1)
                for t in range(NT):
                    pool.tensor_tensor(heads(xs_tok[:, t, :]), heads(xs_tok[:, t, :]), bc(vec[:, l, 32:40], HD),
                                       ALU.mult).then_inc(s_yv, 1)
                for t in range(NT):
                    pool.wait_ge(s_gss, NT * l + t + 1)
                    step(pool.tensor_scalar(gss[:, t, :], gss[:, t, :], 1.0 / 256, EPS, ALU.mult, ALU.add))
                    pool.tensor_tensor(grs[:, t, :], gss[:, t, :], epst[:, 0:2], ALU.pow).then_inc(s_grs, 1)
                norm_rstd(2 * l + 1)
                pool.wait_ge(s_h, 16 * NT * (l + 1))
                for e in range(E):
                    pool.wait_ge(s_idx, 2 * l + (1 if e < 4 else 2))
                    if E * l + e >= 4:
                        pool.wait_ge(s_tx, E * l + e - 3)
                    pool.indirect_dma_start(
                        out=xg[e % 4], out_offset=None, in_=h_rows[:, :],
                        in_offset=bass.IndirectOffsetOnAxis(ap=idx[:, e:e + 1], axis=0)
                    ).then_inc(gathered[e % 4], 16)
                pool.wait_ge(s_tx, E * (l + 1))

                def gather_again(e, q):
                    pool.wait_ge(o_idx, q + 1)
                    pool.sem_inc(o_pass, 1)
                    pool.indirect_dma_start(
                        out=xg[0], out_offset=None, in_=h_rows[:, :],
                        in_offset=bass.IndirectOffsetOnAxis(ap=idx[:, 0:1], axis=0)).then_inc(o_g, 16)

                for b in range(2):
                    pool.wait_ge(y_stored[b], 16 * (E // 2) * (l + 1) + 16)
                pool.wait_ge(s_yidx, l + 1)

                def result(dst, i, t):
                    return pool.indirect_dma_start(
                        out=dst, out_offset=None, in_=y_exp[:, :],
                        in_offset=bass.IndirectOffsetOnAxis(ap=y_idx[:, i, t:t + 1], axis=0))

                for t in range(NT):
                    result(xg[t], 0, t).then_inc(combined[t], 16)
                    result(acc[:, t, :], 1, t).then_inc(combined[t], 16)

                def gather_results(k):
                    pool.wait_ge(o_yst, 16 * E * k + 16 * E)
                    pool.wait_ge(o_rows, k + 1)
                    for j in range(2 * NT):
                        pool.wait_ge(o_add, 2 * NT * k + j + 1)
                        pool.sem_inc(o_pass, 1)
                        result(xg[0], j % 2, j // 2).then_inc(o_c, 16)

                overflow(pool, l, gather_again, stop=gather_results)
            norm_rstd(2 * DEPTH)

        @block.scalar
        def _(act):
            dma = act.dma_start
            act.sem_inc(s_yc, 2)
            for b in range(2):
                act.sem_inc(y_stored[b], 16)
            for dst, src in (
                    (prm_rows[0:16, :], rows(norm1_w)),
                    (prm_rows[16:32, :], rows(norm2_w)),
                    (prm_rows[48:108, :], conv_w.rearrange("l t (m p) -> (l t m) p", p=P))):
                dma(dst, src).then_inc(s_rows, 16)
            dma(bada_rows[0:96, :], rows(b_ada)).then_inc(s_brows, 16)

            act.wait_ge(s_const, 1)
            act.activation(grs[:, 0, 0:1], one[:, :], ACT.Silu)
            act.wait_ge(s_prmT, 1)
            act.activation(prm[:, 0:120], bank[0][:, 0:120], ACT.Copy).then_inc(s_prm, 1)
            act.wait_ge(s_prm, 1)
            act.activation(cT[:, :, :].rearrange("p k g -> p g k"),
                           prm[:, 32:48].rearrange("p (g k) -> p g k", g=2), ACT.Silu).then_inc(s_cT, 1)
            small = [(wr[:, :, :], w_router.rearrange("(k p) n -> p k n", p=P)),
                     (rb[:, :], router_bias.partition_broadcast(P)),
                     (rope[:, 0, :, :], rope_cos.rearrange("(t p) f -> p t f", p=P)),
                     (rope[:, 1, :, :], rope_sin.rearrange("(t p) f -> p t f", p=P))]
            for l in range(DEPTH):
                small += [(wdt[:, l, :, :], w_in[l, :, DT0:IN_W].rearrange("(k p) n -> p k n", p=P)),
                          (vec[:, l, 0:16], dt_bias[l].rearrange("d h -> (d h)").partition_broadcast(P)),
                          (vec[:, l, 16:32], a_log[l].rearrange("d h -> (d h)").partition_broadcast(P)),
                          (vec[:, l, 32:40], d_skip[l].partition_broadcast(P)),
                          (vec[:, l, 40:48], attn_sink[l].partition_broadcast(P)),
                          (ckv[:, 0, l, :], cache_k[0, l].rearrange("s k d -> s (k d)")),
                          (ckv[:, 1, l, :], cache_v[0, l].rearrange("s k d -> s (k d)"))]
            assert len(small) == SMALL
            for dst, src in small:
                dma(dst, src).then_inc(s_small, 16)


            def ada_rows(i):
                n = 2 * (ADA_CUT[i] - (0, *ADA_CUT)[i])
                act.wait_ge(s_ada, ADA_CUT[i])
                act.activation(ada_row(i)[0:n, :], bank[ADA_BANK][0:n, :], ACT.Copy).then_inc(s_row, 1)

            def sumsq(k):
                l = (k - 1) // 2
                if k == 0:
                    act.wait_ge(s_x, 32)
                for t in range(NT):
                    if k % 2:
                        act.wait_ge(s_x1, 6 * l + 4 + t)
                        act.wait_ge(s_mt, KT * (l + 1))
                    elif k:
                        act.wait_ge(s_x2, NT * (k // 2 - 1) + t + 1)
                    act.activation(xn[:, t, :], x[:, t, :], ACT.Square,
                                   accum_out=ss[:, k, t:t + 1]).then_inc(s_ss, 1)

            def modulated(k):
                l, w = k // 2, k % 2
                act.wait_ge(s_amod, k + 1)
                for kt in range(0, KT, 2):
                    act.wait_ge(s_tr, KT * k + kt + 1)
                    for g, (a, b) in enumerate(((0, P), (P, 3 * P))):
                        last = act.activation(hT[:, kt, a:b], bank[kt][:, a:b], ACT.Identity,
                                              bias=modT[:, l, 24 * w + kt, g:g + 1],
                                              scale=amod[:, k, kt, g:g + 1])
                    last.then_inc(s_hA, 1)

            def gate_copies(l, w):
                for k in range(4):
                    act.wait_ge(s_gb, 8 * l + 4 * w + k + 1)
                    act.activation(gate_at[w][k // 2][:, (k % 2) * 512:(k % 2 + 1) * 512],
                                   bank[GATE_BANK[w][k]][:, :], ACT.Copy).then_inc(s_gbc, 1)

            for l in range(DEPTH):
                sumsq(2 * l)
                if l == 0:
                    ada_rows(0)
                modulated(2 * l)
                if l == 0:
                    act.wait_ge(s_small, 16 * SMALL)
                    act.activation(vec[:, :, 16:32], vec[:, :, 16:32], ACT.Exp).then_inc(s_a, 1)
                for t in range(NT):
                    act.wait_ge(s_q, NT * l + t + 1)
                    act.activation(qkv[:, t, 0:AW].rearrange("p (j a d) -> p a j d", a=2, d=HD),
                                   bank[t][:, :].rearrange("p (a j d) -> p a j d", a=2, d=HD),
                                   ACT.Copy).then_inc(s_qc, 1)
                act.wait_ge(s_zero, l + 1)
                for m in range(XM):
                    act.wait_ge(s_xbc, XM * l + m + 1)
                    b = bank[(6 + m) % 8]
                    act.activation(xpd[:, m, 2:2 + P], b[:, 0:P], ACT.Copy)
                    act.activation(xpd[:, m, 134:390], b[:, P:3 * P], ACT.Copy).then_inc(s_xbcc, 1)
                    if m == 1:
                        act.wait_ge(s_dt1, 2 * l + 1)
                        act.activation(dtu[:, :, :, :], dtu[:, :, :, :], ACT.Exp, scale=-1.0).then_inc(s_dt2, 1)
                    if m == 4:
                        act.wait_ge(s_dt1, 2 * l + 2)
                        act.activation(dtw[:, :, :, :], dtv[:, :, :, :], ACT.Ln).then_inc(s_dt2, 1)
                for m in range(XM):
                    act.wait_ge(s_conv, XM * l + m + 1)
                    act.activation(conv[:, m, :], conv[:, m, :], ACT.Silu).then_inc(s_silu, 1)
                for t in range(NT):
                    act.wait_ge(s_z, NT * l + t + 1)
                    act.activation(mixed[:, t, 512:1024], bank[4 + t][:, :], ACT.Silu).then_inc(s_zc, 1)
                act.wait_ge(s_kvc, NT * l + 1)
                dma(new_k[0, l].rearrange("s k d -> s (k d)"), qkv[:, 0, 512:640]).then_inc(s_out, 16)
                dma(new_v[0, l].rearrange("s k d -> s (k d)"), qkv[:, 0, 640:768]).then_inc(s_out, 16)
                for i in range(4):
                    act.wait_ge(s_qtr, 4 * l + i + 1)
                    dst = qT[:, i, :, :] if i < 3 else kT[:, :, :]
                    act.activation(dst.rearrange("p a b -> p (a b)"), bank[i][:, :],
                                   ACT.Copy).then_inc(s_qTc, 1)
                for t in range(NT):
                    nk = P if t == 0 else 3 * P
                    act.wait_ge(s_nm, NT * l + t + 1)
                    for h in range(H):
                        act.activation(probs[:, h, 0:nk], probs[:, h, 0:nk], ACT.Exp, scale=SCALE,
                                       bias=nm[:, t, h:h + 1], accum_out=rs[:, t, h:h + 1]).then_inc(s_exp, 1)
                    act.activation(es[:, t, :], es[:, t, :], ACT.Exp).then_inc(s_es, 1)
                act.wait_ge(s_attn, NT * (l + 1))
                dma(snw, ssd_norm_w[l].partition_broadcast(P)).then_inc(s_snw, 16)
                for i in range(4):
                    act.wait_ge(s_xtr, 5 * l + i + 1)
                    dst = xs_tok[:, i, :] if i < NT else b_tok[:, :, :].rearrange("p t c -> p (t c)")
                    act.activation(dst, bank[i][:, 0:512 if i < NT else NT * P], ACT.Copy).then_inc(s_xtc, 1)
                act.wait_ge(s_xtr, 5 * l + 5)
                act.activation(init_st[:, :, :].rearrange("p d c -> p (d c)"), bank[4][:, :],
                               ACT.Copy).then_inc(s_stc, 1)
                act.wait_ge(s_cs, l + 1)
                act.activation(ecs[:, :, :, :], cs[:, :, :, :], ACT.Exp)
                act.activation(etot[:, :, :, :], tot[:, :, :, :], ACT.Exp)
                act.activation(wend[:, :, :, :], wend[:, :, :, :], ACT.Exp).then_inc(s_ecs, 1)
                act.wait_ge(s_sto, l + 1)
                act.activation(st_out, bank[2][:, :], ACT.Copy).then_inc(s_stoc, 1)
                act.wait_ge(s_stoc, l + 1)
                for d in range(2):
                    for jj in range(2):
                        dma(new_state[0, l, d].rearrange("(g j hh) p n -> j (hh p) g n", g=2, j=2)[jj],
                            st_out.rearrange("p (d j g n) -> p d j g n", d=2, j=2, g=2)[:, d, jj]
                            ).then_inc(s_out, 16)
                def seg(k):
                    t, g, d = k // 4, k // 2 % 2, k % 2
                    act.wait_ge(s_cdec, 12 * l + k + 1)
                    if k >= 2:
                        act.wait_ge(s_scm, 12 * l + k - 1)
                    for h in range(4):
                        last = act.activation(work[:, k % 2, h * P:(h + 1) * P], bank[1 + k % 2][:, h * P:(h + 1) * P],
                                              ACT.Relu, scale=-1.0, bias=cs[:, d, t, 4 * g + h:4 * g + h + 1])
                    last.then_inc(s_seg, 1)

                seg(0)
                for k in range(12):
                    if k + 1 < 12:
                        seg(k + 1)
                    act.wait_ge(s_seg, 12 * l + k + 1)
                    act.activation(work[:, k % 2, :], work[:, k % 2, :], ACT.Exp, scale=-1.0).then_inc(s_dexp, 1)
                ada_rows(2 * l + 1)
                gate_copies(l, 0)
                for kt in MIX_ACT:
                    act.wait_ge(s_mt, KT * l + kt + 1)
                    act.activation(hT[:, kt, :], bank[MIX_BANK[kt]][:, 0:3 * P], ACT.Copy).then_inc(s_mA, 1)
                gate_copies(l, 1)
                sumsq(2 * l + 1)
                modulated(2 * l + 1)
                act.wait_ge(s_r, l + 1)
                act.activation(exp_rows, bank[0][0:E, 0:NT * P], ACT.Exp, scale=-1.0).then_inc(s_re, 1)
                for t in range(NT):
                    for hf in range(2):
                        act.wait_ge(s_bt, 6 * l + 2 * t + hf + 1)
                        act.activation(xn[:, t, hf * 512:(hf + 1) * 512], bank[1 + 2 * t + hf][:, :],
                                       ACT.Copy).then_inc(s_btc, 1)
                    act.wait_ge(s_btc, 6 * l + 2 * t + 2)
                    dma(h_rows[t * P:(t + 1) * P, :], xn[:, t, :]).then_inc(s_h, 16)
                def silu(e, b):
                    act.wait_ge(s_gu, e + (E * l + 1))
                    act.activation(sil[:, b, :], bank[b][:, 0:F], ACT.Silu).then_inc(s_sil, 1)

                def store(e, b, turn):
                    act.wait_ge(s_dn, e + (E * l + 1))
                    act.wait_ge(y_stored[b], 16 * turn + (16 * (E // 2) * l + 16))
                    for hf in range(2):
                        act.activation(y_rows[:, b, hf * 512:(hf + 1) * 512], bank[5 + hf][:, :],
                                       ACT.Copy).then_inc(s_yc, 1)
                    act.wait_ge(s_yc, 2 * e + (2 * E * l + 4))
                    dma(y_exp[bass.ds(e * CAP, CAP), :], y_rows[:, b, :]).then_inc(y_stored[b], 16)

                silu(0, 0)
                with act.Fori(0, E // 2 - 1) as i:
                    silu(2 * i + 1, 1)
                    store(2 * i, 0, i)
                    silu(2 * i + 2, 0)
                    store(2 * i + 1, 1, i)
                silu(E - 1, 1)
                if l == DEPTH - 1:
                    dma(fnw, final_norm_w.partition_broadcast(P)).then_inc(s_fnw, 16)
                store(E - 2, 0, E // 2 - 1)
                store(E - 1, 1, E // 2 - 1)
                act.wait_ge(s_yidx, l + 1)
                for t in range(NT):
                    act.wait_ge(combined[t], 32 * (l + 1))
                    act.activation(acc[:, t, :], acc[:, t, :], ACT.Copy, scale=wt[:, 1, t:t + 1]).then_inc(s_w1, 1)
                if l + 1 < DEPTH:
                    ada_rows(2 * l + 2)

                def results_read(k):
                    for t in range(NT):
                        act.wait_ge(combined[t], 32 * (l + 1))
                    act.wait_ge(o_add, 2 * NT * k + 1)
                    act.sem_inc(o_pass, 1)

                def again(e, q):
                    act.wait_ge(o_gu, q + 1)
                    act.activation(sil[:, 0, :], bank[0][:, 0:F], ACT.Silu).then_inc(o_sil, 1)
                    act.wait_ge(o_dn, q + 2)
                    for hf in range(2):
                        act.activation(y_rows[:, 0, hf * 512:(hf + 1) * 512], bank[5 + hf][:, :],
                                       ACT.Copy).then_inc(o_yc, 1)
                    act.wait_ge(o_yc, 2 * q + 2)
                    dma(y_exp[bass.ds(e * CAP, CAP), :], y_rows[:, 0, :]).then_inc(o_yst, 16)
                    act.wait_ge(o_yst, 16 * q + 16)

                overflow(act, l, again, start=results_read)
            sumsq(2 * DEPTH)

        @block.vector
        def _(dve):
            n = [0]

            def step(ins):
                n[0] += 1
                ins.then_inc(s_dve, 1)
                dve.wait_ge(s_dve, n[0])

            dve.sem_inc(o_add, 1)
            dve.wait_ge(s_iota, 1)
            iota = work[:, 3, :].bitcast(i32)
            dve.tensor_copy(slots_f[:, :], iota[:, 0:CAP])
            dve.tensor_copy(tok_id[:, :, 0], iota[:, CAP:CAP + 3])
            dve.tensor_copy(tok_id[:, :, 1], iota[:, CAP + 3:CAP + 6])
            dve.tensor_copy(e_row[:, :], iota[:, CAP + 6:CAP + 6 + E])
            dve.wait_ge(s_const, 1)
            dve.tensor_copy(tri_b[:, :], tri[:, 0, :])
            dve.tensor_copy(one_b[:, :], one[:, :].broadcast_to([P, 2]))
            dve.tensor_copy(tie[:, :], iota[:, 160:160 + E]).then_inc(s_iota, 1)
            dve.wait_ge(s_prmT, 2)
            dve.tensor_copy(bada[:, :], bank[1][:, 0:96]).then_inc(s_bada, 1)
            dve.wait_ge(s_bada, 1)

            def modulation(i):
                a, b = (ADA_BLK * v for v in ((0, *ADA_CUT)[i], ADA_CUT[i]))
                n = (b - a) // ADA_BLK
                dve.wait_ge(s_rowT, i + 1)
                mod = modT[:, :, :, :].rearrange("p l b g -> p (l b) g")
                for blk in range(ADA_BLK):
                    ins = dve.tensor_tensor(
                        mod[:, a:b, :].rearrange("p (u k) g -> p u k g", k=ADA_BLK)[:, :, blk, :],
                        bank[ADA_BANK][:, 2 * n * blk:2 * n * (blk + 1)].rearrange("p (u g) -> p u g", g=2),
                        bc(bada[:, a:b].rearrange("p (u k) -> p u k", k=ADA_BLK)[:, :, blk], 2), ALU.add)
                ins.then_inc(s_mod, 1)
                dve.wait_ge(s_mod, i + 1)
                if i == 0:
                    dve.wait_ge(s_prm, 1)
                for k in range(2 * DEPTH):
                    l, w = k // 2, k % 2
                    if a < 48 * l + 24 * w + 16 <= b:
                        dve.scalar_tensor_tensor(
                            out=amod[:, k, :, :], in0=modT[:, l, 24 * w + 8:24 * w + 16, :], scalar=1.0,
                            in1=bc(prm[:, 16 * w + 8 * l:16 * w + 8 * l + 8], 2), op0=ALU.add, op1=ALU.mult
                        ).then_inc(s_amod, 1)

            def normed(k):
                for t in range(NT):
                    dve.wait_ge(s_rstd, NT * k + t + 1)
                    dve.tensor_scalar(xn[:, t, :], x[:, t, :], rstd[:, k, t:t + 1], None,
                                      ALU.mult).then_inc(s_xn, 1)

            def modulated(k):
                l, w = k // 2, k % 2
                dve.wait_ge(s_amod, k + 1)
                for kt in range(1, KT, 2):
                    dve.wait_ge(s_tr, KT * k + kt + 1)
                    for g, (a, b) in enumerate(((0, P), (P, 3 * P))):
                        last = dve.tensor_scalar(hT[:, kt, a:b], bank[kt][:, a:b], amod[:, k, kt, g:g + 1],
                                                 modT[:, l, 24 * w + kt, g:g + 1], ALU.mult, ALU.add)
                    last.then_inc(s_hD, 1)

            def gate_diag(l, w, k):
                i = 8 * l + 4 * w + k
                if i:
                    dve.wait_ge(s_gb, i - 1 if k >= 2 else i)
                if w == 0 and k == 0:
                    dve.wait_ge(s_out, 16 * STORES * (l + 1))
                col = 16 + 24 * w + 4 * (k % 2)
                dve.tensor_tensor(diags(w, k), rep(ident[:, :], 4),
                                  bc(modT[:, l, col:col + 4, k // 2], P), ALU.mult).then_inc(s_dg, 1)

            for l in range(DEPTH):
                normed(2 * l)
                if l == 0:
                    modulation(0)
                modulated(2 * l)
                if l == 0:
                    dve.wait_ge(s_a, 1)
                    step(dve.tensor_scalar(vec[:, :, 16:32], vec[:, :, 16:32], -1.0, None, ALU.mult))
                for t in range(NT):
                    dve.wait_ge(s_kv, NT * l + t + 1)
                    dve.tensor_copy(qkv[:, t, 512:768], bank[3 + t][:, 0:256])
                    dve.tensor_tensor(dtr[:, :, t, :], bank[3 + t][:, 256:272].rearrange("p (d h) -> p d h", d=2),
                                      vec[:, l, 0:16].rearrange("p (d h) -> p d h", d=2), ALU.add
                                      ).then_inc(s_kvc, 1)
                dve.wait_ge(s_kvc, NT * (l + 1))
                flat = lambda v: v[:, :, :, :].rearrange("p d t h -> p (d t h)")
                dve.scalar_tensor_tensor(out=flat(dtu), in0=flat(dtr), scalar=-1.0, in1=flat(dtr),
                                         op0=ALU.mult, op1=ALU.max).then_inc(s_dt1, 1)
                for m in range(XM):
                    dve.wait_ge(s_xbcc, XM * l + m + 1)
                    tap = lambda k: prm[:, 48 + 30 * l + 6 * k + m:49 + 30 * l + 6 * k + m]
                    bias = prm[:, 108 + 6 * l + m:109 + 6 * l + m]
                    step(dve.tensor_scalar(conv[:, m, :], xpd[:, m, 0:CONVW], tap(0), bias, ALU.mult, ALU.add))
                    for k in range(1, TAPS):
                        ins = dve.scalar_tensor_tensor(out=conv[:, m, :], in0=xpd[:, m, k:k + CONVW], scalar=tap(k),
                                                       in1=conv[:, m, :], op0=ALU.mult, op1=ALU.add)
                        if k < TAPS - 1:
                            step(ins)
                    ins.then_inc(s_conv, 1)
                    if m == 2:
                        dve.wait_ge(s_dt2, 2 * l + 1)
                        dve.tensor_scalar(dtv[:, :, :, :], dtu[:, :, :, :], 1.0, None, ALU.add).then_inc(s_dt1, 1)
                dve.wait_ge(s_dt1, 2 * l + 2)
                step(dve.tensor_scalar(dt[:, :, :, :], dtv[:, :, :, :], 1.0, None, ALU.subtract))
                step(dve.tensor_tensor(dtu[:, :, :, :], dtu[:, :, :, :], dt[:, :, :, :], ALU.subtract))
                dve.wait_ge(s_dt2, 2 * l + 2)
                step(dve.reciprocal(dtv[:, :, :, :], dtv[:, :, :, :]))
                step(dve.tensor_tensor(dtu[:, :, :, :], dtu[:, :, :, :], dtv[:, :, :, :], ALU.mult))
                step(dve.tensor_tensor(dtu[:, :, :, :], dtu[:, :, :, :], dtw[:, :, :, :], ALU.add))
                step(dve.scalar_tensor_tensor(out=flat(dt), in0=flat(dtr), scalar=0.0, in1=flat(dtu),
                                              op0=ALU.max, op1=ALU.add))
                for d in range(2):
                    ins = dve.tensor_tensor(da[:, d, :, :], dt[:, d, :, :],
                                            rep(vec[:, l, 16 + 8 * d:24 + 8 * d], NT), ALU.mult)
                ins.then_inc(s_da, 1)

                def masked(t, h):
                    k = 24 * l + 8 * t + h
                    nk, m0 = ((P, 2), (3 * P, 2), (3 * P, 0))[t]
                    dve.wait_ge(s_sc, k + 1)
                    dve.tensor_tensor_reduce(out=probs[:, h, 0:nk], in0=bank[(8 * t + h) % 3][:, 0:nk],
                                             in1=amask[:, m0:m0 + nk // P, :].rearrange("p a b -> p (a b)"),
                                             scale=1.0, scalar=2 * NEG, op0=ALU.add, op1=ALU.max,
                                             accum_out=mx[:, t, h:h + 1]).then_inc(s_scc, 1)

                def maxima(t):
                    dve.wait_ge(s_scc, 24 * l + 8 * (t + 1))
                    step(dve.scalar_tensor_tensor(out=mx[:, t, :], in0=mx[:, t, :], scalar=SCALE,
                                                  in1=vec[:, l, 40:48], op0=ALU.mult, op1=ALU.max))
                    dve.tensor_tensor(es[:, t, :], vec[:, l, 40:48], mx[:, t, :], ALU.subtract)
                    dve.tensor_scalar(nm[:, t, :], mx[:, t, :], -1.0, None, ALU.mult).then_inc(s_nm, 1)

                for h in range(H):
                    masked(0, h)
                maxima(0)
                for t in range(NT):
                    nk = P if t == 0 else 3 * P
                    for h in range(H):
                        k = 24 * l + 8 * t + h
                        dve.wait_ge(s_ptr, k + 1)
                        if k >= 2:
                            dve.wait_ge(s_pv, k - 1)
                        dve.tensor_copy(pT[:, h % 2, 0:nk], bank[3 + h % 2][:, 0:nk]).then_inc(s_pTc, 1)
                        if t + 1 < NT:
                            masked(t + 1, h)
                    if t + 1 < NT:
                        maxima(t + 1)
                    dve.wait_ge(s_es, NT * l + t + 1)
                    step(dve.tensor_tensor(den[:, t, :], rs[:, t, :], es[:, t, :], ALU.add))
                    step(dve.reciprocal(den[:, t, :], den[:, t, :]))
                    dve.wait_ge(s_pv, 24 * l + 8 * (t + 1))
                    dve.tensor_tensor(heads(mixed[:, t, 0:512]), heads(bank[PV_BANK[t]][:, :]),
                                      bc(den[:, t, :], HD), ALU.mult).then_inc(s_attn, 1)

                dve.wait_ge(s_g, l + 1)
                dve.tensor_copy(flat(cs), bank[5][:, 0:48])
                step(dve.tensor_copy(flat(tot), bank[5][:, 48:96]))
                dve.tensor_tensor(wend[:, :, :, :], tot[:, :, :, :], cs[:, :, :, :], ALU.subtract).then_inc(s_cs, 1)
                for d in range(2):
                    for g in range(2):
                        ins = dve.tensor_tensor(gm[:, d, :, g, :], heads(g_psum(g), NT),
                                                rep(tri[:, d, :], NT), ALU.mult)
                ins.then_inc(s_gm, 1)
                dve.wait_ge(s_st, 2 * l + 1)
                dve.tensor_copy(final_st[:, :, :].rearrange("p d c -> p (d c)"), bank[0][:, :]).then_inc(s_ctxs, 1)
                dve.wait_ge(s_stc, l + 1)
                dve.wait_ge(s_ecs, l + 1)
                for d, t in STATES[2:]:
                    for g in range(2):
                        r = slice(g * HD, (g + 1) * HD)
                        ins = dve.tensor_tensor(heads(next_st[r, d, :], 4), heads(init_st[r, d, :], 4),
                                                bc(etot[r, d, t, 4 * g:4 * g + 4], HD), ALU.mult)
                step(ins)
                dve.wait_ge(s_st, 2 * l + 2)
                nx = next_st[:, :, :].rearrange("p d c -> p (d c)")
                dve.tensor_tensor(nx, nx, bank[1][:, :], ALU.add).then_inc(s_snx, 1)

                def decayed(k):
                    t, g, d = k // 4, k // 2 % 2, k % 2
                    dve.wait_ge(s_dexp, 12 * l + k + 1)
                    if k >= 3:
                        dve.wait_ge(s_y, 6 * l + (k - 3) // 2 + 1)
                    dve.tensor_tensor(heads(scT[:, k % 3, :], 4), heads(work[:, k % 2, :], 4),
                                      rep(gm[:, d, t, g, :], 4), ALU.mult).then_inc(s_scm, 1)

                def finish(t):
                    v = xs_tok[:, t, :]
                    dve.wait_ge(s_yv, NT * l + t + 1)
                    dve.wait_ge(s_y, 6 * l + 2 * t + 2)
                    step(dve.tensor_tensor(v, v, bank[Y_BANK[t]][:, :], ALU.add))
                    if t:
                        dve.wait_ge(s_yoff, 4 * l + 2 * t)
                        for g in range(2):
                            for d in range(2):
                                ins = dve.tensor_tensor(heads(work[:, 2 + g, d * 256:(d + 1) * 256], 4),
                                                        heads(bank[YOFF_BANK[g]][:, d * 256:(d + 1) * 256], 4),
                                                        bc(ecs[:, d, t, 4 * g:4 * g + 4], HD), ALU.mult)
                        step(ins)
                        for d in range(2):
                            step(dve.tensor_tensor(heads(v, 2), heads(v, 2), work[:, 2:4, d * 256:(d + 1) * 256],
                                                   ALU.add))
                    z = mixed[:, t, 512:1024]
                    step(dve.tensor_tensor(z, v, z, ALU.mult))
                    for g in range(2):
                        zg = z[:, g * 256:(g + 1) * 256]
                        ins = dve.tensor_tensor_reduce(out=work[:, 2, g * 256:(g + 1) * 256], in0=zg, in1=zg, scale=1.0,
                                                       scalar=0.0, op0=ALU.mult, op1=ALU.add,
                                                       accum_out=gss[:, t, g:g + 1])
                    ins.then_inc(s_gss, 1)
                    dve.wait_ge(s_grs, NT * l + t + 1)
                    for g in range(2):
                        zg = z[:, g * 256:(g + 1) * 256]
                        ins = dve.scalar_tensor_tensor(out=zg, in0=zg, scalar=grs[:, t, g:g + 1],
                                                       in1=snw[:, g * 256:(g + 1) * 256],
                                                       op0=ALU.mult, op1=ALU.mult)
                    ins.then_inc(s_ssd, 1)

                dve.wait_ge(s_snw, 16 * (l + 1))
                for k in range(12):
                    decayed(k)
                    if k == 11:
                        modulation(2 * l + 1)
                        for q in range(4):
                            gate_diag(l, 0, q)
                    if k in (5, 9, 11):
                        finish((k - 5) // 3)

                for kt in sorted(set(range(KT)) - set(MIX_ACT)):
                    dve.wait_ge(s_mt, KT * l + kt + 1)
                    dve.tensor_copy(hT[:, kt, :], bank[MIX_BANK[kt]][:, 0:3 * P]).then_inc(s_mD, 1)
                dve.wait_ge(s_gbc, 8 * l + 4)
                for k in range(6):
                    hf, t = k // 3, k % 3
                    dve.wait_ge(s_o, 6 * l + k + 1)
                    dve.tensor_tensor(work[:, k % 4, :], bank[k][:, :],
                                      gate_at[0][grp(t)][:, hf * 512:(hf + 1) * 512], ALU.mult).then_inc(s_oc, 1)
                    dve.wait_ge(s_oc, 6 * l + k + 1)
                    xx = x[:, t, hf * 512:(hf + 1) * 512]
                    dve.tensor_tensor(xx, xx, work[:, k % 4, :], ALU.add).then_inc(s_x1, 1)
                    for q in ((0,), (1,), (2, 3))[k] if k < 3 else ():
                        gate_diag(l, 1, q)
                normed(2 * l + 1)
                modulated(2 * l + 1)

                R = lambda i: rt[:, i, :, :].rearrange("p t e -> p (t e)")
                G4 = lambda v: v.rearrange("p (a j) -> p a j", j=4)
                E3 = lambda v: v.rearrange("p (t e) -> p t e", e=E)
                dve.wait_ge(s_ret, l + 1)
                step(dve.tensor_scalar(R(0), router_psum, 1.0, None, ALU.add))
                step(dve.reciprocal(R(0), R(0)))
                step(dve.tensor_tensor(E3(R(1)), E3(R(0)), rep(rb[:, :], NT), ALU.add))
                s4, p4, q4 = G4(R(1)), G4(R(2)), G4(R(3))
                dve.tensor_tensor(p4[:, :, 0:3], s4[:, :, 0:3], s4[:, :, 1:4], ALU.add)
                dve.tensor_tensor(q4[:, :, 0:2], s4[:, :, 0:2], s4[:, :, 2:4], ALU.add)
                step(dve.tensor_tensor(p4[:, :, 3:4], s4[:, :, 0:1], s4[:, :, 3:4], ALU.add))
                step(dve.tensor_tensor(q4[:, :, 0:2], q4[:, :, 0:2], p4[:, :, 0:2], ALU.max))
                step(dve.tensor_tensor(q4[:, :, 0:2], q4[:, :, 0:2], p4[:, :, 2:4], ALU.max))
                gs = rt[:, 4, :, 0:4]
                step(dve.tensor_tensor(gs, q4[:, :, 0:1].rearrange("p (t a) j -> p t (a j)", t=NT),
                                       q4[:, :, 1:2].rearrange("p (t a) j -> p t (a j)", t=NT), ALU.max))
                gmax = rt[:, 4, :, 4:5]

                def first_of_max(v, src, m, weight, width):
                    step(dve.tensor_reduce(m, src, AX.X, ALU.max))
                    step(dve.tensor_tensor(v, src, m.broadcast_to([P, NT, width]), ALU.is_equal))
                    step(dve.tensor_tensor(v, v, weight, ALU.mult))
                    step(dve.tensor_reduce(m, v, AX.X, ALU.max))
                    step(dve.tensor_tensor(v, v, m.broadcast_to([P, NT, width]), ALU.is_equal))

                first_of_max(gs, gs, gmax, rep(tie[:, 0:4], NT), 4)
                step(dve.tensor_scalar(gs, gs, -NEG, NEG, ALU.mult, ALU.add))
                by_group = lambda v: v.rearrange("p t (a j) -> p t a j", j=4)
                step(dve.tensor_tensor(by_group(rt[:, 2, :, :]), by_group(rt[:, 1, :, :]),
                                       gs.unsqueeze(3).broadcast_to([P, NT, 4, 4]), ALU.add))
                first_of_max(rt[:, 3, :, :], rt[:, 2, :, :], rt[:, 4, :, 5:6], rep(tie[:, :], NT), E)
                step(dve.scalar_tensor_tensor(out=R(2), in0=R(3), scalar=4 * NEG, in1=R(2),
                                              op0=ALU.mult, op1=ALU.add))
                first_of_max(rt[:, 2, :, :], rt[:, 2, :, :], rt[:, 4, :, 6:7], rep(tie[:, :], NT), E)
                dve.tensor_tensor(chosen_b[:, :, :].rearrange("p t e -> p (t e)"), R(3), R(2), ALU.add)
                dve.tensor_tensor(R(5), R(3), R(2), ALU.add).then_inc(s_sel, 1)
                dve.wait_ge(s_pos, l + 1)
                dve.wait_ge(s_sel, l + 1)
                step(dve.tensor_tensor(R(1), bank[7][:, 0:NT * E], R(5), ALU.mult))

                for e in range(E):
                    if e >= 4:
                        dve.wait_ge(s_idm, E * l + e - 3)
                    dve.tensor_tensor(onehot[:, e % 4, :, :], rep(slots_f[:, :], NT), bc(rt[:, 1, :, e], CAP),
                                      ALU.is_equal).then_inc(s_oh, 1)
                    if e in (4, E - 1):
                        a, b = (0, 4) if e == 4 else (4, E)
                        dve.wait_ge(s_idm, E * l + b)
                        v = bank[7 if a == 0 else 0][:, 64:64 + 2 * E].rearrange("p (e i) -> p e i", i=2)
                        step(dve.tensor_copy(R(4)[:, 16 + a:16 + b], v[:, a:b, 0]))
                        dve.tensor_tensor(idx[:, a:b], R(4)[:, 16 + a:16 + b], v[:, a:b, 1],
                                          ALU.add).then_inc(s_idx, 1)
                def result_rows(step):
                    dve.tensor_scalar(R(0), R(1), float(CAP + 1), None, ALU.is_lt)
                    step(dve.tensor_scalar(R(6), R(1), 1.0, None, ALU.is_ge))
                    step(dve.tensor_tensor(R(0), R(0), R(6), ALU.mult))
                    step(dve.tensor_tensor(E3(R(6)), E3(R(1)), rep(e_row[:, :], NT), ALU.add))
                    for i, chosen in enumerate((3, 2)):
                        step(dve.tensor_tensor(R(5), R(chosen), R(0), ALU.mult))
                        dve.tensor_reduce(R(4)[:, 12 + 4 * i:12 + 4 * i + NT].unsqueeze(2), rt[:, 5, :, :],
                                          AX.X, ALU.add)
                        step(dve.tensor_tensor(R(7), R(5), R(6), ALU.mult))
                        step(dve.tensor_reduce(R(4)[:, 4 * i:4 * i + NT].unsqueeze(2), rt[:, 7, :, :],
                                               AX.X, ALU.add))
                        dve.tensor_tensor(wt[:, i, :], gw[:, i, :], R(4)[:, 12 + 4 * i:12 + 4 * i + NT], ALU.mult)
                        step(dve.tensor_copy(y_idx[:, i, :], R(4)[:, 4 * i:4 * i + NT]))

                top = R(4)[:, 8:9]
                step(dve.tensor_reduce(top, bank[0][:, 0:E], AX.X, ALU.max))

                def copy_rows(e, b):
                    dve.wait_ge(s_tx, e + (E * l + 1))
                    for hf in range(2):
                        dve.tensor_copy(xgT[:, b, hf * 512:(hf + 1) * 512], bank[3 + hf][:, :]).then_inc(s_xgc, 1)

                def hidden(e, b):
                    dve.wait_ge(s_sil, e + (E * l + 1))
                    dve.tensor_tensor(hid[:, b, :], sil[:, b, :], bank[b][:, F:2 * F], ALU.mult).then_inc(s_hid, 1)

                def copy_hidden(e, b):
                    dve.wait_ge(s_th, e + (E * l + 1))
                    dve.tensor_copy(hidT[:, b, :], bank[2][:, 0:F]).then_inc(s_htc, 1)

                copy_rows(0, 0)
                copy_rows(1, 1)
                hidden(0, 0)
                with dve.Fori(0, E // 2 - 1) as i:
                    copy_hidden(2 * i, 0)
                    copy_rows(2 * i + 2, 0)
                    hidden(2 * i + 1, 1)
                    copy_hidden(2 * i + 1, 1)
                    copy_rows(2 * i + 3, 1)
                    hidden(2 * i + 2, 0)
                copy_hidden(E - 2, 0)
                hidden(E - 1, 1)
                copy_hidden(E - 1, 1)
                step(dve.tensor_tensor(R(6), R(3), R(0), ALU.mult))
                dve.tensor_reduce(gw[:, 0, :].unsqueeze(2), rt[:, 6, :, :], AX.X, ALU.add)
                step(dve.tensor_tensor(R(7), R(2), R(0), ALU.mult))
                step(dve.tensor_reduce(gw[:, 1, :].unsqueeze(2), rt[:, 7, :, :], AX.X, ALU.add))
                step(dve.tensor_tensor(R(6)[:, 0:NT], gw[:, 0, :], gw[:, 1, :], ALU.add))
                step(dve.reciprocal(R(6)[:, 0:NT], R(6)[:, 0:NT]))
                step(dve.tensor_tensor(gw[:, :, :], gw[:, :, :], rep(R(6)[:, 0:NT], 2), ALU.mult))
                result_rows(step)
                dve.sem_inc(s_yidx, 1)
                step(dve.tensor_scalar(R(4)[:, 9:10], top, float(CAP), None, ALU.is_gt))
                for k in range(2, MORE + 1):
                    step(dve.tensor_scalar(R(4)[:, 10:11], top, float(k * CAP), None, ALU.is_gt))
                    step(dve.tensor_tensor(R(4)[:, 9:10], R(4)[:, 9:10], R(4)[:, 10:11], ALU.add))
                dve.tensor_copy(rounds[:, l:l + 1], R(4)[:, 9:10]).then_inc(s_rounds, 1)

                def next_round(k):
                    dve.tensor_scalar(R(1), R(1), float(CAP), None, ALU.subtract).then_inc(o_pos, 1)
                    dve.wait_ge(o_pos, k + 1)
                    dve.sem_inc(o_pass, 1)

                def again(e, q):
                    dve.tensor_copy(R(7)[:, 0:NT].unsqueeze(2), rt[:, 1, :, bass.ds(e, 1)]).then_inc(o_sel, 1)
                    dve.wait_ge(o_sel, q + 1)
                    dve.tensor_tensor(onehot[:, 0, :, :], rep(slots_f[:, :], NT), bc(R(7)[:, 0:NT], CAP),
                                      ALU.is_equal).then_inc(o_oh, 1)
                    dve.wait_ge(o_idm, q + 1)
                    dve.tensor_copy(R(4)[:, 16:17], bank[7][:, 64:65]).then_inc(o_c0, 1)
                    dve.wait_ge(o_c0, q + 1)
                    dve.tensor_tensor(idx[:, 0:1], R(4)[:, 16:17], bank[7][:, 65:66], ALU.add).then_inc(o_idx, 1)
                    dve.wait_ge(o_tx, q + 1)
                    dve.tensor_copy(xgT[:, 0, 0:512], bank[3][:, :])
                    dve.tensor_copy(xgT[:, 0, 512:1024], bank[4][:, :]).then_inc(o_xgc, 1)
                    dve.wait_ge(o_sil, q + 1)
                    dve.tensor_tensor(hid[:, 0, :], sil[:, 0, :], bank[0][:, F:2 * F], ALU.mult).then_inc(o_hid, 1)
                    dve.wait_ge(o_th, q + 1)
                    dve.tensor_copy(hidT[:, 0, :], bank[2][:, 0:F]).then_inc(o_htc, 1)

                dve.wait_ge(s_gbc, 8 * l + 8)
                for t in range(NT):
                    a = acc[:, t, :]
                    dve.wait_ge(s_w1, NT * l + t + 1)
                    dve.wait_ge(combined[t], 32 * (l + 1))
                    step(dve.scalar_tensor_tensor(out=a, in0=xg[t], scalar=wt[:, 0, t:t + 1], in1=a,
                                                  op0=ALU.mult, op1=ALU.add))
                    dve.tensor_tensor(a, a, gate_at[1][grp(t)], ALU.mult).then_inc(s_fin, 1)
                    dve.wait_ge(s_fin, NT * l + t + 1)
                    dve.tensor_tensor(x[:, t, :], x[:, t, :], a, ALU.add).then_inc(s_xa, 1)
                dve.wait_ge(s_xa, NT * (l + 1))

                def add_results(k):
                    n = [0]

                    def round_step(ins):
                        n[0] += 1
                        ins.then_inc(o_step, 1)
                        dve.wait_ge(o_step, k * RESULT_STEPS + n[0])

                    result_rows(round_step)
                    assert n[0] == RESULT_STEPS
                    dve.sem_inc(o_rows, 1)
                    for j in range(2 * NT):
                        t, i = j // 2, j % 2
                        dve.wait_ge(o_c, 16 * 2 * NT * k + 16 * (j + 1))
                        dve.scalar_tensor_tensor(out=acc[:, t, :], in0=xg[0], scalar=wt[:, i, t:t + 1],
                                                 in1=gate_at[1][grp(t)], op0=ALU.mult, op1=ALU.mult).then_inc(o_gated, 1)
                        dve.wait_ge(o_gated, 2 * NT * k + j + 1)
                        dve.tensor_tensor(x[:, t, :], x[:, t, :], acc[:, t, :], ALU.add).then_inc(o_add, 1)
                        dve.wait_ge(o_add, 2 * NT * k + j + 2)
                    dve.sem_inc(o_pass, 1)

                overflow(dve, l, again, start=next_round, stop=add_results)

                dve.sem_inc(s_x2, NT)
                if l + 1 < DEPTH:
                    modulation(2 * l + 2)
            dve.wait_ge(s_fnw, 16)
            for t in range(NT):
                dve.wait_ge(s_rstd, 2 * DEPTH * NT + t + 1)
                dve.scalar_tensor_tensor(out=xn[:, t, :], in0=x[:, t, :], scalar=rstd[:, 2 * DEPTH, t:t + 1],
                                         in1=fnw, op0=ALU.mult, op1=ALU.mult).then_inc(s_y_out, 1)

        @block.tensor
        def _(pe):
            mm, tr = pe.matmul, pe.transpose
            pe.sem_inc(o_dn, 1)

            def arrived(u):
                pe.wait_ge(landed[u % SLOTS], 32 * (u // SLOTS + 1))

            pe.wait_ge(s_const, 1)
            pe.wait_ge(s_rows, 16 * 6)
            tr(bank[0][:, 0:120], prm_rows[0:120, :], ident[0:120, 0:120]).then_inc(s_prmT, 1)

            n_ada = [0]

            def ada(upto):
                while n_ada[0] < upto:
                    j, kt = divmod(n_ada[0], KT)
                    i = sum(j >= v for v in ADA_CUT)
                    a, b = (0, *ADA_CUT)[i], ADA_CUT[i]
                    if kt == 0:
                        arrived(ADA_AT[j])
                    c = C0 + kt * 2 * ADA_PART - 2 * (j - a)
                    last = mm(bank[ADA_BANK][0:2 * (b - a), :], cpad[:, c:c + 2 * (b - a)],
                              slot(ADA_AT[j])[:, kt, :], start=j == a and kt == 0, stop=j == b - 1 and kt == KT - 1)
                    n_ada[0] += 1
                    if kt == KT - 1:
                        last.then_inc(s_ada, 1)

            def fill(l, share):
                a, b = (v * KT for v in ADA_CUT[2 * l:2 * l + 2])
                ada(a + (b - a) * share // 1000)

            def ada_columns(i):
                n = 2 * (ADA_CUT[i] - (0, *ADA_CUT)[i])
                pe.wait_ge(s_row, i + 1)
                for blk in range(ADA_BLK):
                    last = tr(bank[ADA_BANK][:, n * blk:n * (blk + 1)], ada_row(i)[0:n, blk * P:(blk + 1) * P],
                              ident[0:n, 0:n])
                last.then_inc(s_rowT, 1)

            def norm_transposes(k):
                for t in range(NT):
                    pe.wait_ge(s_xn, NT * k + t + 1)
                for kt in range(KT):
                    if k % 2 == 0 and kt == ADA_BANK:
                        pe.wait_ge(s_mod, k + 1)
                    for t in range(NT):
                        last = tr(bank[kt][:, t * P:(t + 1) * P], xn[:, t, kt * P:(kt + 1) * P], ident[:, :])
                    last.then_inc(s_tr, 1)
                pe.wait_ge(s_hA, 4 * (k + 1))
                pe.wait_ge(s_hD, 4 * (k + 1))

            def gate_rows(l, w, quarters):
                for k in quarters:
                    pe.wait_ge(s_dg, 8 * l + 4 * w + k + 1)
                    mm(bank[GATE_BANK[w][k]][:, :], onesP, diags(w, k).rearrange("p a c -> p (a c)"),
                       start=True, stop=True).then_inc(s_gb, 1)

            pe.wait_ge(s_cT, 1)
            pe.wait_ge(s_brows, 16)
            tr(bank[1][:, 0:96], bada_rows[0:96, :], ident[0:96, 0:96]).then_inc(s_prmT, 1)
            ada(ADA_CUT[0] * KT)
            ada_columns(0)
            for l in range(DEPTH):
                u = IN_AT[l]
                norm_transposes(2 * l)

                tok = lambda kt, t: hT[:, kt, t * P:(t + 1) * P]
                arrived(u)
                for t in range(NT):
                    for kt in range(KT):
                        last = mm(bank[t][:, :], tok(kt, t), slot(u)[:, kt, :], start=kt == 0, stop=kt == KT - 1)
                    last.then_inc(s_q, 1)
                arrived(u + 1)
                if l == 0:
                    pe.wait_ge(s_small, 16 * SMALL)
                for t in range(NT):
                    for kt in range(KT):
                        mm(bank[3 + t][:, 0:256], tok(kt, t), slot(u + 1)[:, kt, 0:256],
                           start=kt == 0, stop=kt == KT - 1)
                    for kt in range(KT):
                        last = mm(bank[3 + t][:, 256:272], tok(kt, t), wdt[:, l, kt, :],
                                  start=kt == 0, stop=kt == KT - 1)
                    last.then_inc(s_kv, 1)
                for m in range(XM):
                    v, col = (u + 1, 256 + m * P) if m < 2 else (u + 2, (m - 2) * P)
                    if m == 2:
                        arrived(v)
                    if 2 <= m < 5:
                        pe.wait_ge(s_qc, NT * l + m - 1)
                    if m == 5:
                        pe.wait_ge(s_kvc, NT * l + 1)
                    for kt in range(KT):
                        last = mm(bank[(6 + m) % 8][:, 0:3 * P], slot(v)[:, kt, col:col + P], hT[:, kt, :],
                                  start=kt == 0, stop=kt == KT - 1)
                    last.then_inc(s_xbc, 1)
                arrived(u + 3)
                for t in range(NT):
                    if t < 2:
                        pe.wait_ge(s_kvc, NT * l + t + 2)
                    else:
                        pe.wait_ge(s_xbcc, XM * l + 1)
                    for kt in range(KT):
                        last = mm(bank[4 + t][:, :], tok(kt, t), slot(u + 3)[:, kt, :],
                                  start=kt == 0, stop=kt == KT - 1)
                    last.then_inc(s_z, 1)
                u = OUT_AT[l]

                pe.wait_ge(s_xbcc, XM * l + 2)
                fill(l, 20)
                for t in range(NT):
                    pe.wait_ge(s_xbcc, XM * l + t + 3)
                    if t:
                        pe.wait_ge(s_rope, 2 * l + t)
                    else:
                        pe.wait_ge(s_qc, NT * l + 1)
                        pe.wait_ge(s_kvc, NT * l + 1)
                    src = qkv[:, 0, 0:512] if t == 0 else rot[:, t - 1, 0:512]
                    for j in range(4):
                        last = tr(bank[t][:, j * P:(j + 1) * P], src[:, j * P:(j + 1) * P], ident[:, :])
                    last.then_inc(s_qtr, 1)
                fill(l, 50)
                pe.wait_ge(s_xbcc, XM * l + 6)
                for i, src in enumerate((ckv[:, 0, l, :], rot[:, 0, 512:640], rot[:, 1, 512:640], qkv[:, 0, 512:640])):
                    last = tr(bank[3][:, i * P:(i + 1) * P], src, ident[:, :])
                last.then_inc(s_qtr, 1)

                def scores(t, h):
                    k = 24 * l + 8 * t + h
                    if 8 * t + h >= 3:
                        pe.wait_ge(s_scc, k - 2)
                    r = slice(HD * (h // 4), HD * (h // 4 + 1))
                    keys = kT[r, 3:4, :] if t == 0 else kT[r, 0:3, :]
                    nk = P if t == 0 else 3 * P
                    mm(bank[(8 * t + h) % 3][:, 0:nk], qT[r, t, h % 4, :], keys.rearrange("p a c -> p (a c)"),
                       start=True, stop=True).then_inc(s_sc, 1)

                pe.wait_ge(s_qTc, 4 * (l + 1))
                pe.wait_ge(s_zc, NT * (l + 1))
                pe.wait_ge(s_xbcc, XM * (l + 1))
                fill(l, 100)
                for h in range(H):
                    scores(0, h)
                def turned(t, h):
                    k = 24 * l + 8 * t + h
                    pe.wait_ge(s_exp, k + 1)
                    if 8 * t + h >= 2:
                        pe.wait_ge(s_pTc, k - 1)
                    for a in range(1 if t == 0 else 3):
                        last = tr(bank[3 + h % 2][:, a * P:(a + 1) * P], probs[:, h, a * P:(a + 1) * P],
                                  ident[:, :])
                    last.then_inc(s_ptr, 1)

                turned(0, 0)
                for t in range(NT):
                    parts = 1 if t == 0 else 3
                    for h in range(H):
                        k = 24 * l + 8 * t + h
                        if t + 1 < NT:
                            scores(t + 1, h)
                        if h == H - 1:
                            fill(l, F0 + (F1 - F0) * (t + 1) // 3)
                        if 8 * t + h + 1 < NT * H:
                            turned(t + (h + 1) // H, (h + 1) % H)
                        fill(l, F0 + (F1 - F0) * t // 3 + (F1 - F0) * (h + 1) // 36)
                        pe.wait_ge(s_pTc, k + 1)
                        if t == 2 and h == 0:
                            pe.wait_ge(s_attn, NT * l + 1)
                        kv = HD * (h // 4)
                        vals = (qkv[:, 0, 640:768],) if t == 0 else (ckv[:, 1, l, :], qkv[:, 1, 640:768],
                                                                     qkv[:, 2, 640:768])
                        for a in range(parts):
                            last = mm(bank[PV_BANK[t]][:, h * HD:(h + 1) * HD], pT[:, h % 2, a * P:(a + 1) * P],
                                      vals[a][:, kv:kv + HD], start=a == 0, stop=a == parts - 1)
                        last.then_inc(s_pv, 1)

                pe.wait_ge(s_silu, XM * (l + 1))
                for t in range(NT):
                    o = tile_at(t)
                    for m in range(4):
                        last = tr(bank[t][:, m * P:(m + 1) * P], conv[:, m, o:o + P], ident[:, :])
                    last.then_inc(s_xtr, 1)
                for t in range(NT):
                    o = tile_at(t)
                    last = tr(bank[3][:, t * P:(t + 1) * P], conv[:, 4, o:o + P], ident[:, :])
                last.then_inc(s_xtr, 1)
                pe.wait_ge(s_state, 64 * (l + 1))
                for d in range(2):
                    for jj in range(2):
                        i = 2 * d + jj
                        last = tr(bank[4][:, i * P:(i + 1) * P],
                                  st_in[:, d, jj, :, :].rearrange("p g n -> p (g n)"), ident[:, :])
                last.then_inc(s_xtr, 1)
                pe.wait_ge(s_da, l + 1)
                pe.wait_ge(s_attn, NT * (l + 1))
                for d in range(2):
                    mm(bank[5][:, 24 * d:24 * d + 24], tri[:, d, :], da[:, d, :, :].rearrange("p t h -> p (t h)"),
                       start=True, stop=True)
                mm(bank[5][:, 48:96], onesP, da[:, :, :, :].rearrange("p d t h -> p (d t h)"),
                   start=True, stop=True)
                for i in range(6):
                    t, g = i // 2, i % 2
                    o, r = tile_at(t), slice(g * HD, (g + 1) * HD)
                    last = mm(g_psum(g)[:, t * P:(t + 1) * P], conv[r, 4, o:o + P],
                              conv[r, 5, o:o + P], start=True, stop=True)
                last.then_inc(s_g, 1)
                fill(l, F2)
                pe.wait_ge(s_xtc, 4 * (l + 1))
                for k, (d, t) in enumerate(STATES):
                    pe.wait_ge(s_xw, 4 * l + k + 1)
                    for g in range(2):
                        r = slice(g * HD, (g + 1) * HD)
                        last = mm(bank[k // 2][r, d * 256:(d + 1) * 256], b_tok[:, t, g * HD:(g + 1) * HD],
                                  work[:, k, g * 256:(g + 1) * 256], start=True, stop=True)
                    if k % 2:
                        last.then_inc(s_st, 1)
                pe.wait_ge(s_ctxs, l + 1)
                for i in range(4):
                    last = tr(bank[2][:, i * P:(i + 1) * P], final_st[:, i // 2, (i % 2) * P:(i % 2 + 1) * P],
                              ident[:, :])
                last.then_inc(s_sto, 1)
                pe.wait_ge(s_stc, l + 1)
                pe.wait_ge(s_cs, l + 1)
                def from_states(t):
                    o = tile_at(t)
                    for d, s in ((0, init_st), (1, next_st)) if t == 1 else ((1, init_st), (0, next_st)):
                        for g in range(2):
                            r = slice(g * HD, (g + 1) * HD)
                            last = mm(bank[YOFF_BANK[g]][:, d * 256:(d + 1) * 256], conv[r, 5, o:o + P],
                                      s[r, d, :], start=True, stop=True)
                        last.then_inc(s_yoff, 1)

                pe.wait_ge(s_snx, l + 1)
                from_states(1)
                fill(l, F3)

                def decay_rows(k):
                    t, g, d = k // 4, k // 2 % 2, k % 2
                    if k >= 2:
                        pe.wait_ge(s_seg, 12 * l + k - 1)
                    for h in range(4):
                        last = mm(bank[1 + k % 2][:, h * P:(h + 1) * P],
                                  da[:, d, t, 4 * g + h:4 * g + h + 1].broadcast_to([P, P]), tri[:, d, :],
                                  start=True, stop=True)
                    last.then_inc(s_cdec, 1)

                pe.wait_ge(s_stoc, l + 1)
                pe.wait_ge(s_snx, l + 1)
                pe.wait_ge(s_gm, l + 1)
                pe.wait_ge(s_xdt, l + 1)
                decay_rows(0)
                decay_rows(1)
                for p in range(6):
                    if p < 5:
                        decay_rows(2 * p + 2)
                        decay_rows(2 * p + 3)
                    t, g = p // 2, p % 2
                    fill(l, F3 + (F4 - F3) * (p + 1) // 6)
                    if p == 5:
                        pe.wait_ge(s_gss, NT * l + 2)
                        from_states(2)
                    pe.wait_ge(s_scm, 12 * l + 2 * p + 2)
                    for h in range(4):
                        hh = 4 * g + h
                        for d in range(2):
                            last = mm(bank[Y_BANK[t]][:, hh * HD:(hh + 1) * HD],
                                      scT[:, (2 * p + d) % 3, h * P:(h + 1) * P],
                                      xdt[:, d, t, hh * HD:(hh + 1) * HD], start=d == 0, stop=d == 1)
                    last.then_inc(s_y, 1)

                fill(l, 1000)
                ada_columns(2 * l + 1)
                pe.wait_ge(s_seg, 12 * (l + 1))
                pe.wait_ge(s_mod, 2 * l + 2)
                gate_rows(l, 0, range(4))
                pe.wait_ge(s_gbc, 8 * l + 4)
                for kt in range(KT):
                    if kt == KT // 2:
                        pe.wait_ge(s_ssd, NT * (l + 1))
                    for t in range(NT):
                        last = tr(bank[MIX_BANK[kt]][:, t * P:(t + 1) * P], mixed[:, t, kt * P:(kt + 1) * P],
                                  ident[:, :])
                    last.then_inc(s_mt, 1)
                pe.wait_ge(s_mA, len(MIX_ACT) * (l + 1))
                pe.wait_ge(s_mD, (KT - len(MIX_ACT)) * (l + 1))
                for hf in range(2):
                    arrived(u + hf)
                    for t in range(NT):
                        for kt in range(KT):
                            last = mm(bank[3 * hf + t][:, :], tok(kt, t), slot(u + hf)[:, kt, :],
                                      start=kt == 0, stop=kt == KT - 1)
                        last.then_inc(s_o, 1)
                        if 3 * hf + t == 2:
                            gate_rows(l, 1, (0, 1))
                        if 3 * hf + t == 4:
                            pe.wait_ge(s_oc, 6 * l + 2)
                            gate_rows(l, 1, (2, 3))
                pe.wait_ge(s_gbc, 8 * l + 8)
                norm_transposes(2 * l + 1)

                for kt in range(KT):
                    last = mm(bank[0][0:E, 0:NT * P], wr[:, kt, :], hT[:, kt, :], start=kt == 0, stop=kt == KT - 1)
                last.then_inc(s_r, 1)
                for t in range(NT):
                    if t == 1:
                        pe.wait_ge(s_re, l + 1)
                        for tt in range(NT):
                            last = tr(router_psum[:, tt * E:(tt + 1) * E], exp_rows[:, tt * P:(tt + 1) * P],
                                      ident[0:E, 0:E])
                        last.then_inc(s_ret, 1)
                    for hf in range(2):
                        for j in range(4):
                            last = tr(bank[1 + 2 * t + hf][:, j * P:(j + 1) * P], tok(4 * hf + j, t), ident[:, :])
                        last.then_inc(s_bt, 1)
                pe.wait_ge(s_sel, l + 1)
                pos = bank[7][:, 0:NT * E]
                mm(pos, tri_b[:, :], chosen_b[:, :, :].rearrange("p t e -> p (t e)"), start=True, stop=False)
                mm(pos[:, E:2 * E], ones_b, chosen_b[:, 0, :], start=False, stop=False)
                for a in range(NT - 1):
                    last = mm(pos[:, 2 * E:3 * E], ones_b, chosen_b[:, a, :], start=False, stop=a == NT - 2)
                last.then_inc(s_pos, 1)
                for a in range(NT):
                    mm(bank[0][:, 0:E], ones_b, chosen_b[:, a, :], start=a == 0, stop=a == NT - 1)

                def slot_tokens(b, e, done):
                    for t in range(NT):
                        last = mm(bank[7 if e < 4 else 0][:, 64 + 2 * e:66 + 2 * e], onehot[:, b, t, :], tok_id[:, t, :],
                                  start=t == 0, stop=t == NT - 1)
                    last.then_inc(done, 1)

                for e in range(E):
                    pe.wait_ge(s_oh, E * l + e + 1)
                    slot_tokens(e % 4, e, s_idm)

                turn = MOE_AT[l] // SLOTS

                def rows_transposed(buf, done):
                    for kt in range(KT):
                        last = tr(bank[3 + kt // 4][:, kt % 4 * P:(kt % 4 + 1) * P], buf[:, kt * P:(kt + 1) * P],
                                  ident[:, :])
                    last.then_inc(done, 1)

                def gate_up(b, w, done):
                    for kt in range(KT):
                        last = mm(bank[b][:, :], xgT[:, b, kt * P:(kt + 1) * P], w[:, kt, :],
                                  start=kt == 0, stop=kt == KT - 1)
                    last.then_inc(done, 1)

                def hidden_transposed(b, done):
                    for f in range(2):
                        last = tr(bank[2][:, f * P:(f + 1) * P], hid[:, b, f * P:(f + 1) * P], ident[:, :])
                    last.then_inc(done, 1)

                def down(b, w, done):
                    w = w.rearrange("p (f n) -> p f n", f=2)
                    for hf in range(2):
                        for f in range(2):
                            last = mm(bank[5 + hf][:, :], hidT[:, b, f * P:(f + 1) * P],
                                      w[:, f, hf * 512:(hf + 1) * 512], start=f == 0, stop=f == 1)
                    last.then_inc(done, 1)

                GU, DN = (0, 1, 3, 4), (2, 2, 5, 5)

                def rows(e, j, i):
                    pe.wait_ge(gathered[j], 16 * i + (4 * 16 * l + 16))
                    rows_transposed(xg[j], s_tx)

                def first_half(e, j, i):
                    pe.wait_ge(s_xgc, 2 * e + (2 * E * l + 2))
                    pe.wait_ge(landed[GU[j]], 32 * i + 32 * (turn + 1))
                    gate_up(j % 2, slot(GU[j]), s_gu)

                def hid_of(e, j):
                    pe.wait_ge(s_hid, e + (E * l + 1))
                    hidden_transposed(j % 2, s_th)

                def second_half(e, j, i):
                    pe.wait_ge(s_htc, e + (E * l + 1))
                    pe.wait_ge(s_yc, 2 * e + (2 * E * l + 2))
                    if j % 2 == 0:
                        pe.wait_ge(landed[DN[j]], 32 * i + 32 * (turn + 1))
                    down(j % 2, ring[:, DN[j], j % 2 * 2 * DM:(j % 2 + 1) * 2 * DM], s_dn)

                pe.wait_ge(s_btc, 6 * (l + 1))
                rows(0, 0, 0)
                pe.wait_ge(s_xgc, 2 * E * l + 2)
                rows(1, 1, 0)
                first_half(0, 0, 0)

                def body(i, last=False):
                    for j in range(4):
                        e, n1, n2 = 4 * i + j, (j + 1) % 4, (j + 2) % 4
                        if not (last and j == 3):
                            first_half(e + 1, n1, i + (j == 3))
                        hid_of(e, j)
                        if not (last and j >= 2):
                            rows(e + 2, n2, i + (j >= 2))
                        second_half(e, j, i)

                with pe.Fori(0, E // 4 - 1) as i:
                    body(i)
                body(E // 4 - 1, True)
                if l + 1 < DEPTH:
                    ada(ADA_CUT[2 * l + 2] * KT)
                    pe.wait_ge(s_row, 2 * l + 3)

                def again(e, q):
                    pe.wait_ge(o_oh, q + 1)
                    slot_tokens(0, 0, o_idm)
                    pe.wait_ge(o_g, 16 * q + 16)
                    rows_transposed(xg[0], o_tx)
                    pe.wait_ge(o_xgc, q + 1)
                    pe.wait_ge(o_w, 48 * q + 48)
                    gate_up(0, slot(OVER_GU), o_gu)
                    pe.wait_ge(o_hid, q + 1)
                    hidden_transposed(0, o_th)
                    pe.wait_ge(o_htc, q + 1)
                    down(0, ring[:, OVER_DN, 0:2 * DM], o_dn)

                def banks_read(steps):
                    pe.wait_ge(o_yc, 2 * steps)
                    pe.sem_inc(o_pass, 1)

                overflow(pe, l, again, end=banks_read)
                if l + 1 < DEPTH:
                    ada_columns(2 * l + 2)
                pe.wait_ge(s_yc, 2 * E * (l + 1) + 2)


def rope_tables():
    tokens, grid_w = 256, 64
    row = (np.arange(tokens) // grid_w).astype(np.float32)
    col = (np.arange(tokens) % grid_w).astype(np.float32)
    n = HD // 4
    inv = np.power(np.float32(10000.0), -np.arange(n, dtype=np.float32) / np.float32(n)).astype(np.float32)
    ang = np.concatenate([row[:, None] * inv, col[:, None] * inv], axis=-1).astype(np.float32)
    return np.cos(ang).astype(np.float32), np.sin(ang).astype(np.float32)


_INS = ['x_prompt', 'x_sample', 'cache_k', 'cache_v', 'state_ssm', 'c', 'c_ctx', 'norm1_w', 'norm2_w',
        'final_norm_w', 'w_ada', 'b_ada', 'w_in', 'conv_w', 'conv_b', 'attn_sink', 'dt_bias', 'a_log',
        'd_skip', 'ssd_norm_w', 'w_out', 'w_router', 'router_bias', 'w_gate', 'w_up', 'w_down']
_OUTS = [(1, 128, 1024), (1, 256, 1024), (1, 2, 128, 2, 64), (1, 2, 128, 2, 64), (1, 2, 2, 8, 64, 64)]


def kernel(**inputs):
    import numpy as _np
    import concourse.bacc as _bacc
    from concourse import mybir as _mybir
    from concourse.bass_utils import run_bass_kernel_spmd as _run

    nc = _bacc.Bacc("TRN2", target_bir_lowering=False, num_devices=1)
    arrays, args = {}, []
    cos, sin = rope_tables()
    for name, a in [(n, inputs[n]) for n in _INS] + [("rope_cos", cos), ("rope_sin", sin)]:
        a = _np.ascontiguousarray(a)
        arrays[f"in_{name}_dram"] = a
        args.append(nc.dram_tensor(f"in_{name}_dram", a.shape, _mybir.dt.from_np(a.dtype), kind="ExternalInput").ap())
    for i, shape in enumerate(_OUTS):
        args.append(nc.dram_tensor(f"out_{i}_dram", shape, _mybir.dt.float32, kind="ExternalOutput").ap())
    hybrid_step(nc, *args)
    r = _run(nc, [arrays], core_ids=[0])
    return tuple(r.results[0][f"out_{i}_dram"] for i in range(len(_OUTS)))
```
